# Optimizing a Trainium2 kernel written in Bass

```python
import jax, jax.numpy as jnp
from jax import lax
import numpy as np

D_MODEL = 1024
BATCH = 1
SEQ = 256
DEPTH = 1

GRID_W = 64
CTX_LEN = 256
EPS = 1e-6
D_RNN = 1024
LRU_HEADS = 8
LRU_BW = D_RNN // LRU_HEADS
CONV_W = 4
CONV_PAD_L = 2
LRU_C = 8.0
HG_HEADS = 8
HG_DK = 128
HG_DV = 128
HG_WIDTH = HG_HEADS * HG_DK
HG_VW = HG_HEADS * HG_DV
CHUNK = 32
SPLITS = (D_RNN, 2 * D_RNN, 2 * D_RNN + HG_WIDTH, 2 * D_RNN + 2 * HG_WIDTH, 2 * D_RNN + 3 * HG_WIDTH,
          2 * D_RNN + 3 * HG_WIDTH + HG_VW, 2 * D_RNN + 3 * HG_WIDTH + 2 * HG_VW,
          2 * D_RNN + 3 * HG_WIDTH + 2 * HG_VW + D_MODEL)
IN_WIDTH = 2 * D_RNN + 3 * HG_WIDTH + 2 * HG_VW + 2 * D_MODEL
N_GROUPS = 4
EXP_PER_GROUP = 8
N_EXPERTS = N_GROUPS * EXP_PER_GROUP
TOP_K = 2
D_EXPERT = 512

kernel_name = "hybrid_rglru_hgrn2_hmoe_dit_block"

F32 = jnp.float32

def rmsnorm(x, g):
    xf = x.astype(F32)
    y = xf * lax.rsqrt(jnp.mean(xf * xf, axis=-1, keepdims=True) + EPS)
    return (y * g.astype(F32)).astype(x.dtype)

def modulate(h, shift, scale):
    return h * (1.0 + scale) + shift

def to_colmajor(t, rows):
    b, L, ch = t.shape
    return t.reshape(b, rows, GRID_W, ch).swapaxes(1, 2).reshape(b, L, ch)

def from_colmajor(t, rows):
    b, L, ch = t.shape
    return t.reshape(b, GRID_W, rows, ch).swapaxes(1, 2).reshape(b, L, ch)

def dwconv_centred(u, w, b):
    L = u.shape[1]
    up = jnp.pad(u, ((0, 0), (CONV_PAD_L, CONV_W - 1 - CONV_PAD_L), (0, 0)))
    return sum(up[:, k:k + L] * w[k] for k in range(CONV_W)) + b

def rglru_coeffs(u, wa, ba, wx, bx, lam):
    bsz, L, _ = u.shape
    uf = u.astype(F32)
    ub = uf.reshape(bsz, L, LRU_HEADS, LRU_BW)
    r = jax.nn.sigmoid(jnp.einsum('blhi,hij->blhj', ub, wa.astype(F32)).reshape(bsz, L, D_RNN) + ba)
    i = jax.nn.sigmoid(jnp.einsum('blhi,hij->blhj', ub, wx.astype(F32)).reshape(bsz, L, D_RNN) + bx)
    log_a = -LRU_C * r * jax.nn.softplus(-lam.astype(F32))
    a = jnp.exp(log_a)
    b = jnp.sqrt(-jnp.expm1(2.0 * log_a)) * (i * uf)
    return a, b

def linear_scan(a, b, h0, reverse):
    idx = -1 if reverse else 0
    b = b.at[:, idx].add(a[:, idx] * h0.astype(F32))

    def combine(l, r):
        return l[0] * r[0], r[0] * l[1] + r[1]

    _, h = lax.associative_scan(combine, (a, b), reverse=reverse, axis=1)
    return h, h[:, idx]

def hgrn2_chunk_scan(q, k, v, logf, s0, with_output):
    bsz, nh, L, _ = q.shape
    n = L // CHUNK

    def blocks(t):
        return t.reshape(bsz, nh, n, CHUNK, t.shape[-1]).transpose(2, 0, 1, 3, 4)

    lc = jnp.cumsum(blocks(logf), axis=3)
    mask = jnp.tril(jnp.ones((CHUNK, CHUNK), dtype=bool))

    def step(s, inp):
        qc, kc, vc, lcc = inp
        ltot = lcc[:, :, -1:, :]
        s_new = jnp.exp(lcc[:, :, -1, :])[..., None] * s + jnp.einsum('bhck,bhcv->bhkv', kc * jnp.exp(ltot - lcc), vc)
        if not with_output:
            return s_new, None
        lmid = lcc[:, :, CHUNK // 2:CHUNK // 2 + 1, :]
        o_inter = jnp.einsum('bhck,bhkv->bhcv', qc * jnp.exp(lcc), s)
        att = jnp.einsum('bhck,bhsk->bhcs', qc * jnp.exp(lcc - lmid), kc * jnp.exp(lmid - lcc))
        att = jnp.where(mask, att, 0.0)
        return s_new, o_inter + jnp.einsum('bhcs,bhsv->bhcv', att, vc)

    s, o = lax.scan(step, s0, (blocks(q), blocks(k), blocks(v), lc))
    if with_output:
        o = o.transpose(1, 2, 0, 3, 4).reshape(bsz, nh, L, -1)
    return o, s

def hgrn2_direction(q, f, v, lb, s0, reverse, with_output):
    bsz, L, _ = q.shape
    g = lb + (1.0 - lb) * jax.nn.sigmoid(f.astype(F32))

    def heads(t):
        t = t.astype(F32).reshape(bsz, L, HG_HEADS, -1).transpose(0, 2, 1, 3)
        return jnp.flip(t, axis=2) if reverse else t

    o, s = hgrn2_chunk_scan(heads(jax.nn.silu(q.astype(F32))), heads(1.0 - g), heads(v), heads(jnp.log(g)),
                            s0, with_output)
    if with_output and reverse:
        o = jnp.flip(o, axis=2)
    return o, s

def head_rmsnorm(o, g):
    o = o * lax.rsqrt(jnp.mean(o * o, axis=-1, keepdims=True) + EPS) * g.astype(F32).reshape(HG_HEADS, 1, HG_DV)
    b, h, L, dv = o.shape
    return o.transpose(0, 2, 1, 3).reshape(b, L, h * dv)

def branch_merge(ya, ay, yb, og, ga, gb, w_proj_a, w_proj_b, w_out):
    dt = ay.dtype
    pa = (ya * jax.nn.gelu(ay.astype(F32))).astype(dt) @ w_proj_a
    pb = (yb * jax.nn.silu(og.astype(F32))).astype(dt) @ w_proj_b
    return (jax.nn.sigmoid(ga) * pa + jax.nn.sigmoid(gb) * pb) @ w_out

def token_mixer(hx, hc, rows, lb, w_in, conv_w, conv_b, lru_wa, lru_ba, lru_wx, lru_bx, lru_lam,
                hg_norm_g, w_proj_a, w_proj_b, w_out, need_ctx):
    bsz = hx.shape[0]
    ax, ayx, qx, ffx, fbx, vx, ogx, gax, gbx = jnp.split(hx @ w_in, SPLITS, axis=-1)
    ac, ayc, qc, ffc, fbc, vc, ogc, gac, gbc = jnp.split(hc @ w_in, SPLITS, axis=-1)

    ux = dwconv_centred(ax, conv_w, conv_b)
    uc = dwconv_centred(ac, conv_w, conv_b)
    h0 = jnp.zeros((bsz, D_RNN), F32)
    ya_x, ya_c = 0.0, 0.0
    for d, rev in enumerate((False, True)):
        a_c, b_c = rglru_coeffs(uc, lru_wa[d], lru_ba[d], lru_wx[d], lru_bx[d], lru_lam[d])
        h_c, s_c = linear_scan(a_c, b_c, h0, rev)
        a_x, b_x = rglru_coeffs(ux, lru_wa[d], lru_ba[d], lru_wx[d], lru_bx[d], lru_lam[d])
        h_x, _ = linear_scan(a_x, b_x, s_c, rev)
        ya_x = ya_x + h_x
        if need_ctx:
            ya_c = ya_c + h_c

    qx_cm, ffx_cm, fbx_cm, vx_cm = (to_colmajor(t, rows) for t in (qx, ffx, fbx, vx))
    s0 = jnp.zeros((bsz, HG_HEADS, HG_DK, HG_DV), F32)
    yb_x, yb_c = 0.0, 0.0
    for rev, f_x, f_c in ((False, ffx_cm, ffc), (True, fbx_cm, fbc)):
        o_c, s_c = hgrn2_direction(qc, f_c, vc, lb, s0, rev, need_ctx)
        o_x, _ = hgrn2_direction(qx_cm, f_x, vx_cm, lb, s_c, rev, True)
        yb_x = yb_x + o_x
        if need_ctx:
            yb_c = yb_c + o_c
    yb_x = from_colmajor(head_rmsnorm(yb_x, hg_norm_g), rows)

    out_x = branch_merge(ya_x, ayx, yb_x, ogx, gax, gbx, w_proj_a, w_proj_b, w_out)
    out_c = None
    if need_ctx:
        out_c = branch_merge(ya_c, ayc, head_rmsnorm(yb_c, hg_norm_g), ogc, gac, gbc, w_proj_a, w_proj_b, w_out)
    return out_x, out_c

def expert_mlp(t, w1, w3, w2):
    return (jax.nn.silu(t @ w1) * (t @ w3)) @ w2

def hier_moe(h, w_rg, b_rg, w_re, b_re, w1, w3, w2):
    shp = h.shape
    t = h.reshape(-1, shp[-1])
    n_tok = t.shape[0]
    tf = t.astype(F32)
    p_grp = jax.nn.softmax(tf @ w_rg.astype(F32) + b_rg, axis=-1)
    pg, gi = lax.top_k(p_grp, 1)
    e_logit = (tf @ w_re.astype(F32) + b_re).reshape(n_tok, N_GROUPS, EXP_PER_GROUP)
    e_sel = jnp.einsum('tge,tg->te', e_logit, jax.nn.one_hot(gi[:, 0], N_GROUPS, dtype=F32))
    pe, ei = lax.top_k(jax.nn.softmax(e_sel, axis=-1), TOP_K)
    wts = pg * pe / jnp.sum(pe, axis=-1, keepdims=True)
    eid = gi * EXP_PER_GROUP + ei
    cw = jnp.einsum('tk,tkn->tn', wts, jax.nn.one_hot(eid, N_EXPERTS, dtype=F32))
    y = jnp.zeros_like(t)
    for e in range(N_EXPERTS):
        y = y + (cw[:, e:e + 1] * expert_mlp(t, w1[e], w3[e], w2[e])).astype(t.dtype)
    return y.reshape(shp)

def setup_inputs(seed: int = 0) -> dict:
    key = jax.random.key(seed)
    ks = jax.random.split(key, 32)

    def nrm(k, shape, scale):
        return jax.random.normal(k, shape, F32) * scale

    u = jax.random.uniform(ks[14], (DEPTH, 2, D_RNN), F32, 0.9, 0.999)
    a0 = u ** (1.0 / LRU_C)
    return {
        "x": nrm(ks[0], (BATCH, SEQ, D_MODEL), 1.0),
        "c": nrm(ks[1], (BATCH, D_MODEL), 1.0),
        "ctx": nrm(ks[2], (BATCH, CTX_LEN, D_MODEL), 1.0),
        "c_ctx": nrm(ks[3], (D_MODEL,), 1.0),
        "w_mod": nrm(ks[4], (DEPTH, D_MODEL, 6 * D_MODEL), 0.5 * D_MODEL ** -0.5),
        "b_mod": nrm(ks[5], (DEPTH, 6 * D_MODEL), 0.02),
        "norm1_g": 1.0 + nrm(ks[6], (DEPTH, D_MODEL), 0.05),
        "w_in": nrm(ks[7], (DEPTH, D_MODEL, IN_WIDTH), D_MODEL ** -0.5),
        "conv_w": nrm(ks[8], (DEPTH, CONV_W, D_RNN), CONV_W ** -0.5),
        "conv_b": nrm(ks[9], (DEPTH, D_RNN), 0.02),
        "lru_wa": nrm(ks[10], (DEPTH, 2, LRU_HEADS, LRU_BW, LRU_BW), LRU_BW ** -0.5),
        "lru_ba": nrm(ks[11], (DEPTH, 2, D_RNN), 0.02),
        "lru_wx": nrm(ks[12], (DEPTH, 2, LRU_HEADS, LRU_BW, LRU_BW), LRU_BW ** -0.5),
        "lru_bx": nrm(ks[13], (DEPTH, 2, D_RNN), 0.02),
        "lru_lam": jnp.log(a0) - jnp.log1p(-a0),
        "hg_lb": nrm(ks[15], (DEPTH + 1, HG_WIDTH), 0.1),
        "hg_norm_g": 1.0 + nrm(ks[16], (DEPTH, HG_VW), 0.05),
        "w_proj_a": nrm(ks[17], (DEPTH, D_RNN, D_MODEL), D_RNN ** -0.5),
        "w_proj_b": nrm(ks[18], (DEPTH, HG_VW, D_MODEL), HG_VW ** -0.5),
        "w_out": nrm(ks[19], (DEPTH, D_MODEL, D_MODEL), D_MODEL ** -0.5),
        "norm2_g": 1.0 + nrm(ks[20], (DEPTH, D_MODEL), 0.05),
        "w_rg": nrm(ks[21], (DEPTH, D_MODEL, N_GROUPS), D_MODEL ** -0.5),
        "b_rg": nrm(ks[22], (DEPTH, N_GROUPS), 0.01),
        "w_re": nrm(ks[23], (DEPTH, D_MODEL, N_EXPERTS), D_MODEL ** -0.5),
        "b_re": nrm(ks[24], (DEPTH, N_EXPERTS), 0.01),
        "w1": nrm(ks[25], (DEPTH, N_EXPERTS, D_MODEL, D_EXPERT), D_MODEL ** -0.5),
        "w3": nrm(ks[26], (DEPTH, N_EXPERTS, D_MODEL, D_EXPERT), D_MODEL ** -0.5),
        "w2": nrm(ks[27], (DEPTH, N_EXPERTS, D_EXPERT, D_MODEL), D_EXPERT ** -0.5),
        "final_g": 1.0 + nrm(ks[28], (D_MODEL,), 0.05),
    }

def reference(x, c, ctx, c_ctx, w_mod, b_mod, norm1_g, w_in, conv_w, conv_b, lru_wa, lru_ba, lru_wx, lru_bx,
              lru_lam, hg_lb, hg_norm_g, w_proj_a, w_proj_b, w_out, norm2_g, w_rg, b_rg, w_re, b_re,
              w1, w3, w2, final_g):
    rows = x.shape[1] // GRID_W
    lb_all = jnp.cumsum(jax.nn.softmax(hg_lb.astype(F32), axis=0), axis=0)
    sc = jax.nn.silu(c)
    scc = jax.nn.silu(c_ctx)
    for l in range(DEPTH):
        need_ctx = l < DEPTH - 1
        mx = jnp.split((sc @ w_mod[l] + b_mod[l])[:, None, :], 6, axis=-1)
        mc = jnp.split(scc @ w_mod[l] + b_mod[l], 6, axis=-1)
        hx = modulate(rmsnorm(x, norm1_g[l]), mx[0], mx[1])
        hc = modulate(rmsnorm(ctx, norm1_g[l]), mc[0], mc[1])
        ox, oc = token_mixer(hx, hc, rows, lb_all[l], w_in[l], conv_w[l], conv_b[l], lru_wa[l], lru_ba[l],
                             lru_wx[l], lru_bx[l], lru_lam[l], hg_norm_g[l], w_proj_a[l], w_proj_b[l],
                             w_out[l], need_ctx)
        x = x + mx[2] * ox
        hx2 = modulate(rmsnorm(x, norm2_g[l]), mx[3], mx[4])
        x = x + mx[5] * hier_moe(hx2, w_rg[l], b_rg[l], w_re[l], b_re[l], w1[l], w3[l], w2[l])
        if need_ctx:
            ctx = ctx + mc[2] * oc
            hc2 = modulate(rmsnorm(ctx, norm2_g[l]), mc[3], mc[4])
            ctx = ctx + mc[5] * hier_moe(hc2, w_rg[l], b_rg[l], w_re[l], b_re[l], w1[l], w3[l], w2[l])
    return rmsnorm(x, final_g)


_drawn_inputs = setup_inputs


def setup_inputs(seed=0):
    import zlib

    import numpy as np

    out = dict(_drawn_inputs(seed))
    spreads = {}
    factors = {'ctx': 6.959,
     'c_ctx': 8.0,
     'norm1_g': 2.973,
     'conv_b': 3.057,
     'lru_ba': 25.113,
     'lru_bx': 8.0,
     'hg_lb': 8.0,
     'hg_norm_g': 8.0,
     'norm2_g': 2.778,
     'b_rg': 8.0,
     'b_re': 22.104}
    for name, (base, spread) in spreads.items():
        noise = np.random.default_rng([zlib.crc32(name.encode()), seed]).standard_normal(out[name].shape)
        drawn = base * np.exp(spread * noise) if base else spread * noise
        out[name] = __import__('jax').numpy.asarray(drawn.astype(out[name].dtype))
    for name, factor in factors.items():
        out[name] = (out[name] * factor).astype(out[name].dtype)
    return out
```

```python
import concourse.bass as bass
from concourse import mybir
from contextlib import ExitStack

D = 1024
P = 128
KT = D // P
T = 256
GW = 64
ROWS = T // GW
HEADS = 8
CH = 32
NCH = T // CH
MID = CH // 2
EPS = 1e-6
NE = 32
NG = 4
EPG = NE // NG
F = 512
SLOTS = 64
PAIRS = NE // 2
BIG = 1e30

BLK = {"a": 0, "ay": 1, "q": 2, "ff": 3, "fb": 4, "v": 5, "og": 6, "ga": 7, "gb": 8}
ORDER = ["a", "q", "ay", "ff", "fb", "v", "og", "ga", "gb"]
SHARED = {"ay": "q", "ga": "og"}

V_CW, V_CB, V_BA, V_BX, V_LAM, V_LB, V_HG, V_N1, V_N2 = 0, 4, 5, 7, 9, 11, 13, 14, 15
V_NSP, V_PSP, V_LBV, V_OML = 16, 18, 20, 21
NV = 22

SLOT = 4096
A_WBLK = 0
A_WLRU = 9 * 1024
A_WMOD = A_WLRU + 512
A_PRO = 8192
A_R = A_WMOD + 4096
A_HT = 6 * SLOT
EDGE = 6
TU = T + 2
A_YA = A_HT + KT * (EDGE + 2 * T)
A_YB = A_YA + 2048
A_GA = A_YB + 2048
A_GB = A_GA + 2048
A_MG = A_GB + 2048
A_T = A_MG + 2048
ARENA = A_T + 11784


def build(nc, x, c, ctx_in, c_ctx, w_mod, b_mod, norm1_g, w_in, conv_w, conv_b, lru_wa, lru_ba, lru_wx, lru_bx,
          lru_lam, hg_lb, hg_norm_g, w_proj_a, w_proj_b, w_out, norm2_g, w_rg, b_rg, w_re, b_re,
          w1, w3, w2, final_g, out):
    f32 = mybir.dt.float32
    bf16 = mybir.dt.bfloat16
    u32 = mybir.dt.uint32
    i32 = mybir.dt.int32
    ACT = mybir.ActivationFunctionType
    ALU = mybir.AluOpType
    AX = mybir.AxisListType

    with ExitStack() as es:
        arena = es.enter_context(nc.sbuf_tensor("arena", [P, ARENA], f32))

        def at(start, *shape):
            n = 1
            for s in shape:
                n *= s
            v = arena[:, start:start + n]
            if len(shape) == 2:
                v = v.rearrange("p (a b) -> p a b", a=shape[0])
            if len(shape) == 3:
                v = v.rearrange("p (a b c) -> p a b c", a=shape[0], b=shape[1])
            return v

        def sb(name, *shape, dt=f32):
            return es.enter_context(nc.sbuf_tensor(name, [P, *shape], dt))

        sems = {}

        def S(name):
            if name not in sems:
                sems[name] = es.enter_context(nc.semaphore(name))
            return sems[name]

        ident = sb("ident", P)
        mean_w = sb("mean_w", P)
        ones = sb("ones", T)
        resets = sb("resets", T)
        causal = [sb("causal_f", P), sb("causal_b", P)]
        before = sb("before", P)
        slot_no = sb("slot_no", SLOTS)
        zb = sb("zb", 4 * P, dt=bf16)
        prows = at(A_T + 5120, 2, P)
        par = sb("par", NV, HEADS)
        par2 = sb("par2", 64)
        csil = sb("csil", KT, 2)
        modA = sb("modA", 16, 2)
        modB = sb("modB", 32)
        aff1 = sb("aff1", 2, KT)
        aff2 = sb("aff2", KT)
        ssq = sb("ssq", 4)
        rstd = sb("rstd", 4)
        hp = sb("hp", NV)
        etot = sb("etot", 2, NCH)
        w_rt = sb("w_rt", KT, NG + NE)
        b_rt = sb("b_rt", NG + NE)
        spt = sb("spt", 5, 16)
        rcnt = sb("rcnt", 4)
        rcnt_i = sb("rcnt_i", 4, dt=i32)
        eps_t = sb("eps_t", 1)
        cw = sb("cw", 2, NE)

        bank = [es.enter_context(nc.psum_tensor(f"bank{i}", [P, 512], f32)) for i in range(8)]
        PJ = [bank[0], bank[1]]
        GT = [bank[2], bank[3]]
        TB, KB, AB, OB = bank[4:8]

        h_ct = at(A_HT, KT, EDGE + 2 * T)
        wblk = {n: at(A_WBLK + 1024 * i, KT, P) for i, n in enumerate(ORDER)}
        wlru = at(A_WLRU, 4, P)
        wmod = at(A_WMOD, KT, 512)
        wpro = [at(A_PRO + 2048 * i, KT, T) for i in range(8)]
        ya_g, yb_g, s_ga, s_gb = (at(a, HEADS, T) for a in (A_YA, A_YB, A_GA, A_GB))
        merged = at(A_MG, KT, T)
        tok = at(A_T, 4, D)
        junk = at(A_YA, 4, D)
        o = A_T
        a_pad = at(o, T + 3)
        a_edge = at(o + T + 4, EDGE + 4)
        o += 520
        u = at(o, TU)
        o += 512
        rg, ig, tz, aa, rc, hs = ([at(o + 512 * (2 * j + d), TU) for d in range(2)] for j in range(6))
        o += 12 * 512
        gl = at(o, T)
        hsum = at(o + 256, T)
        qs = at(o + 512, T)
        sq = at(o + 768, T)
        o += 1024
        kdT = [at(o + 512 * d, 4, P) for d in range(2)]
        o += 1024
        att = [at(o + 256 * d, 2, P) for d in range(2)]
        o += 512
        st = [at(o + 1024 * d, NCH, P) for d in range(2)]
        o += 2048
        assert o <= ARENA
        o = A_R
        gg, kk, lf = ([at(o + 512 * (2 * j + d), 2 * T) for d in range(2)] for j in range(3))
        o += 6 * 512
        lcx, rcx, dm, d4, e1, e2, e3, e4, ec = ([at(o + 256 * (2 * j + d), T) for d in range(2)] for j in range(9))
        o += 18 * 256
        vv = at(o, 4, P)
        o += 512
        vbd = at(o, 2, 4, P)
        o += 1024
        osq, orr, on, sog = (at(o + 256 * j, T) for j in range(4))
        o += 1024
        assert o <= A_HT
        wp = [[at(2048 * b + 1024 * j, KT, P) for j in range(2)] for b in range(2)]
        wo = at(A_T, KT, D)
        xr = at(A_HT, 2, D)
        x1 = at(A_HT + 2048, 2, D)
        gate1, gate2, fin_g = (at(A_T + 8192 + 1024 * j, D) for j in range(3))
        diag = at(A_YA, KT, P)
        m1 = [at(A_HT + 2048 + 512 * b, T) for b in range(2)]
        m2 = [at(A_HT + 2048 + 512 * b + 256, T) for b in range(2)]
        junk2 = at(A_YA + 1024, 2, D)
        res = at(A_T, D)
        xn = at(A_MG, 2, D)
        h2 = at(A_T, KT, T)
        xg = at(A_YA + 4096, KT, 2 * SLOTS)
        o = A_T + 2048
        hot = at(o, 2, 2, SLOTS)
        o += 256
        hotw = [at(o + 256 * b, 2, 2, SLOTS) for b in range(2)]
        o += 512
        ct = [at(o + 256 * b, 2, P) for b in range(2)]
        o += 512
        sh = [at(o + 256 * b, 256) for b in range(2)]
        o += 512
        gm = [at(o + 256 * b, 256) for b in range(2)]
        o += 512
        gT = [at(o + 256 * b, 2, P) for b in range(2)]
        o += 512
        ys = [at(o + 512 * b, 512) for b in range(2)]
        o += 1024
        lg = at(o, 2, NG + NE)
        o += 72
        rt_g = at(o, 2, 4, NG)
        o += 32
        rt = at(o, 12, 2, NE)
        o += 12 * 64
        rcol = at(o, 16, 2)
        o += 32
        rank = at(o, 2, NE + 2)
        o += 2 * (NE + 2)
        assert o <= A_T + 8192
        ring = [at(SLOT * s, SLOT) for s in range(6)]
        SL = {("w1", 0): 1, ("w3", 0): 2, ("w2", 0): 3, ("w1", 1): 4, ("w3", 1): 5, ("w2", 1): 0}

        def wslot(kind, b):
            s = ring[SL[kind, b]]
            return s.rearrange("p (k n) -> p k n", n=D if kind == "w2" else F)

        ACC = [[bank[0], bank[1]], [bank[2], bank[3]]]
        HB, YB, TT, XB = bank[4:8]

        cm = "(r c) d -> c r d"
        x_cm = x[0].rearrange(cm, r=ROWS)
        out_cm = out[0].rearrange(cm, r=ROWS)
        wi_v = w_in[0].rearrange("(k p) n -> p k n", p=P)
        wm_v = w_mod[0].rearrange("(k p) n -> p k n", p=P)
        lru_v = [[w[0, d].rearrange("h i j -> i h j") for w in (lru_wa, lru_wx)] for d in range(2)]
        wpa_v, wpb_v, wo_v = (w[0].rearrange("(k p) n -> p k n", p=P) for w in (w_proj_a, w_proj_b, w_out))
        w1_v, w3_v, w2_v = (w[0].rearrange("e (k p) n -> e p k n", p=P) for w in (w1, w3, w2))
        rows = [(conv_w[0], 4), (conv_b, 1), (lru_ba[0], 2), (lru_bx[0], 2), (lru_lam[0], 2), (hg_lb, 2),
                (hg_norm_g, 1), (norm1_g, 1), (norm2_g, 1)]

        def this(h, d=None):
            return h + 2 if d is None else 2 * h + d + 3

        def last(h, d=None):
            return h + 1 if d is None else 2 * h + d + 1

        HEAD_SEMS = ("a_mm q_mm ff_mm fb_mm v_mm og_mm gb_mm mod_mm rms_mm a_out sq_out ay_out ff_out fb_out "
                     "v_out og_out ga_out gb_out osq_out orms_out hp_out conv_out qs_out ya_out mod_out on_out "
                     "yb_out").split()
        DIR_SEMS = ("kdt_mm att_mm kv_a kv_b inter_mm rg_out "
                     " ig_out tz_out ln_out aa_out exps_out ec_out e4_out e1_out kdT_out sqrt_out g_out lc_out w_out prod_k prod_q att_out chain_a chain_b scan_out iu_out b_out kdc_out qe3_out ra_mm ix_mm").split()
        MOE_SEMS = "mc0 mc1 acc_read hotc".split()
        EXP_SEMS = "mh mt my mx sh gm ctc gtc ysc hw xgc".split()

        block = es.enter_context(nc.Block())

        @block.sync
        def _(sp):
            r0 = 0
            for v, n in rows:
                sp.dma_start(prows[r0:r0 + 8 * n, 0, :], v.rearrange("a (h n) -> (a h) n", n=P)).then_inc(S("par_in"), 16)
                r0 += 8 * n
            sp.dma_start(prows[0:48, 1, :], b_mod[0].rearrange("(h n) -> h n", n=P)).then_inc(S("par_in"), 16)
            sp.dma_start(prows[48:56, 1, :], c[0].rearrange("(h n) -> h n", n=P)).then_inc(S("par_in"), 16)
            sp.dma_start(prows[56:64, 1, :], c_ctx.rearrange("(h n) -> h n", n=P)).then_inc(S("par_in"), 16)
            for t in range(2):
                sp.dma_start(tok[:, t, :], x_cm[32 * t:32 * t + 32]).then_inc(S("x_in"), 16)
            for t in range(2):
                sp.dma_start(tok[:, 2 + t, :], ctx_in[0, P * t:P * t + P, :]).then_inc(S("ctx_in"), 16)
            for i in range(8):
                sp.dma_start(wpro[i], wm_v[:, :, T * i:T * i + T]).then_inc(S(f"pro_in{i // 2}"), 16)

            def head_loads(h, first):
                for n, used in zip(ORDER, ("a", "q", "q", "ff", "fb", "v", "og", "og", "gb")):
                    if not first:
                        sp.wait_ge(S(used + "_mm"), last(h))
                    elif n == "gb":
                        sp.wait_ge(S("pro_mm"), 1)
                    sp.dma_start(wblk[n], wi_v[:, :, bass.ds(BLK[n] * D + h * P, P)]).then_inc(S("in_" + SHARED.get(n, n)), 16)
                    if n == "fb":
                        if first:
                            sp.wait_ge(S("pro_mm"), 1)
                        else:
                            sp.wait_ge(S("ix_mm"), last(h, 1))
                        for d in range(2):
                            for j in range(2):
                                sp.dma_start(wlru[:, 2 * d + j, :], lru_v[d][j][:, h, :]).then_inc(S("in_lru"), 16)
                if not first:
                    sp.wait_ge(S("mod_mm"), last(h))
                sp.dma_start(wmod, wm_v[:, :, bass.ds(2 * D + h * 512, 512)]).then_inc(S("in_wmod"), 16)

            head_loads(0, True)
            sp.dma_start(w_rt[:, :, 0:NG], w_rg[0].rearrange("(k p) n -> p k n", p=P)).then_inc(S("rt_in"), 16)
            sp.dma_start(w_rt[:, :, NG:], w_re[0].rearrange("(k p) n -> p k n", p=P)).then_inc(S("rt_in"), 16)
            sp.dma_start(b_rt[:, 0:NG], b_rg.to_broadcast([P, NG])).then_inc(S("rt_in"), 16)
            sp.dma_start(b_rt[:, NG:], b_re.to_broadcast([P, NE])).then_inc(S("rt_in"), 16)
            with sp.Fori(1, HEADS) as h:
                head_loads(h, False)

            def proj_loads(m, b, first):
                if first:
                    sp.wait_ge(S("ff_mm"), this(HEADS - 1))
                else:
                    sp.wait_ge(S(f"proj_mm{b}"), (m - b) // 2 if isinstance(m, int) else m)
                mm = m if isinstance(m, int) else 2 * m + b
                sp.dma_start(wp[b][0], wpa_v[:, :, bass.ds(mm * P, P)]).then_inc(S(f"wp_in{b}"), 16)
                sp.dma_start(wp[b][1], wpb_v[:, :, bass.ds(mm * P, P)]).then_inc(S(f"wp_in{b}"), 16)

            for b in range(2):
                proj_loads(b, b, True)
            sp.wait_ge(S("yb_out"), this(HEADS - 1))
            sp.wait_ge(S("ya_out"), this(HEADS - 1))
            for i in range(2):
                sp.dma_start(wo[:, 4 * i:4 * i + 4, :], wo_v[:, 4 * i:4 * i + 4, :]).then_inc(S("wo_in"), 16)
            sp.wait_ge(S("gb_mm"), this(HEADS - 1))
            for t in range(2):
                sp.dma_start(xr[:, t, :], x_cm[32 * t:32 * t + 32]).then_inc(S("xr_in"), 16)
            sp.dma_start(fin_g, final_g[None, :].to_broadcast([P, D])).then_inc(S("fg_in"), 16)
            with sp.Fori(1, KT // 2) as m:
                for b in range(2):
                    proj_loads(m, b, False)

            src = {"w1": w1_v, "w3": w3_v, "w2": w2_v}
            kinds = [(k, b) for b in range(2) for k in ("w1", "w3", "w2")]
            for k, b in kinds:
                if (k, b) == ("w2", 1):
                    sp.wait_ge(S("proj_mm1"), KT // 2)
                sp.dma_start(wslot(k, b), src[k][b]).then_inc(S(f"in_{k}{b}"), 16)
            sp.wait_ge(S("rounds_ready"), 1)
            n_rounds = sp.value_load(rcnt_i[0:1, 0:1], min_val=1, max_val=T // SLOTS)
            with sp.Fori(1, n_rounds * PAIRS) as q:
                e = [sp.snap((q & (PAIRS - 1)) * 2 + b) for b in range(2)]
                for k, b in kinds:
                    sp.wait_ge(S("my" if k == "w2" else "mh"), last(q, b))
                    if (k, b) == kinds[0]:
                        sp.sem_inc(S("slot_free"), 1)
                    sp.dma_start(wslot(k, b), src[k][e[b]]).then_inc(S(f"in_{k}{b}"), 16)
            for t in range(2):
                sp.wait_ge(S("y_out"), t + 1)
                sp.dma_start(out_cm[32 * t:32 * t + 32], xn[:, t, :]).then_inc(S("stored"), 16)
            sp.wait_ge(S("stored"), 32)

        @block.gpsimd
        def _(pool):
            for const in (ident, resets, causal[0], causal[1], before, ones):
                i = pool.memset(const[:], 1.0)
            i.then_inc(S("consts"), 1)
            pool.wait_ge(S("consts"), 1)

            def keep(v, base, pattern, per_partition, op=ALU.is_ge):
                return pool.affine_select(out=v, in_=v, compare_op=op, fill=0.0, base=base, pattern=pattern,
                                          channel_multiplier=per_partition)
            keep(ident[:], 0, [[1, P]], -1, ALU.is_equal).then_inc(S("ident_set"), 1)
            pool.memset(mean_w[:], 1.0 / P)
            pool.memset(resets[:, 0:T:CH], 0.0)
            keep(before[:], -1, [[1, P]], -1)
            blocks = [m[:].rearrange("p (a b) -> p a b", b=CH) for m in causal]
            keep(blocks[0], 0, [[CH, P // CH], [1, CH]], -1)
            keep(blocks[1], 0, [[-CH, P // CH], [-1, CH]], 1).then_inc(S("consts"), 1)
            pool.wait_ge(S("consts"), 2)
            keep(blocks[0], 0, [[-CH, P // CH], [0, CH]], 1)
            keep(blocks[1], CH - 1, [[CH, P // CH], [0, CH]], -1)
            pool.iota(slot_no[:], pattern=[[1, SLOTS]], base=0, channel_multiplier=0,
                      allow_small_or_imprecise_dtypes=True)
            pool.memset(zb[:], 0.0).then_inc(S("const_set"), 1)
            for n in HEAD_SEMS + MOE_SEMS:
                pool.sem_inc(S(n), 1)
            for n in DIR_SEMS + EXP_SEMS:
                pool.sem_inc(S(n), 2)
            pool.wait_ge(S("pro_mm"), 1)
            pool.wait_ge(S("tok_T"), 8)
            for d in range(2):
                pool.memset(att[d], 0.0)
            pool.memset(vbd, 0.0)
            pool.memset(a_pad, 0.0)
            pool.memset(a_edge, 0.0)
            for d in range(2):
                pool.memset(rcx[d], 0.0)
            last_set = pool.memset(etot[:], 0.0)
            last_set.then_inc(S("zero_set"), 1)
            pool.wait_ge(S("zero_set"), 1)
            with pool.Fori(0, HEADS) as h:
                def gates(d):
                    pool.wait_ge(S("ig_out"), this(h, d))
                    pool.wait_ge(S("conv_out"), this(h))
                    pool.tensor_tensor(ig[d], ig[d], u, ALU.mult).then_inc(S("iu_out"), 1)

                def prods(d):
                    pool.wait_ge(S("ec_out"), this(h, d))
                    pool.tensor_tensor(ec[d], ec[d], kk[d][:, T:], ALU.mult).then_inc(S("kdc_out"), 1)
                    pool.wait_ge(S("exps_out"), this(h, d))
                    pool.wait_ge(S("qs_out"), this(h))
                    pool.tensor_tensor(e3[d], e3[d], qs, ALU.mult).then_inc(S("qe3_out"), 1)

                def inputs(d):
                    pool.wait_ge(S("sqrt_out"), this(h, d))
                    pool.wait_ge(S("iu_out"), this(h, d))
                    pool.tensor_tensor(tz[d], tz[d], ig[d], ALU.mult).then_inc(S("b_out"), 1)

                gates(0)
                prods(0)
                gates(1)
                prods(1)
                inputs(0)
                inputs(1)

        @block.tensor
        def _(pe):
            mm = pe.matmul

            def down_k(dst, w, rhs, start=True):
                for k in range(KT):
                    i = mm(dst, w(k), rhs(k), start=start and k == 0, stop=k == KT - 1)
                return i

            pe.wait_ge(S("ident_set"), 1)
            pe.wait_ge(S("par_in"), 16 * (len(rows) + 3))
            pe.transpose(bank[7][:, 0:P], prows[:, 0, :], ident[:])
            pe.transpose(bank[7][:, P:P + 64], prows[0:64, 1, :], ident[0:64, 0:64]).then_inc(S("par_T"), 1)
            for k in range(KT):
                if k == 0:
                    pe.wait_ge(S("xs_out"), 4)
                if k >= 2:
                    pe.wait_ge(S("tok_copy"), k - 1)
                for t in range(4):
                    i = pe.transpose(PJ[k % 2][:, P * t:P * t + P], tok[:, t, P * k:P * k + P], ident[:])
                i.then_inc(S("tok_T"), 1)
            pe.wait_ge(S("csil_out"), 1)
            for i in range(8):
                pe.wait_ge(S(f"pro_in{i // 2}"), 32)
                for j in range(2):
                    m = 2 * i + j
                    ins = down_k(bank[6][:, 2 * m:2 * m + 2], lambda k: wpro[i][:, k, P * j:P * j + P],
                                 lambda k: csil[:, k, :])
            ins.then_inc(S("pro_mm"), 1)
            pe.wait_ge(S("h_ct_out"), 1)
            pe.wait_ge(S("edges_out"), 1)
            pe.wait_ge(S("const_set"), 1)
            pe.wait_ge(S("zero_set"), 1)

            with pe.Fori(0, HEADS) as h:
                h_edge_x = lambda k: h_ct[:, k, 0:EDGE + T]
                h_x = lambda k: h_ct[:, k, EDGE:EDGE + T]
                h_all = lambda k: h_ct[:, k, EDGE:]
                W = lambda n: (lambda k: wblk[n][:, k, :])

                def loaded(n, times=1):
                    pe.wait_ge(S("in_" + n), (h + 1) * (16 * times))

                def gate_products(d):
                    if d == 0:
                        loaded("lru", 4)
                        pe.wait_ge(S("conv_out"), this(h))
                        pe.wait_ge(S("rg_out"), last(h, 1))
                        pe.wait_ge(S("ig_out"), last(h, 1))
                    else:
                        pe.wait_ge(S("rg_out"), this(h, 0))
                        pe.wait_ge(S("ig_out"), this(h, 0))
                    mm(GT[0][:, 0:TU], wlru[:, 2 * d, :], u, start=True, stop=True).then_inc(S("ra_mm"), 1)
                    mm(GT[1][:, 0:TU], wlru[:, 2 * d + 1, :], u, start=True, stop=True).then_inc(S("ix_mm"), 1)

                def decayed_keys_T(d):
                    pe.wait_ge(S("prod_k"), this(h, d))
                    pe.wait_ge(S("kdc_out"), this(h, d))
                    if d == 0:
                        pe.wait_ge(S("chain_b"), last(h, 1))
                    else:
                        pe.wait_ge(S("chain_b"), this(h, 0))
                    for t in range(2):
                        pe.transpose(TB[:, P * t:P * t + P], e4[d][:, P * t:P * t + P], ident[:])
                    for t in range(2):
                        i = pe.transpose(TB[:, P * (2 + t):P * (3 + t)], ec[d][:, P * t:P * t + P], ident[:])
                    i.then_inc(S("kdt_mm"), 1)

                def attention(d):
                    pe.wait_ge(S("prod_q"), this(h, d))
                    if d == 0:
                        pe.wait_ge(S("orms_out"), last(h))
                    else:
                        pe.wait_ge(S("att_out"), this(h, 0))
                    for t in range(2):
                        s = slice(P * t, P * t + P)
                        mm(AB[:, s], e2[d][:, s], e1[d][:, s], start=True, stop=True)
                    pe.wait_ge(S("kdT_out"), this(h, d))
                    pe.wait_ge(S("v_out"), this(h))
                    for t in range(2):
                        i = mm(AB[:, 256:384], kdT[d][:, 2 + t, :], vv[:, 2 + t, :], start=t == 0, stop=t == 1)
                    i.then_inc(S("att_mm"), 1)

                def chunk_states(d):
                    ta, tb = (0, 1) if d == 0 else (1, 0)
                    if d == 0:
                        pe.wait_ge(S("chain_a"), last(h, 1))
                    else:
                        pe.wait_ge(S("chain_a"), this(h, 0))
                    mm(KB[:], kdT[d][:, ta, :], vbd[:, ta].rearrange("p a b -> p (a b)"),
                       start=True, stop=True).then_inc(S("kv_a"), 1)
                    s = slice(0, 384) if d == 0 else slice(128, 512)
                    mm(TB[:, s], kdT[d][:, tb, :], vbd[:, tb].rearrange("p a b -> p (a b)")[:, s],
                       start=True, stop=True).then_inc(S("kv_b"), 1)

                def outputs(d):
                    if d == 0:
                        pe.wait_ge(S("on_out"), last(h))
                    pe.wait_ge(S("att_out"), this(h, d))
                    for t in range(2):
                        s = slice(P * t, P * t + P)
                        mm(OB[:, s], vv[:, t, :], att[d][:, t, :], start=d == 0 and t == 0, stop=False,
                           skip_group_check=True)
                    pe.wait_ge(S("qe3_out"), this(h, d))
                    pe.wait_ge(S("chain_a"), this(h, d))
                    pe.wait_ge(S("chain_b"), this(h, d))
                    for j in range(NCH):
                        cj = j if d == 0 else NCH - 1 - j
                        s = slice(CH * cj, CH * cj + CH)
                        i = mm(OB[:, s], st[d][:, j, :], e3[d][:, s], start=False, stop=d == 1,
                               skip_group_check=True)
                    i.then_inc(S("inter_mm"), 1)

                loaded("a")
                pe.wait_ge(S("gb_out"), last(h))
                down_k(PJ[0][:, 0:EDGE + T], W("a"), h_edge_x).then_inc(S("a_mm"), 1)
                loaded("q", 2)
                pe.wait_ge(S("mod_out"), last(h))
                down_k(PJ[1][:, 0:T], W("q"), h_x)
                down_k(PJ[1][:, T:], W("ay"), h_x).then_inc(S("q_mm"), 1)
                loaded("ff")
                pe.wait_ge(S("a_out"), this(h))
                down_k(PJ[0][:], W("ff"), h_all).then_inc(S("ff_mm"), 1)
                gate_products(0)
                loaded("fb")
                pe.wait_ge(S("ay_out"), this(h))
                pe.wait_ge(S("qs_out"), this(h))
                down_k(PJ[1][:], W("fb"), h_all).then_inc(S("fb_mm"), 1)
                gate_products(1)
                loaded("v")
                pe.wait_ge(S("ff_out"), this(h))
                for t in range(4):
                    i = down_k(PJ[0][:, P * t:P * t + P], lambda k: h_ct[:, k, EDGE + P * t:EDGE + P * t + P], W("v"))
                i.then_inc(S("v_mm"), 1)
                decayed_keys_T(0)
                loaded("og", 2)
                pe.wait_ge(S("fb_out"), this(h))
                down_k(PJ[1][:, 0:T], W("og"), h_x)
                down_k(PJ[1][:, T:], W("ga"), h_x).then_inc(S("og_mm"), 1)
                attention(0)
                chunk_states(0)
                loaded("gb")
                pe.wait_ge(S("v_out"), this(h))
                down_k(PJ[0][:, 0:T], W("gb"), h_x).then_inc(S("gb_mm"), 1)
                decayed_keys_T(1)
                loaded("wmod")
                pe.wait_ge(S("ga_out"), this(h))
                for m in range(4):
                    i = down_k(PJ[1][:, m:m + 1], lambda k: wmod[:, k, P * m:P * m + P], lambda k: csil[:, k, 0:1])
                i.then_inc(S("mod_mm"), 1)
                attention(1)
                chunk_states(1)
                outputs(0)
                outputs(1)
                pe.wait_ge(S("osq_out"), this(h))
                pe.wait_ge(S("att_out"), this(h, 1))
                mm(AB[:, 0:T], mean_w[:], osq, start=True, stop=True).then_inc(S("rms_mm"), 1)

            pe.wait_ge(S("yb_out"), this(HEADS - 1))
            pe.wait_ge(S("ya_out"), this(HEADS - 1))
            pe.wait_ge(S("gb_out"), this(HEADS - 1))
            pe.wait_ge(S("mod_out"), this(HEADS - 1))
            def project(i, b, first):
                pe.wait_ge(S(f"wp_in{b}"), 32 * (i + 1))
                if not first:
                    pe.wait_ge(S(f"merged_out{b}"), i)
                down_k(PJ[b][:, 0:T], lambda k: wp[b][0][:, k, :], lambda k: ya_g[:, k, :])
                down_k(PJ[b][:, T:], lambda k: wp[b][1][:, k, :], lambda k: yb_g[:, k, :]).then_inc(S(f"proj_mm{b}"), 1)
            for b in range(2):
                project(0, b, True)
            with pe.Fori(1, KT // 2) as i:
                for b in range(2):
                    project(i, b, False)
            for v in range(2):
                pe.wait_ge(S("diag_out"), v + 1)
                if v == 0:
                    pe.wait_ge(S("orms_out"), this(HEADS - 1))
                    pe.wait_ge(S("on_out"), this(HEADS - 1))
                else:
                    pe.wait_ge(S("gate_rows"), 1)
                for hf in range(2):
                    i = mm(bank[6 + hf][:], ones[:, 0:P],
                           diag[:, 4 * hf:4 * hf + 4, :].rearrange("p a b -> p (a b)"), start=True, stop=True)
                i.then_inc(S("gate_mm"), 1)
            pe.wait_ge(S("wo_in"), 32)
            pe.wait_ge(S("merged_out1"), KT // 2)
            pe.wait_ge(S("gate_rows"), 2)
            for t in range(2):
                for hf in range(2):
                    i = down_k(bank[4 + 2 * t + hf][:] if t == 0 else bank[hf][:],
                               lambda k: merged[:, k, P * t:P * t + P],
                               lambda k: wo[:, k, 512 * hf:512 * hf + 512])
                i.then_inc(S("wo_mm"), 1)
            for k in range(KT):
                if k == 0:
                    pe.wait_ge(S("xn_out"), 2)
                if k >= 2:
                    pe.wait_ge(S("h2_out"), k - 1)
                for t in range(2):
                    i = pe.transpose(bank[6 + k % 2][:, P * t:P * t + P], xn[:, t, P * k:P * k + P], ident[:])
                i.then_inc(S("xn_T"), 1)
            pe.wait_ge(S("rt_in"), 64)
            pe.wait_ge(S("h2_out"), KT)
            for t in range(2):
                i = down_k(bank[6][:, 64 * t:64 * t + NG + NE], lambda k: h2[:, k, P * t:P * t + P],
                           lambda k: w_rt[:, k, :])
            i.then_inc(S("rt_mm"), 1)
            pe.wait_ge(S("sel_out"), 1)
            sel = rt[:, 8]
            mm(bank[7][:, 0:NE], before[:], sel[:, 0, :], start=True, stop=True)
            mm(bank[7][:, NE:2 * NE], ones[:, 0:P], sel[:, 0, :], start=True, stop=False)
            mm(bank[7][:, NE:2 * NE], before[:], sel[:, 1, :], start=False, stop=True)
            mm(bank[7][:, 2 * NE:3 * NE], ones[:, 0:P], sel[:, 0, :], start=True, stop=False)
            mm(bank[7][:, 2 * NE:3 * NE], ones[:, 0:P], sel[:, 1, :], start=False, stop=True).then_inc(S("rank_mm"), 1)

            def gather(half):
                for k in range(4):
                    kt = 4 * half + k
                    for t in range(2):
                        i = mm(XB[:, P * k:P * k + P], xn[:, t, P * kt:P * kt + P],
                               hot[:, t].rearrange("p e s -> p (e s)"), start=t == 0, stop=t == 1)
                i.then_inc(S("mx"), 1)

            def up(b, q):
                pe.wait_ge(S("gm"), last(q, 1) if b == 0 else this(q, 0))
                for col, kind in ((0, "w1"), (256, "w3")):
                    pe.wait_ge(S(f"in_{kind}{b}"), (q + 1) * 16)
                    w = wslot(kind, b)
                    for k in range(KT):
                        for hf in range(2):
                            i = mm(HB[64 * hf:64 * hf + 64, col:col + 256], xg[:, k, SLOTS * b:SLOTS * b + SLOTS],
                                   w[:, k, 256 * hf:256 * hf + 256], start=k == 0, stop=k == KT - 1)
                i.then_inc(S("mh"), 1)

            def turn(b, q):
                pe.wait_ge(S("hw"), this(q, b))
                pe.wait_ge(S("gtc"), last(q, 1) if b == 0 else this(q, 0))
                pe.wait_ge(S("ctc"), last(q, 1) if b == 0 else this(q, 0))
                for t in range(2):
                    pe.transpose(TT[:, P * t:P * t + P], hotw[b][:, t].rearrange("p a s -> p (a s)"), ident[:])
                pe.wait_ge(S("gm"), this(q, b))
                for j in range(2):
                    i = pe.transpose(TT[:, 256 + P * j:256 + P * j + P], gm[b][:, P * j:P * j + P], ident[:])
                i.then_inc(S("mt"), 1)

            def down(b, q):
                pe.wait_ge(S(f"in_w2{b}"), (q + 1) * 16)
                pe.wait_ge(S("gtc"), this(q, b))
                pe.wait_ge(S("ysc"), last(q, 1) if b == 0 else this(q, 0))
                w = wslot("w2", b)
                for kk_ in range(4):
                    fh, j = kk_ // 2, kk_ % 2
                    for hf in range(2):
                        i = mm(YB[64 * hf:64 * hf + 64, :], gT[b][:, j, 64 * fh:64 * fh + 64],
                               w[:, kk_, 512 * hf:512 * hf + 512], start=kk_ == 0, stop=kk_ == 3)
                i.then_inc(S("my"), 1)

            def combine(b, q):
                pe.wait_ge(S("ysc"), this(q, b))
                pe.wait_ge(S("ctc"), this(q, b))
                for t in range(2):
                    for hf in range(2):
                        s = slice(64 * hf, 64 * hf + 64)
                        i = mm(ACC[t][hf][:], ct[b][s, t, :], ys[b][s, :], start=False, stop=False,
                               skip_group_check=True)
                i.then_inc(S(f"mc{b}"), 1)

            pe.wait_ge(S("rounds_ready"), 1)
            n_rounds = pe.value_load(rcnt_i[0:1, 0:1], min_val=1, max_val=T // SLOTS)
            with pe.Fori(0, n_rounds) as r:
                pe.wait_ge(S("acc_read"), r + 1)
                for t in range(2):
                    for hf in range(2):
                        mm(ACC[t][hf][:], zb[:, 0:P], zb[:], start=True, stop=False, skip_group_check=True)
                for half in range(2):
                    pe.wait_ge(S("hotc"), r * (PAIRS + 1) + 2)
                    g = r * (PAIRS + 1)
                    pe.wait_ge(S("xgc"), last(g, 1) if half == 0 else this(g, 0))
                    gather(half)
                with pe.Fori(0, PAIRS) as p:
                    q = r * PAIRS + p
                    g = r * (PAIRS + 1) + p
                    pe.wait_ge(S("xgc"), this(g, 1))
                    up(0, q)
                    combine(1, q - 1)
                    turn(0, q)
                    down(0, q)
                    up(1, q)
                    combine(0, q)
                    turn(1, q)
                    pe.wait_ge(S("hotc"), g + 3)
                    pe.wait_ge(S("xgc"), this(g, 1))
                    gather(0)
                    down(1, q)
                    pe.wait_ge(S("xgc"), this(g + 1, 0))
                    gather(1)
                combine(1, r * PAIRS + PAIRS - 1)

        @block.scalar
        def _(act):
            A = act.activation
            for t in range(4):
                act.wait_ge(S("x_in" if t < 2 else "ctx_in"), 32)
                A(junk[:, t, :], tok[:, t, :], ACT.Square, accum_out=ssq[:, t:t + 1]).then_inc(S("ssq_out"), 1)
            act.wait_ge(S("ms_out"), 1)
            A(rstd[:], rstd[:], ACT.Sqrt).then_inc(S("rms_out"), 1)
            act.wait_ge(S("par_copy"), 1)
            A(csil[:], par2[:, 48:64].rearrange("p (s k) -> p k s", s=2), ACT.Silu).then_inc(S("csil_out"), 1)
            act.wait_ge(S("sp0"), 1)
            A(spt[:, 0, :], spt[:, 0, :], ACT.Exp, scale=-1.0).then_inc(S("sp1"), 1)
            A(par[:, V_LBV, :], spt[:, 3, 0:8], ACT.Sigmoid).then_inc(S("lb_out"), 1)
            for k in range(KT):
                act.wait_ge(S("tok_T"), k + 1)
                A(h_ct[:, k, EDGE:], PJ[k % 2][:], ACT.Copy).then_inc(S("tok_copy"), 1)
            act.wait_ge(S("aff1_out"), 1)
            act.wait_ge(S("tok_copy"), KT)
            for k in range(0, KT, 2):
                for s in range(2):
                    i = A(h_ct[:, k, EDGE + T * s:EDGE + T * s + T], h_ct[:, k, EDGE + T * s:EDGE + T * s + T], ACT.Identity,
                          scale=aff1[:, s, k:k + 1], bias=modA[:, k, s:s + 1])
            i.then_inc(S("h_ct_out"), 1)
            act.wait_ge(S("zero_set"), 1)

            with act.Fori(0, HEADS) as h:
                def col(v):
                    return hp[:, v:v + 1]

                act.wait_ge(S("a_mm"), this(h))
                act.wait_ge(S("conv_out"), last(h))
                A(a_pad[:, 2:2 + T].rearrange("p (r c) -> p r c", r=ROWS),
                  PJ[0][:, EDGE:EDGE + T].rearrange("p (c r) -> p r c", r=ROWS), ACT.Copy)
                A(a_edge[:, 2:2 + EDGE], PJ[0][:, 0:EDGE], ACT.Copy).then_inc(S("a_out"), 1)
                act.wait_ge(S("q_mm"), this(h))
                act.wait_ge(S("qs_out"), last(h))
                A(sq, PJ[1][:, 0:T], ACT.Sigmoid).then_inc(S("sq_out"), 1)
                act.wait_ge(S("ya_out"), last(h))
                A(gl, PJ[1][:, T:], ACT.Gelu_apprx_tanh).then_inc(S("ay_out"), 1)

                def forget(d, bank_, mm_sem, out_sem):
                    act.wait_ge(S(mm_sem), this(h))
                    act.wait_ge(S("ln_out"), last(h, d))
                    act.wait_ge(S("g_out"), last(h, d))
                    A(gg[d], bank_[:], ACT.Sigmoid).then_inc(S(out_sem), 1)

                def gates(d):
                    act.wait_ge(S("ra_mm"), this(h, d))
                    act.wait_ge(S("hp_out"), this(h))
                    act.wait_ge(S("aa_out"), last(h, d))
                    A(rg[d], GT[0][:, 0:TU], ACT.Sigmoid, bias=col(V_BA + d)).then_inc(S("rg_out"), 1)
                    act.wait_ge(S("ix_mm"), this(h, d))
                    act.wait_ge(S("b_out"), last(h, d))
                    A(ig[d], GT[1][:, 0:TU], ACT.Sigmoid, bias=col(V_BX + d)).then_inc(S("ig_out"), 1)
                    act.wait_ge(S("scan_out"), last(h, d))
                    act.wait_ge(S("rg_out"), this(h, d))
                    A(tz[d], rg[d], ACT.Tanh, scale=col(V_PSP + d)).then_inc(S("tz_out"), 1)

                def logs(d):
                    act.wait_ge(S("g_out"), this(h, d))
                    act.wait_ge(S("lc_out"), last(h, d))
                    A(lf[d], gg[d], ACT.Ln).then_inc(S("ln_out"), 1)

                def exps(d):
                    act.wait_ge(S("rg_out"), this(h, d))
                    act.wait_ge(S("scan_out"), last(h, d))
                    A(aa[d], rg[d], ACT.Exp, scale=col(V_NSP + d)).then_inc(S("aa_out"), 1)
                    act.wait_ge(S("lc_out"), this(h, d))
                    act.wait_ge(S("kdt_mm"), last(h, d))
                    A(ec[d], rcx[d], ACT.Exp).then_inc(S("ec_out"), 1)
                    A(e4[d], d4[d], ACT.Exp).then_inc(S("e4_out"), 1)
                    act.wait_ge(S("att_mm"), last(h, d))
                    A(e1[d], dm[d], ACT.Exp)
                    A(e2[d], dm[d], ACT.Exp, scale=-1.0).then_inc(S("e1_out"), 1)
                    act.wait_ge(S("inter_mm"), last(h, d))
                    act.wait_ge(S("chain_b"), last(h, d))
                    A(etot[:, d, :], lcx[d][:, (CH - 1 if d == 0 else 0):T:CH], ACT.Exp)
                    A(e3[d], lcx[d], ACT.Exp).then_inc(S("exps_out"), 1)

                forget(0, PJ[0], "ff_mm", "ff_out")
                gates(0)
                logs(0)
                exps(0)
                forget(1, PJ[1], "fb_mm", "fb_out")
                gates(1)
                logs(1)
                exps(1)
                act.wait_ge(S("v_mm"), this(h))
                act.wait_ge(S("zero_set"), 1)
                act.wait_ge(S("inter_mm"), last(h, 1))
                for j in range(P // CH):
                    s = slice(CH * j, CH * j + CH)
                    A(vbd[s, :, j, :], PJ[0][s, 0:2 * P].rearrange("p (t n) -> p t n", t=2), ACT.Copy)
                A(vv.rearrange("p a b -> p (a b)"), PJ[0][:], ACT.Copy).then_inc(S("v_out"), 1)

                def keys_out(d):
                    act.wait_ge(S("kdt_mm"), this(h, d))
                    act.wait_ge(S("kv_b"), last(h, d))
                    A(kdT[d].rearrange("p a b -> p (a b)"), TB[:], ACT.Copy).then_inc(S("kdT_out"), 1)

                keys_out(0)
                for d in range(2):
                    act.wait_ge(S("w_out"), this(h, d))
                    A(tz[d], tz[d], ACT.Sqrt, scale=2.0).then_inc(S("sqrt_out"), 1)
                act.wait_ge(S("og_mm"), this(h))
                act.wait_ge(S("yb_out"), last(h))
                A(sog, PJ[1][:, 0:T], ACT.Silu).then_inc(S("og_out"), 1)
                A(s_ga[:, h, :], PJ[1][:, T:], ACT.Sigmoid).then_inc(S("ga_out"), 1)
                act.wait_ge(S("gb_mm"), this(h))
                A(s_gb[:, h, :], PJ[0][:, 0:T], ACT.Sigmoid).then_inc(S("gb_out"), 1)
                keys_out(1)
                act.wait_ge(S("inter_mm"), this(h, 1))
                act.wait_ge(S("rms_mm"), last(h))
                A(osq, OB[:, 0:T], ACT.Square).then_inc(S("osq_out"), 1)
                act.wait_ge(S("rms_mm"), this(h))
                act.wait_ge(S("on_out"), last(h))
                A(orr, AB[:, 0:T], ACT.Sqrt, bias=eps_t[:, 0:1]).then_inc(S("orms_out"), 1)

            for t in range(2):
                act.wait_ge(S("x1_out"), t + 1)
                A(junk2[:, t, :], x1[:, t, :], ACT.Square, accum_out=ssq[:, t:t + 1]).then_inc(S("ssq_out"), 1)
            act.wait_ge(S("ms_out"), 2)
            A(rstd[:, 0:2], rstd[:, 0:2], ACT.Sqrt).then_inc(S("rms_out"), 1)
            act.wait_ge(S("aff2_out"), 1)
            for k in range(KT):
                act.wait_ge(S("xn_T"), k + 1)
                A(h2[:, k, :], bank[6 + k % 2][:, 0:T], ACT.Identity, scale=aff2[:, k:k + 1],
                  bias=modB[:, 8 + k:9 + k]).then_inc(S("h2_out"), 1)
            for n in range(2):
                act.wait_ge(S("rt_sub"), n + 1)
                src_ = rt_g[:, :, 1, :] if n == 0 else rcol[:, 6, :]
                A(src_, src_, ACT.Exp).then_inc(S("rt_exp"), 1)

            act.wait_ge(S("rounds_ready"), 1)
            n_rounds = act.value_load(rcnt_i[0:1, 0:1], min_val=1, max_val=T // SLOTS)
            with act.Fori(0, n_rounds) as r:
                def xg_out(half, g):
                    act.wait_ge(S("mx"), this(g, half))
                    for k in range(4):
                        kt = 4 * half + k
                        i = A(xg[:, kt, :], XB[:, P * k:P * k + P], ACT.Identity, scale=aff2[:, kt:kt + 1],
                              bias=modB[:, 8 + kt:9 + kt])
                    i.then_inc(S("xgc"), 1)

                act.wait_ge(S("mh"), last(r * PAIRS, 1))
                for half in range(2):
                    xg_out(half, r * (PAIRS + 1))
                with act.Fori(0, PAIRS) as p:
                    q = r * PAIRS + p
                    g = r * (PAIRS + 1) + p

                    def hidden(b):
                        act.wait_ge(S("mh"), this(q, b))
                        act.wait_ge(S("gm"), last(q, b))
                        A(sh[b], HB[:, 0:256], ACT.Silu).then_inc(S("sh"), 1)

                    def turned(b):
                        act.wait_ge(S("mt"), this(q, b))
                        act.wait_ge(S("my"), last(q, b))
                        A(gT[b].rearrange("p a b -> p (a b)"), TT[:, 256:512], ACT.Copy).then_inc(S("gtc"), 1)
                        act.wait_ge(S(f"mc{b}"), q + 1 if b == 0 else g + 2)
                        A(ct[b].rearrange("p a b -> p (a b)"), TT[:, 0:256], ACT.Copy).then_inc(S("ctc"), 1)

                    hidden(0)
                    turned(0)
                    hidden(1)
                    turned(1)
                    xg_out(0, g + 1)
                    xg_out(1, g + 1)

            act.wait_ge(S("ms_out"), 3)
            A(rstd[:, 0:2], rstd[:, 0:2], ACT.Sqrt).then_inc(S("rms_out"), 1)

        @block.vector
        def _(dve):
            cp, tt, ts, stt = dve.tensor_copy, dve.tensor_tensor, dve.tensor_scalar, dve.scalar_tensor_tensor

            class Chain:

                def __init__(self, name, base=0, per=None):
                    self.sem, self.base, self.n, self.per = S(name), base, 0, per

                def __call__(self, ins):
                    self.n += 1
                    ins.then_inc(self.sem, 1)
                    dve.wait_ge(self.sem, self.base + self.n)

            serial = Chain("serial_step")
            link = serial
            link(dve.memset(eps_t[:], EPS))
            dve.wait_ge(S("par_T"), 1)
            cp(par[:, 0:16, :].rearrange("p a b -> p (a b)"), bank[7][:, 0:P])
            cp(par2[:], bank[7][:, P:P + 64]).then_inc(S("par_copy"), 1)
            dve.wait_ge(S("par_copy"), 1)
            lam = par[:, V_LAM:V_LAM + 2, :].rearrange("p a b -> p (a b)")
            link(ts(spt[:, 1, :], lam, -1.0, None, ALU.mult))
            tt(spt[:, 3, 0:8], par[:, V_LB, :], par[:, V_LB + 1, :], ALU.subtract)
            tt(spt[:, 0, :], spt[:, 1, :], lam, ALU.max).then_inc(S("sp0"), 1)
            dve.wait_ge(S("ssq_out"), 4)
            ts(rstd[:], ssq[:], 1.0 / D, EPS, ALU.mult, ALU.add).then_inc(S("ms_out"), 1)
            dve.wait_ge(S("rms_out"), 1)
            link(dve.reciprocal(rstd[:], rstd[:]))
            for t in range(4):
                ts(tok[:, t, :], tok[:, t, :], rstd[:, t:t + 1], None, ALU.mult).then_inc(S("xs_out"), 1)
            dve.wait_ge(S("sp1"), 1)
            e_, s_, s2 = spt[:, 0, :], spt[:, 2, :], spt[:, 4, :]
            link(ts(s_, e_, 2.0, None, ALU.add))
            link(dve.reciprocal(s_, s_))
            link(tt(s_, s_, e_, ALU.mult))
            link(tt(s2, s_, s_, ALU.mult))
            acc = spt[:, 0, :]
            link(ts(acc, s2, 1.0 / 17, None, ALU.mult))
            for n in range(15, 1, -2):
                link(stt(acc, acc, 1.0 / n, s2, ALU.add, ALU.mult))
            link(stt(acc, acc, 1.0, s_, ALU.add, ALU.mult))
            link(ts(acc, acc, 2.0, None, ALU.mult))
            link(stt(acc, spt[:, 1, :], 0.0, acc, ALU.max, ALU.add))
            sp2 = lambda v: par[:, v:v + 2, :].rearrange("p a b -> p (a b)")
            ts(sp2(V_PSP), acc, 8.0, None, ALU.mult)
            ts(sp2(V_NSP), acc, -8.0, None, ALU.mult)
            dve.wait_ge(S("lb_out"), 1)
            ts(par[:, V_OML, :], par[:, V_LBV, :], -1.0, 1.0, ALU.mult, ALU.add).then_inc(S("par_done"), 1)
            dve.wait_ge(S("pro_mm"), 1)
            link(tt(modA[:], bank[6][:, 0:32].rearrange("p (m s) -> p m s", s=2),
               par2[:, 0:16].unsqueeze(2).to_broadcast([P, 16, 2]), ALU.add))
            link(ts(aff1[:], modA[:, 8:16, :].rearrange("p m s -> p s m"), 1.0, None, ALU.add))
            tt(aff1[:], aff1[:], par[:, V_N1, :].unsqueeze(1).to_broadcast([P, 2, KT]), ALU.mult).then_inc(S("aff1_out"), 1)
            dve.wait_ge(S("aff1_out"), 1)
            dve.wait_ge(S("tok_copy"), KT)
            for k in range(1, KT, 2):
                for s in range(2):
                    i = ts(h_ct[:, k, EDGE + T * s:EDGE + T * s + T], h_ct[:, k, EDGE + T * s:EDGE + T * s + T], aff1[:, s, k:k + 1],
                           modA[:, k, s:s + 1], ALU.mult, ALU.add)
            link(i)
            dve.wait_ge(S("h_ct_out"), 1)
            cp(h_ct[:, :, 0:3], h_ct[:, :, EDGE + T:EDGE + T + 3])
            cp(h_ct[:, :, 3:EDGE], h_ct[:, :, EDGE + 2 * T - 3:]).then_inc(S("edges_out"), 1)
            dve.wait_ge(S("par_done"), 1)
            dve.wait_ge(S("zero_set"), 1)

            N_STEP = 13
            with dve.Fori(0, HEADS) as h:
                link = Chain("head_step", h * N_STEP)

                def col(v):
                    return hp[:, v:v + 1]

                dve.wait_ge(S("aa_out"), last(h, 1))
                dve.wait_ge(S("yb_out"), last(h))
                cp(hp[:], par[:, :, h]).then_inc(S("hp_out"), 1)
                dve.wait_ge(S("hp_out"), this(h))
                dve.wait_ge(S("a_out"), this(h))
                dve.wait_ge(S("ix_mm"), last(h, 1))
                dve.wait_ge(S("iu_out"), last(h, 1))
                parts = [(u[:, 0:T], lambda k: a_pad[:, k:k + T]), (u[:, T:], lambda k: a_edge[:, k:k + 6:5])]
                for n, k in enumerate((2, 0, 1, 3)):
                    for dst, window in parts:
                        if n == 0:
                            i = ts(dst, window(k), col(V_CW + k), col(V_CB), ALU.mult, ALU.add)
                        else:
                            i = stt(dst, window(k), col(V_CW + k), dst, ALU.mult, ALU.add)
                    if n < 3:
                        link(i)
                i.then_inc(S("conv_out"), 1)
                dve.wait_ge(S("sq_out"), this(h))
                dve.wait_ge(S("ay_out"), this(h))
                dve.wait_ge(S("prod_q"), last(h, 1))
                dve.wait_ge(S("qe3_out"), last(h, 1))
                tt(qs, PJ[1][:, 0:T], sq, ALU.mult).then_inc(S("qs_out"), 1)

                def forget(d):
                    dve.wait_ge(S(("ff_out", "fb_out")[d]), this(h))
                    dve.wait_ge(S("prod_q"), last(h, d))
                    dve.wait_ge(S("kdc_out"), last(h, d))
                    link(ts(gg[d], gg[d], col(V_OML), col(V_LBV), ALU.mult, ALU.add))
                    ts(kk[d], gg[d], -1.0, 1.0, ALU.mult, ALU.add).then_inc(S("g_out"), 1)

                def logs(d):
                    dve.wait_ge(S("ln_out"), this(h, d))
                    dve.wait_ge(S("exps_out"), last(h, d))
                    if d == 0:
                        link(dve.tensor_tensor_scan(lcx[d], resets[:], lf[d][:, 0:T], 0.0, ALU.mult, ALU.add))
                        dve.tensor_tensor_scan(rcx[d][:, T - 2::-1], ones[:, 0:T - 1], lf[d][:, 2 * T - 1:T:-1],
                                               0.0, ALU.mult, ALU.add)
                    else:
                        link(dve.tensor_tensor_scan(lcx[d][:, T - 1::-1], resets[:], lf[d][:, T - 1::-1], 0.0,
                                                    ALU.mult, ALU.add))
                        dve.tensor_tensor_scan(rcx[d][:, 1:T], ones[:, 0:T - 1], lf[d][:, T:2 * T - 1],
                                               0.0, ALU.mult, ALU.add)
                    lc = lcx[d].rearrange("p (c s) -> p c s", s=CH)
                    mid, tot = (MID, CH - 1) if d == 0 else (CH - 1 - MID, 0)
                    tt(dm[d].rearrange("p (c s) -> p c s", s=CH), lc,
                       lc[:, :, mid:mid + 1].to_broadcast([P, NCH, CH]), ALU.subtract)
                    tt(d4[d].rearrange("p (c s) -> p c s", s=CH),
                       lc[:, :, tot:tot + 1].to_broadcast([P, NCH, CH]), lc, ALU.subtract).then_inc(S("lc_out"), 1)

                def ratios(d):
                    dve.wait_ge(S("tz_out"), this(h, d))
                    link(ts(rc[d], tz[d], 1.0, None, ALU.add))
                    link(dve.reciprocal(rc[d], rc[d]))
                    tt(tz[d], tz[d], rc[d], ALU.mult).then_inc(S("w_out"), 1)

                def prods(d):
                    dve.wait_ge(S("e4_out"), this(h, d))
                    tt(e4[d], e4[d], kk[d][:, 0:T], ALU.mult).then_inc(S("prod_k"), 1)
                    dve.wait_ge(S("e1_out"), this(h, d))
                    dve.wait_ge(S("qs_out"), this(h))
                    tt(e2[d], e2[d], kk[d][:, 0:T], ALU.mult)
                    tt(e1[d], e1[d], qs, ALU.mult).then_inc(S("prod_q"), 1)

                def scans(d):
                    dve.wait_ge(S("b_out"), this(h, d))
                    dve.wait_ge(S("aa_out"), this(h, d))
                    dve.wait_ge(S("ya_out"), last(h))
                    seq = slice(0, T) if d == 0 else slice(T - 1, None, -1)
                    dve.tensor_tensor_scan(hs[d][:, seq], aa[d][:, seq], tz[d][:, seq], tz[d][:, T + d:T + d + 1],
                                           ALU.mult, ALU.add).then_inc(S("scan_out"), 1)

                def states(d):
                    dve.wait_ge(S("zero_set"), 1)
                    dve.wait_ge(S("att_mm"), this(h, d))
                    dve.wait_ge(S("inter_mm"), last(h, d))
                    dve.wait_ge(S("exps_out"), this(h, d))
                    dve.copy_predicated(att[d], causal[d][:].bitcast(u32).unsqueeze(1).to_broadcast([P, 2, P]),
                                        AB[:, 0:256].rearrange("p (a b) -> p a b", a=2))
                    cp(st[d][:, 0, :], AB[:, 256:384]).then_inc(S("att_out"), 1)
                    dve.wait_ge(S("att_out"), this(h, d))
                    step = Chain(f"state_step{d}", h * (NCH - 3))
                    for j in range(NCH - 1):
                        cj = j if d == 0 else NCH - 1 - j
                        if j == 0:
                            dve.wait_ge(S("kv_a"), this(h, d))
                        if j == 4:
                            dve.wait_ge(S("kv_b"), this(h, d))
                        kv = (KB if j < 4 else TB)[:, P * (cj % 4):P * (cj % 4) + P]
                        i = stt(st[d][:, j + 1, :], st[d][:, j, :], etot[:, d, cj:cj + 1], kv, ALU.mult, ALU.add)
                        if j == 3:
                            i.then_inc(S("chain_a"), 1)
                            dve.wait_ge(S("chain_a"), this(h, d))
                        elif j == NCH - 2:
                            i.then_inc(S("chain_b"), 1)
                        else:
                            step(i)
                    assert step.n == NCH - 3

                forget(0)
                logs(0)
                ratios(0)
                prods(0)
                forget(1)
                logs(1)
                ratios(1)
                prods(1)
                scans(0)
                scans(1)
                dve.wait_ge(S("scan_out"), this(h, 0))
                dve.wait_ge(S("scan_out"), this(h, 1))
                link(tt(hsum, hs[0][:, 0:T], hs[1][:, 0:T], ALU.add))
                tt(ya_g[:, h, :].rearrange("p (c r) -> p c r", r=ROWS), hsum.rearrange("p (r c) -> p c r", r=ROWS),
                   gl.rearrange("p (c r) -> p c r", r=ROWS), ALU.mult).then_inc(S("ya_out"), 1)
                states(0)
                dve.wait_ge(S("mod_mm"), this(h))
                tt(modB[:, bass.ds(h * 4, 4)], PJ[1][:, 0:4], par2[:, bass.ds(h * 4 + 16, 4)], ALU.add).then_inc(S("mod_out"), 1)
                states(1)
                dve.wait_ge(S("orms_out"), this(h))
                link(dve.reciprocal(orr, orr))
                dve.wait_ge(S("osq_out"), this(h))
                tt(on, OB[:, 0:T], orr, ALU.mult).then_inc(S("on_out"), 1)
                dve.wait_ge(S("on_out"), this(h))
                dve.wait_ge(S("og_out"), this(h))
                stt(yb_g[:, h, :], on, col(V_HG), sog, ALU.mult, ALU.mult).then_inc(S("yb_out"), 1)
                assert link.n == N_STEP, link.n

            def merge(i, b, first):
                m = 2 * i + b
                dve.wait_ge(S(f"proj_mm{b}"), i + 1)
                if not first:
                    dve.wait_ge(S(f"merged_out{b}"), i)
                tt(m1[b], PJ[b][:, 0:T], s_ga[:, m, :], ALU.mult)
                tt(m2[b], PJ[b][:, T:], s_gb[:, m, :], ALU.mult).then_inc(S(f"m2_out{b}"), 1)
                dve.wait_ge(S(f"m2_out{b}"), i + 1)
                tt(merged[:, m, :], m1[b], m2[b], ALU.add).then_inc(S(f"merged_out{b}"), 1)
            dve.wait_ge(S("ga_out"), this(HEADS - 1))
            dve.wait_ge(S("gb_out"), this(HEADS - 1))
            for b in range(2):
                merge(0, b, True)
            with dve.Fori(1, KT // 2) as i:
                for b in range(2):
                    merge(i, b, False)

            def diagonal(cols):
                i = tt(diag, ident[:].unsqueeze(1).to_broadcast([P, KT, P]),
                       cols.unsqueeze(2).to_broadcast([P, KT, P]), ALU.mult)
                i.then_inc(S("diag_out"), 1)
            dve.wait_ge(S("mod_out"), this(HEADS - 1))
            dve.wait_ge(S("proj_mm1"), KT // 2)
            for v, (row, c0) in enumerate(((gate1, 0), (gate2, 24))):
                if v:
                    dve.wait_ge(S("gate_mm"), 1)
                diagonal(modB[:, c0:c0 + KT])
                dve.wait_ge(S("gate_mm"), v + 1)
                for hf in range(2):
                    i = cp(row[:, 512 * hf:512 * hf + 512], bank[6 + hf][:])
                i.then_inc(S("gate_rows"), 1)
            link = serial
            link(ts(aff2[:], modB[:, 16:24], 1.0, None, ALU.add))
            tt(aff2[:], aff2[:], par[:, V_N2, :], ALU.mult).then_inc(S("aff2_out"), 1)
            dve.wait_ge(S("gate_rows"), 2)
            dve.wait_ge(S("xr_in"), 32)
            for t in range(2):
                dve.wait_ge(S("wo_mm"), t + 1)
                for hf in range(2):
                    s = slice(512 * hf, 512 * hf + 512)
                    b_ = bank[4 + hf] if t == 0 else bank[hf]
                    i = tt(x1[:, t, s], b_[:], gate1[:, s], ALU.mult)
                link(i)
                tt(x1[:, t, :], x1[:, t, :], xr[:, t, :], ALU.add).then_inc(S("x1_out"), 1)
            dve.wait_ge(S("ssq_out"), 6)
            ts(rstd[:, 0:2], ssq[:, 0:2], 1.0 / D, EPS, ALU.mult, ALU.add).then_inc(S("ms_out"), 1)
            dve.wait_ge(S("rms_out"), 2)
            link(dve.reciprocal(rstd[:, 0:2], rstd[:, 0:2]))
            dve.wait_ge(S("x1_out"), 2)
            for t in range(2):
                ts(xn[:, t, :], x1[:, t, :], rstd[:, t:t + 1], None, ALU.mult).then_inc(S("xn_out"), 1)

            dve.wait_ge(S("rt_mm"), 1)
            link(tt(lg, bank[6][:, 0:128].rearrange("p (t n) -> p t n", t=2)[:, :, 0:NG + NE],
                    b_rt[:].unsqueeze(1).to_broadcast([P, 2, NG + NE]), ALU.add))
            R = lambda j: rcol[:, j, :]
            bc = lambda a, n: a.unsqueeze(2).to_broadcast([P, 2, n])
            lgg = lg[:, :, 0:NG]
            link(dve.tensor_reduce(R(0), lgg, AX.X, ALU.max))
            tt(rt_g[:, :, 1, :], lgg, bc(R(0), NG), ALU.subtract).then_inc(S("rt_sub"), 1)
            link(tt(rt_g[:, :, 0, :], lgg, bc(R(0), NG), ALU.is_equal))

            def first_of(eq, dst, cum):
                for t in range(2):
                    i = dve.tensor_tensor_scan(cum[:, t, :], ones[:, 0:eq[:, t, :].shape[-1]], eq[:, t, :], 0.0,
                                               ALU.mult, ALU.add)
                link(i)
                link(stt(dst, cum, 1.0, eq, ALU.is_equal, ALU.mult))
            first_of(rt_g[:, :, 0, :], rt_g[:, :, 3, :], rt_g[:, :, 2, :])
            dve.wait_ge(S("rt_exp"), 1)
            link(dve.tensor_reduce(R(1), rt_g[:, :, 1, :], AX.X, ALU.add))
            link(dve.reciprocal(R(2), R(1)))
            link(ts(rt_g[:, :, 0, :], rt_g[:, :, 3, :], 1.0, BIG, ALU.subtract, ALU.mult))
            for t in range(2):
                i = tt(rt[:, 0, t, :].rearrange("p (g e) -> p g e", g=NG),
                       lg[:, t, NG:].rearrange("p (g e) -> p g e", g=NG),
                       rt_g[:, t, 0, :].unsqueeze(2).to_broadcast([P, NG, EPG]), ALU.add)
            link(i)
            link(dve.tensor_reduce(R(3), rt[:, 0], AX.X, ALU.max))
            link(tt(rt[:, 1], rt[:, 0], bc(R(3), NE), ALU.is_equal))
            first_of(rt[:, 1], rt[:, 3], rt[:, 2])
            link(stt(rt[:, 4], rt[:, 3], -3 * BIG, rt[:, 0], ALU.mult, ALU.add))
            link(dve.tensor_reduce(R(4), rt[:, 4], AX.X, ALU.max))
            link(tt(rt[:, 5], rt[:, 4], bc(R(4), NE), ALU.is_equal))
            tt(R(6), R(4), R(3), ALU.subtract).then_inc(S("rt_sub"), 1)
            first_of(rt[:, 5], rt[:, 7], rt[:, 6])
            dve.wait_ge(S("rt_exp"), 2)
            link(ts(R(7), R(6), 1.0, None, ALU.add))
            link(dve.reciprocal(R(7), R(7)))
            link(tt(R(8), R(7), R(2), ALU.mult))
            link(tt(R(9), R(8), R(6), ALU.mult))
            tt(rt[:, 8], rt[:, 3], rt[:, 7], ALU.add).then_inc(S("sel_out"), 1)
            link(tt(rt[:, 9], rt[:, 3], bc(R(8), NE), ALU.mult))
            link(tt(rt[:, 10], rt[:, 7], bc(R(9), NE), ALU.mult))
            tt(cw[:], rt[:, 9], rt[:, 10], ALU.add)
            link(dve.memset(rank, -1.0))
            dve.wait_ge(S("sel_out"), 1)
            dve.wait_ge(S("rank_mm"), 1)
            link(stt(rt[:, 11], bank[7][:, 0:2 * NE].rearrange("p (t n) -> p t n", t=2), 1.0, rt[:, 8],
                     ALU.add, ALU.mult))
            link(ts(rank[:, :, 0:NE], rt[:, 11], 1.0, None, ALU.subtract))
            link(dve.tensor_reduce(rcnt[:, 0:1], bank[7][:, 2 * NE:3 * NE], AX.X, ALU.max))
            link(ts(rcnt[:, 1:2], rcnt[:, 0:1], float(SLOTS), 1.0, ALU.is_gt, ALU.add))
            link(stt(rcnt[:, 2:3], rcnt[:, 0:1], float(2 * SLOTS), rcnt[:, 1:2], ALU.is_gt, ALU.add))
            link(stt(rcnt[:, 3:4], rcnt[:, 0:1], float(3 * SLOTS), rcnt[:, 2:3], ALU.is_gt, ALU.add))
            dve.memset(ct[1], 0.0)
            dve.memset(ys[1], 0.0)
            cp(rcnt_i[:], rcnt[:, 3:4].to_broadcast([P, 4])).then_inc(S("rounds_ready"), 1)
            dve.wait_ge(S("rounds_ready"), 1)
            n_rounds = dve.value_load(rcnt_i[0:1, 0:1], min_val=1, max_val=T // SLOTS)
            with dve.Fori(0, n_rounds) as r:
                def one_hots(first, g):
                    dve.wait_ge(S("mx"), last(g, 1))
                    for e in range(2):
                        i = tt(hot[:, :, e, :], slot_no[:].unsqueeze(1).to_broadcast([P, 2, SLOTS]),
                               rank[:, :, bass.ds(first + e, 1)].to_broadcast([P, 2, SLOTS]), ALU.is_equal)
                    i.then_inc(S("hotc"), 1)

                def weighted(b, p, q):
                    dve.wait_ge(S("mt"), last(q, b))
                    for cpy in range(2):
                        i = tt(hotw[b][:, :, cpy, :], hot[:, :, b, :],
                               cw[:, :, bass.ds(p * 2 + b, 1)].to_broadcast([P, 2, SLOTS]), ALU.mult)
                    i.then_inc(S("hw"), 1)

                dve.wait_ge(S("hw"), last(r * PAIRS, 1))
                one_hots(0, r * (PAIRS + 1))
                with dve.Fori(0, PAIRS) as p:
                    q = r * PAIRS + p
                    g = r * (PAIRS + 1) + p
                    dve.wait_ge(S("hotc"), g + 2)
                    weighted(0, p, q)
                    weighted(1, p, q)

                    def hidden(b):
                        dve.wait_ge(S("sh"), this(q, b))
                        dve.wait_ge(S("mt"), last(q, b))
                        tt(gm[b], sh[b], HB[:, 256:512], ALU.mult).then_inc(S("gm"), 1)

                    def y_out(b):
                        dve.wait_ge(S("my"), this(q, b))
                        dve.wait_ge(S(f"mc{b}"), q + 1 if b == 0 else g + 2)
                        cp(ys[b], YB[:]).then_inc(S("ysc"), 1)

                    hidden(0)
                    dve.wait_ge(S("hw"), this(q, 1))
                    one_hots(p * 2 + 2, g + 1)
                    y_out(0)
                    hidden(1)
                    y_out(1)
                dve.wait_ge(S("mc1"), (r + 1) * (PAIRS + 1) + 1)
                dve.memset(ct[1], 0.0)
                step = Chain("res_step", r * 4)
                for t in range(2):
                    for hf in range(2):
                        s = slice(512 * hf, 512 * hf + 512)
                        i = tt(res[:, s], ACC[t][hf][:], gate2[:, s], ALU.mult)
                    step(i)
                    step(tt(x1[:, t, :], x1[:, t, :], res, ALU.add))
                ts(rank, rank, float(SLOTS), None, ALU.subtract).then_inc(S("acc_read"), 1)
                dve.wait_ge(S("acc_read"), r + 2)

            link = serial
            for t in range(2):
                link(dve.tensor_tensor(xn[:, t, :], x1[:, t, :], x1[:, t, :], ALU.mult))
                link(dve.tensor_reduce(ssq[:, t:t + 1], xn[:, t, :], AX.X, ALU.add))
            ts(rstd[:, 0:2], ssq[:, 0:2], 1.0 / D, EPS, ALU.mult, ALU.add).then_inc(S("ms_out"), 1)
            dve.wait_ge(S("rms_out"), 3)
            link(dve.reciprocal(rstd[:, 0:2], rstd[:, 0:2]))
            dve.wait_ge(S("fg_in"), 16)
            for t in range(2):
                stt(xn[:, t, :], x1[:, t, :], rstd[:, t:t + 1], fin_g, ALU.mult, ALU.mult).then_inc(S("y_out"), 1)


_INS = ['x', 'c', 'ctx', 'c_ctx', 'w_mod', 'b_mod', 'norm1_g', 'w_in', 'conv_w', 'conv_b', 'lru_wa', 'lru_ba',
        'lru_wx', 'lru_bx', 'lru_lam', 'hg_lb', 'hg_norm_g', 'w_proj_a', 'w_proj_b', 'w_out', 'norm2_g', 'w_rg',
        'b_rg', 'w_re', 'b_re', 'w1', 'w3', 'w2', 'final_g']


def kernel(**inputs):
    import numpy as np
    import concourse.bacc as bacc
    from concourse.bass_utils import run_bass_kernel_spmd

    nc = bacc.Bacc("TRN2", target_bir_lowering=False, num_devices=1)
    arrays, args = {}, []
    for name in _INS:
        a = np.ascontiguousarray(inputs[name])
        arrays[f"in_{name}"] = a
        args.append(nc.dram_tensor(f"in_{name}", a.shape, mybir.dt.from_np(a.dtype), kind="ExternalInput").ap())
    out = nc.dram_tensor("out_0", (1, T, D), mybir.dt.float32, kind="ExternalOutput").ap()
    build(nc, *args, out)
    r = run_bass_kernel_spmd(nc, [arrays], core_ids=[0])
    return r.results[0]["out_0"]
```

```python
import concourse.bass as bass
from concourse import mybir
from contextlib import ExitStack

D = 1024
P = 128
KT = D // P
T = 256
GW = 64
ROWS = T // GW
HEADS = 8
CH = 32
NCH = T // CH
MID = CH // 2
EPS = 1e-6
NE = 32
NG = 4
EPG = NE // NG
F = 512
SLOTS = 64
PAIRS = NE // 2
BIG = 1e30

BLK = {"a": 0, "ay": 1, "q": 2, "ff": 3, "fb": 4, "v": 5, "og": 6, "ga": 7, "gb": 8}
ORDER = ["a", "q", "ay", "ff", "fb", "v", "og", "ga", "gb"]
SHARED = {"ay": "q", "ga": "og"}

V_CW, V_CB, V_BA, V_BX, V_LAM, V_LB, V_HG, V_N1, V_N2 = 0, 4, 5, 7, 9, 11, 13, 14, 15
V_NSP, V_PSP, V_LBV, V_OML = 16, 18, 20, 21
NV = 22

SLOT = 4096
A_WBLK = 0
A_WLRU = 9 * 1024
A_WMOD = A_WLRU + 512
A_PRO = 7680
A_R = A_WMOD + 4096
A_HT = 6 * SLOT
A_CS = A_HT - 256
EDGE = 6
TU = T + 2
A_YA = A_HT + KT * (EDGE + 2 * T)
A_YB = A_YA + 2048
A_GA = A_YB + 2048
A_GB = A_GA + 2048
A_MG = A_GB + 2048
A_T = A_MG + 2048
ARENA = A_T + 11784


def build(nc, x, c, ctx_in, c_ctx, w_mod, b_mod, norm1_g, w_in, conv_w, conv_b, lru_wa, lru_ba, lru_wx, lru_bx,
          lru_lam, hg_lb, hg_norm_g, w_proj_a, w_proj_b, w_out, norm2_g, w_rg, b_rg, w_re, b_re,
          w1, w3, w2, final_g, out):
    f32 = mybir.dt.float32
    bf16 = mybir.dt.bfloat16
    u32 = mybir.dt.uint32
    i32 = mybir.dt.int32
    ACT = mybir.ActivationFunctionType
    ALU = mybir.AluOpType
    AX = mybir.AxisListType

    with ExitStack() as es:
        arena = es.enter_context(nc.sbuf_tensor("arena", [P, ARENA], f32))

        def at(start, *shape):
            n = 1
            for s in shape:
                n *= s
            v = arena[:, start:start + n]
            if len(shape) == 2:
                v = v.rearrange("p (a b) -> p a b", a=shape[0])
            if len(shape) == 3:
                v = v.rearrange("p (a b c) -> p a b c", a=shape[0], b=shape[1])
            return v

        def sb(name, *shape, dt=f32):
            return es.enter_context(nc.sbuf_tensor(name, [P, *shape], dt))

        sems = {}

        def S(name):
            if name not in sems:
                sems[name] = es.enter_context(nc.semaphore(name))
            return sems[name]

        ident = sb("ident", P)
        mean_w = sb("mean_w", P)
        ones = sb("ones", T)
        resets = sb("resets", T)
        causal = [sb("causal_f", P), sb("causal_b", P)]
        before = sb("before", P)
        slot_no = sb("slot_no", SLOTS)
        zb = sb("zb", 4 * P, dt=bf16)
        prows = at(A_T + 5120, 2, P)
        par = sb("par", NV, HEADS)
        par2 = sb("par2", 64)
        quad = sb("quad", 2)
        modA = sb("modA", 16, 2)
        modB = sb("modB", 32)
        aff1 = sb("aff1", 2, KT)
        aff2 = sb("aff2", KT)
        ssq = sb("ssq", 4)
        rstd = sb("rstd", 4)
        hp = sb("hp", NV)
        etot = sb("etot", 2, NCH)
        w_rt = sb("w_rt", KT, NG + NE)
        b_rt = sb("b_rt", NG + NE)
        spt = sb("spt", 5, 16)
        rcnt = sb("rcnt", 4)
        rcnt_i = sb("rcnt_i", 4, dt=i32)
        eps_t = sb("eps_t", 1)
        cw = sb("cw", 2, NE)

        bank = [es.enter_context(nc.psum_tensor(f"bank{i}", [P, 512], f32)) for i in range(8)]
        PJ = [bank[0], bank[1]]
        GT = [bank[2], bank[3]]
        TB, KB, AB, OB = bank[4:8]

        h_ct = at(A_HT, KT, EDGE + 2 * T)
        wblk = {n: at(A_WBLK + 1024 * i, KT, P) for i, n in enumerate(ORDER)}
        wlru = at(A_WLRU, 4, P)
        wmod = at(A_WMOD, KT, 512)
        wpro = [at(A_PRO + 4096 * i, KT, 512) for i in range(4)]
        csil = at(A_CS, KT, 2, 16)
        ya_g, yb_g, s_ga, s_gb = (at(a, HEADS, T) for a in (A_YA, A_YB, A_GA, A_GB))
        merged = at(A_MG, KT, T)
        tok = at(A_T, 4, D)
        junk = at(A_YA, 4, D)
        o = A_T
        a_pad = at(o, T + 3)
        a_edge = at(o + T + 4, EDGE + 4)
        o += 520
        u = at(o, TU)
        o += 512
        rg, ig, tz, aa, rc, hs = ([at(o + 512 * (2 * j + d), TU) for d in range(2)] for j in range(6))
        o += 12 * 512
        gl = at(o, T)
        hsum = at(o + 256, T)
        qs = at(o + 512, T)
        sq = at(o + 768, T)
        o += 1024
        kdT = [at(o + 512 * d, 4, P) for d in range(2)]
        o += 1024
        att = [at(o + 256 * d, 2, P) for d in range(2)]
        o += 512
        st = [at(o + 1024 * d, NCH, P) for d in range(2)]
        o += 2048
        assert o <= ARENA
        o = A_R
        gg, kk, lf = ([at(o + 512 * (2 * j + d), 2 * T) for d in range(2)] for j in range(3))
        o += 6 * 512
        lcx, rcx, dm, d4, e1, e2, e3, e4, ec = ([at(o + 256 * (2 * j + d), T) for d in range(2)] for j in range(9))
        o += 18 * 256
        vv = at(o, 4, P)
        o += 512
        vbd = at(o, 2, 4, P)
        o += 1024
        osq, orr, on, sog = (at(o + 256 * j, T) for j in range(4))
        o += 1024
        assert o <= A_CS
        wp = [[at(2048 * b + 1024 * j, KT, P) for j in range(2)] for b in range(2)]
        wo = at(A_T, KT, D)
        xr = at(A_HT, 2, D)
        x1 = at(A_HT + 2048, 2, D)
        gate1, gate2, fin_g = (at(A_T + 8192 + 1024 * j, D) for j in range(3))
        diag = at(A_HT + 3072, KT, P)
        w_sh = at(A_HT + 3072, KT, NG + NE)
        m1 = [at(A_HT + 2048 + 512 * b, T) for b in range(2)]
        m2 = [at(A_HT + 2048 + 512 * b + 256, T) for b in range(2)]
        junk2 = at(A_YA + 2048, 2, D)
        res = at(A_T, D)
        xn = at(A_MG, 2, D)
        x1T = at(A_YA, KT, T)
        xg = at(A_YA + 4096, KT, 2 * SLOTS)
        o = A_T + 2048
        hot = at(o, 2, 2, SLOTS)
        o += 256
        hotw = at(o, 2, 2, SLOTS)
        o += 256
        ct = at(o, 2, P)
        o += 256
        sh = at(o, F)
        o += 512
        gm = at(o, F)
        o += 512
        gT = at(o, 4, P)
        o += 512
        ys = at(o, 2, F)
        o += 1024
        lg = at(o, 2, NG + NE)
        o += 72
        rt_g = at(o, 2, 4, NG)
        o += 32
        rt = at(o, 12, 2, NE)
        o += 12 * 64
        rcol = at(o, 16, 2)
        o += 32
        rank = at(o, 2, NE + 2)
        o += 2 * (NE + 2)
        assert o <= A_T + 8192
        ring = [at(SLOT * s, SLOT) for s in range(6)]
        SL = {("w1", 0): 1, ("w1", 1): 2, ("w3", 0): 3, ("w3", 1): 4, ("w2", 0): 5, ("w2", 1): 0}

        def wslot(kind, b):
            s = ring[SL[kind, b]]
            return s.rearrange("p (k n) -> p k n", n=D if kind == "w2" else F)

        ACC = [[bank[0], bank[1]], [bank[2], bank[3]]]
        UX, VY, CY, GX = bank[4:8]

        cm = "(r c) d -> c r d"
        x_cm = x[0].rearrange(cm, r=ROWS)
        out_cm = out[0].rearrange(cm, r=ROWS)
        wi_v = w_in[0].rearrange("(k p) n -> p k n", p=P)
        wm_v = w_mod[0].rearrange("(k p) n -> p k n", p=P)
        lru_v = [[w[0, d].rearrange("h i j -> i h j") for w in (lru_wa, lru_wx)] for d in range(2)]
        wpa_v, wpb_v, wo_v = (w[0].rearrange("(k p) n -> p k n", p=P) for w in (w_proj_a, w_proj_b, w_out))
        w1_v, w3_v, w2_v = (w[0].rearrange("e (k p) n -> e p k n", p=P) for w in (w1, w3, w2))
        rows = [(conv_w[0], 4), (conv_b, 1), (lru_ba[0], 2), (lru_bx[0], 2), (lru_lam[0], 2), (hg_lb, 2),
                (hg_norm_g, 1), (norm1_g, 1), (norm2_g, 1)]

        def this(h, d=None):
            return h + 2 if d is None else 2 * h + d + 3

        def last(h, d=None):
            return h + 1 if d is None else 2 * h + d + 1

        HEAD_SEMS = ("a_mm q_mm ff_mm fb_mm v_mm og_mm gb_mm mod_mm modr_mm rms_mm a_out sq_out ay_out ff_out fb_out "
                     "v_out og_out ga_out gb_out osq_out orms_out hp_out conv_out qs_out ya_out mod_out modr_out on_out "
                     "yb_out").split()
        DIR_SEMS = ("kdt_mm att_mm kv_a kv_b inter_mm rg_out "
                     " ig_out tz_out ln_out aa_out exps_out ec_out e4_out e1_out kdT_out sqrt_out g_out lc_out w_out prod_k prod_q att_out chain_a chain_b scan_out iu_out b_out kdc_out qe3_out ra_mm ix_mm").split()
        MOE_SEMS = "m1 m3 mtc mtg mc acc_read hotc sh gm ctc gtc hw".split()
        EXP_SEMS = "my mx ysc xgc".split()

        block = es.enter_context(nc.Block())

        @block.sync
        def _(sp):
            r0 = 0
            for v, n in rows:
                sp.dma_start(prows[r0:r0 + 8 * n, 0, :], v.rearrange("a (h n) -> (a h) n", n=P)).then_inc(S("par_in"), 16)
                r0 += 8 * n
            sp.dma_start(prows[0:48, 1, :], b_mod[0].rearrange("(h n) -> h n", n=P)).then_inc(S("par_in"), 16)
            sp.dma_start(prows[48:56, 1, :], c[0].rearrange("(h n) -> h n", n=P)).then_inc(S("par_in"), 16)
            sp.dma_start(prows[56:64, 1, :], c_ctx.rearrange("(h n) -> h n", n=P)).then_inc(S("par_in"), 16)
            for t in range(2):
                sp.dma_start(tok[:, t, :], x_cm[32 * t:32 * t + 32]).then_inc(S("x_in"), 16)
            for t in range(2):
                sp.dma_start(tok[:, 2 + t, :], ctx_in[0, P * t:P * t + P, :]).then_inc(S("ctx_in"), 16)
            for i in range(4):
                sp.dma_start(wpro[i], wm_v[:, :, 512 * i:512 * i + 512]).then_inc(S(f"pro_in{i}"), 16)

            def head_loads(h, first):
                for n, used in zip(ORDER, ("a", "q", "q", "ff", "fb", "v", "og", "og", "gb")):
                    if not first:
                        sp.wait_ge(S(used + "_mm"), last(h))
                    elif n == "ga":
                        sp.wait_ge(S("pro_mm"), 1)
                    sp.dma_start(wblk[n], wi_v[:, :, bass.ds(BLK[n] * D + h * P, P)]).then_inc(S("in_" + SHARED.get(n, n)), 16)
                    if n == "fb":
                        if first:
                            sp.wait_ge(S("pro_mm"), 1)
                        else:
                            sp.wait_ge(S("ix_mm"), last(h, 1))
                        for d in range(2):
                            for j in range(2):
                                sp.dma_start(wlru[:, 2 * d + j, :], lru_v[d][j][:, h, :]).then_inc(S("in_lru"), 16)
                if not first:
                    sp.wait_ge(S("mod_mm"), last(h))
                sp.dma_start(wmod, wm_v[:, :, bass.ds(2 * D + h * 512, 512)]).then_inc(S("in_wmod"), 16)

            head_loads(0, True)
            sp.dma_start(w_rt[:, :, 0:NG], w_rg[0].rearrange("(k p) n -> p k n", p=P)).then_inc(S("rt_in"), 16)
            sp.dma_start(w_rt[:, :, NG:], w_re[0].rearrange("(k p) n -> p k n", p=P)).then_inc(S("rt_in"), 16)
            sp.dma_start(b_rt[:, 0:NG], b_rg.to_broadcast([P, NG])).then_inc(S("rt_in"), 16)
            sp.dma_start(b_rt[:, NG:], b_re.to_broadcast([P, NE])).then_inc(S("rt_in"), 16)
            with sp.Fori(1, HEADS) as h:
                head_loads(h, False)

            def proj_loads(m, b, first):
                if first:
                    sp.wait_ge(S("ff_mm"), this(HEADS - 1))
                else:
                    sp.wait_ge(S(f"proj_mm{b}"), (m - b) // 2 if isinstance(m, int) else m)
                mm = m if isinstance(m, int) else 2 * m + b
                sp.dma_start(wp[b][0], wpa_v[:, :, bass.ds(mm * P, P)]).then_inc(S(f"wp_in{b}"), 16)
                sp.dma_start(wp[b][1], wpb_v[:, :, bass.ds(mm * P, P)]).then_inc(S(f"wp_in{b}"), 16)

            for b in range(2):
                proj_loads(b, b, True)
            sp.wait_ge(S("yb_out"), this(HEADS - 1))
            sp.wait_ge(S("ya_out"), this(HEADS - 1))
            for i in range(2):
                sp.dma_start(wo[:, 4 * i:4 * i + 4, :], wo_v[:, 4 * i:4 * i + 4, :]).then_inc(S("wo_in"), 16)
            with sp.Fori(1, KT // 2) as m:
                for b in range(2):
                    proj_loads(m, b, False)
            sp.wait_ge(S("gb_mm"), this(HEADS - 1))
            for t in range(2):
                sp.dma_start(xr[:, t, :], x_cm[32 * t:32 * t + 32]).then_inc(S("xr_in"), 16)
            sp.dma_start(fin_g, final_g[None, :].to_broadcast([P, D])).then_inc(S("fg_in"), 16)

            src = {"w1": w1_v, "w3": w3_v, "w2": w2_v}
            kinds = [(k, b) for k in ("w1", "w3", "w2") for b in range(2)]
            for k, b in kinds:
                if (k, b) == ("w2", 1):
                    sp.wait_ge(S("proj_mm1"), KT // 2)
                sp.dma_start(wslot(k, b), src[k][b]).then_inc(S("in_" + k), 16)
            sp.wait_ge(S("rounds_ready"), 1)
            n_rounds = sp.value_load(rcnt_i[0:1, 0:1], min_val=1, max_val=T // SLOTS)
            with sp.Fori(1, n_rounds * PAIRS) as q:
                e = [sp.snap((q & (PAIRS - 1)) * 2 + b) for b in range(2)]
                for k, b in kinds:
                    if b == 0:
                        if k == "w2":
                            sp.wait_ge(S("my"), last(q, 1))
                        else:
                            sp.wait_ge(S("m1" if k == "w1" else "m3"), last(q))
                    if (k, b) == kinds[0]:
                        sp.sem_inc(S("slot_free"), 1)
                    sp.dma_start(wslot(k, b), src[k][e[b]]).then_inc(S("in_" + k), 16)
            for t in range(2):
                sp.wait_ge(S("y_out"), t + 1)
                sp.dma_start(out_cm[32 * t:32 * t + 32], xn[:, t, :]).then_inc(S("stored"), 16)
            sp.wait_ge(S("stored"), 32)

        @block.gpsimd
        def _(pool):
            for const in (ident, resets, causal[0], causal[1], before, ones):
                i = pool.memset(const[:], 1.0)
            i.then_inc(S("consts"), 1)
            pool.wait_ge(S("consts"), 1)

            def keep(v, base, pattern, per_partition, op=ALU.is_ge):
                return pool.affine_select(out=v, in_=v, compare_op=op, fill=0.0, base=base, pattern=pattern,
                                          channel_multiplier=per_partition)
            keep(ident[:], 0, [[1, P]], -1, ALU.is_equal).then_inc(S("ident_set"), 1)
            pool.memset(mean_w[:], 1.0 / P)
            pool.memset(resets[:, 0:T:CH], 0.0)
            keep(before[:], -1, [[1, P]], -1)
            blocks = [m[:].rearrange("p (a b) -> p a b", b=CH) for m in causal]
            keep(blocks[0], 0, [[CH, P // CH], [1, CH]], -1)
            keep(blocks[1], 0, [[-CH, P // CH], [-1, CH]], 1).then_inc(S("consts"), 1)
            pool.wait_ge(S("consts"), 2)
            keep(blocks[0], 0, [[-CH, P // CH], [0, CH]], 1)
            keep(blocks[1], CH - 1, [[CH, P // CH], [0, CH]], -1)
            pool.iota(slot_no[:], pattern=[[1, SLOTS]], base=0, channel_multiplier=0,
                      allow_small_or_imprecise_dtypes=True)
            pool.memset(zb[:], 0.0).then_inc(S("const_set"), 1)
            for n in HEAD_SEMS + MOE_SEMS:
                pool.sem_inc(S(n), 1)
            for n in DIR_SEMS + EXP_SEMS:
                pool.sem_inc(S(n), 2)
            pool.wait_ge(S("pro_mm"), 1)
            pool.wait_ge(S("tok_T"), 8)
            for d in range(2):
                pool.memset(att[d], 0.0)
            pool.memset(vbd, 0.0)
            pool.memset(a_pad, 0.0)
            pool.memset(a_edge, 0.0)
            for d in range(2):
                pool.memset(rcx[d], 0.0)
            last_set = pool.memset(etot[:], 0.0)
            last_set.then_inc(S("zero_set"), 1)
            pool.wait_ge(S("zero_set"), 1)
            with pool.Fori(0, HEADS) as h:
                def gates(d):
                    pool.wait_ge(S("ig_out"), this(h, d))
                    pool.wait_ge(S("conv_out"), this(h))
                    pool.tensor_tensor(ig[d], ig[d], u, ALU.mult).then_inc(S("iu_out"), 1)

                def prods(d):
                    pool.wait_ge(S("ec_out"), this(h, d))
                    pool.tensor_tensor(ec[d], ec[d], kk[d][:, T:], ALU.mult).then_inc(S("kdc_out"), 1)
                    pool.wait_ge(S("exps_out"), this(h, d))
                    pool.wait_ge(S("qs_out"), this(h))
                    pool.tensor_tensor(e3[d], e3[d], qs, ALU.mult).then_inc(S("qe3_out"), 1)

                def inputs(d):
                    pool.wait_ge(S("sqrt_out"), this(h, d))
                    pool.wait_ge(S("iu_out"), this(h, d))
                    pool.tensor_tensor(tz[d], tz[d], ig[d], ALU.mult).then_inc(S("b_out"), 1)

                gates(0)
                prods(0)
                gates(1)
                prods(1)
                inputs(0)
                inputs(1)

        @block.tensor
        def _(pe):
            mm = pe.matmul

            def down_k(dst, w, rhs, start=True):
                for k in range(KT):
                    i = mm(dst, w(k), rhs(k), start=start and k == 0, stop=k == KT - 1)
                return i

            pe.wait_ge(S("ident_set"), 1)
            pe.wait_ge(S("par_in"), 16 * (len(rows) + 3))
            pe.transpose(bank[7][:, 0:P], prows[:, 0, :], ident[:])
            pe.transpose(bank[7][:, P:P + 64], prows[0:64, 1, :], ident[0:64, 0:64]).then_inc(S("par_T"), 1)
            for k in range(KT):
                if k == 0:
                    pe.wait_ge(S("xs_out"), 4)
                if k >= 2:
                    pe.wait_ge(S("tok_copy"), k - 1)
                for t in range(4):
                    i = pe.transpose(PJ[k % 2][:, P * t:P * t + P], tok[:, t, P * k:P * k + P], ident[:])
                i.then_inc(S("tok_T"), 1)
            def mod_rows(dst, w):
                for k in range(KT):
                    r = 32 * (k % 4)
                    i = mm(dst[r:r + 32, :], csil[:, k].rearrange("p s r -> p (s r)"), w[:, k, :],
                           start=k < 4, stop=k >= 4)
                return i

            def mod_sums(dst, n, rows_):
                for m in range(4):
                    i = mm(dst[:, n * m:n * m + n], rows_[:, P * m:P * m + P], quad[:, 0:n], start=True, stop=True)
                return i

            pe.wait_ge(S("csil_out"), 1)
            pe.wait_ge(S("quad_set"), 1)
            for i in range(5):
                if i < 4:
                    pe.wait_ge(S(f"pro_in{i}"), 16)
                    mod_rows(bank[2 + i], wpro[i]).then_inc(S("pro_rows"), 1)
                if i > 0:
                    pe.wait_ge(S("pro_part"), i)
                    ins = mod_sums(bank[6][:, 8 * i - 8:8 * i], 2, wpro[i - 1][:, 0, :])
            ins.then_inc(S("pro_mm"), 1)
            pe.wait_ge(S("h_ct_out"), 1)
            pe.wait_ge(S("edges_out"), 1)
            pe.wait_ge(S("const_set"), 1)
            pe.wait_ge(S("zero_set"), 1)

            with pe.Fori(0, HEADS) as h:
                h_edge_x = lambda k: h_ct[:, k, 0:EDGE + T]
                h_x = lambda k: h_ct[:, k, EDGE:EDGE + T]
                h_all = lambda k: h_ct[:, k, EDGE:]
                W = lambda n: (lambda k: wblk[n][:, k, :])

                def loaded(n, times=1):
                    pe.wait_ge(S("in_" + n), (h + 1) * (16 * times))

                def gate_products(d):
                    if d == 0:
                        loaded("lru", 4)
                        pe.wait_ge(S("conv_out"), this(h))
                        pe.wait_ge(S("rg_out"), last(h, 1))
                        pe.wait_ge(S("ig_out"), last(h, 1))
                    else:
                        pe.wait_ge(S("rg_out"), this(h, 0))
                        pe.wait_ge(S("ig_out"), this(h, 0))
                    mm(GT[0][:, 0:TU], wlru[:, 2 * d, :], u, start=True, stop=True).then_inc(S("ra_mm"), 1)
                    mm(GT[1][:, 0:TU], wlru[:, 2 * d + 1, :], u, start=True, stop=True).then_inc(S("ix_mm"), 1)

                def decayed_keys_T(d):
                    pe.wait_ge(S("prod_k"), this(h, d))
                    pe.wait_ge(S("kdc_out"), this(h, d))
                    if d == 0:
                        pe.wait_ge(S("chain_b"), last(h, 1))
                    else:
                        pe.wait_ge(S("kdT_out"), this(h, 0))
                    for t in range(2):
                        pe.transpose(TB[:, P * t:P * t + P], e4[d][:, P * t:P * t + P], ident[:])
                    for t in range(2):
                        i = pe.transpose(TB[:, P * (2 + t):P * (3 + t)], ec[d][:, P * t:P * t + P], ident[:])
                    i.then_inc(S("kdt_mm"), 1)

                def attention(d):
                    pe.wait_ge(S("prod_q"), this(h, d))
                    if d == 0:
                        pe.wait_ge(S("orms_out"), last(h))
                    else:
                        pe.wait_ge(S("att_out"), this(h, 0))
                    for t in range(2):
                        s = slice(P * t, P * t + P)
                        mm(AB[:, s], e2[d][:, s], e1[d][:, s], start=True, stop=True)
                    pe.wait_ge(S("kdT_out"), this(h, d))
                    pe.wait_ge(S("v_out"), this(h))
                    for t in range(2):
                        i = mm(AB[:, 256:384], kdT[d][:, 2 + t, :], vv[:, 2 + t, :], start=t == 0, stop=t == 1)
                    i.then_inc(S("att_mm"), 1)

                def chunk_states(d):
                    ta, tb = (0, 1) if d == 0 else (1, 0)
                    if d == 0:
                        pe.wait_ge(S("chain_a"), last(h, 1))
                    else:
                        pe.wait_ge(S("chain_a"), this(h, 0))
                    mm(KB[:], kdT[d][:, ta, :], vbd[:, ta].rearrange("p a b -> p (a b)"),
                       start=True, stop=True).then_inc(S("kv_a"), 1)
                    if d == 0:
                        pe.wait_ge(S("kdT_out"), this(h, 1))
                    else:
                        pe.wait_ge(S("chain_b"), this(h, 0))
                    s = slice(0, 384) if d == 0 else slice(128, 512)
                    mm(TB[:, s], kdT[d][:, tb, :], vbd[:, tb].rearrange("p a b -> p (a b)")[:, s],
                       start=True, stop=True).then_inc(S("kv_b"), 1)

                def outputs(d):
                    if d == 0:
                        pe.wait_ge(S("on_out"), last(h))
                    pe.wait_ge(S("att_out"), this(h, d))
                    for t in range(2):
                        s = slice(P * t, P * t + P)
                        mm(OB[:, s], vv[:, t, :], att[d][:, t, :], start=d == 0 and t == 0, stop=False,
                           skip_group_check=True)
                    pe.wait_ge(S("qe3_out"), this(h, d))
                    pe.wait_ge(S("chain_a"), this(h, d))
                    pe.wait_ge(S("chain_b"), this(h, d))
                    for j in range(NCH):
                        cj = j if d == 0 else NCH - 1 - j
                        s = slice(CH * cj, CH * cj + CH)
                        i = mm(OB[:, s], st[d][:, j, :], e3[d][:, s], start=False, stop=d == 1,
                               skip_group_check=True)
                    i.then_inc(S("inter_mm"), 1)

                loaded("a")
                pe.wait_ge(S("gb_out"), last(h))
                down_k(PJ[0][:, 0:EDGE + T], W("a"), h_edge_x).then_inc(S("a_mm"), 1)
                loaded("q", 2)
                pe.wait_ge(S("mod_out"), last(h))
                down_k(PJ[1][:, 0:T], W("q"), h_x)
                down_k(PJ[1][:, T:], W("ay"), h_x).then_inc(S("q_mm"), 1)
                loaded("ff")
                pe.wait_ge(S("a_out"), this(h))
                down_k(PJ[0][:], W("ff"), h_all).then_inc(S("ff_mm"), 1)
                gate_products(0)
                loaded("fb")
                pe.wait_ge(S("ay_out"), this(h))
                pe.wait_ge(S("qs_out"), this(h))
                down_k(PJ[1][:], W("fb"), h_all).then_inc(S("fb_mm"), 1)
                gate_products(1)
                loaded("v")
                pe.wait_ge(S("ff_out"), this(h))
                for t in range(4):
                    i = down_k(PJ[0][:, P * t:P * t + P], lambda k: h_ct[:, k, EDGE + P * t:EDGE + P * t + P], W("v"))
                i.then_inc(S("v_mm"), 1)
                decayed_keys_T(0)
                loaded("og", 2)
                pe.wait_ge(S("fb_out"), this(h))
                down_k(PJ[1][:, 0:T], W("og"), h_x)
                decayed_keys_T(1)
                down_k(PJ[1][:, T:], W("ga"), h_x).then_inc(S("og_mm"), 1)
                attention(0)
                chunk_states(0)
                loaded("gb")
                down_k(PJ[0][:, 0:T], W("gb"), h_x).then_inc(S("gb_mm"), 1)
                attention(1)
                chunk_states(1)
                loaded("wmod")
                pe.wait_ge(S("ga_out"), this(h))
                mod_rows(PJ[1], wmod).then_inc(S("modr_mm"), 1)
                outputs(0)
                outputs(1)
                pe.wait_ge(S("modr_out"), this(h))
                mod_sums(PJ[1], 1, wmod[:, 0, :]).then_inc(S("mod_mm"), 1)
                pe.wait_ge(S("osq_out"), this(h))
                pe.wait_ge(S("att_out"), this(h, 1))
                mm(AB[:, 0:T], mean_w[:], osq, start=True, stop=True).then_inc(S("rms_mm"), 1)

            pe.wait_ge(S("yb_out"), this(HEADS - 1))
            pe.wait_ge(S("ya_out"), this(HEADS - 1))
            pe.wait_ge(S("gb_out"), this(HEADS - 1))
            pe.wait_ge(S("mod_out"), this(HEADS - 1))
            def project(i, b, first):
                pe.wait_ge(S(f"wp_in{b}"), 32 * (i + 1))
                if not first:
                    pe.wait_ge(S(f"merged_out{b}"), i)
                down_k(PJ[b][:, 0:T], lambda k: wp[b][0][:, k, :], lambda k: ya_g[:, k, :])
                down_k(PJ[b][:, T:], lambda k: wp[b][1][:, k, :], lambda k: yb_g[:, k, :]).then_inc(S(f"proj_mm{b}"), 1)
            for b in range(2):
                pe.wait_ge(S("diag_out"), b + 1)
                if b == 0:
                    pe.wait_ge(S("orms_out"), this(HEADS - 1))
                    pe.wait_ge(S("on_out"), this(HEADS - 1))
                else:
                    pe.wait_ge(S("gate_rows"), 1)
                for hf in range(2):
                    i = mm(bank[6 + hf][:], ones[:, 0:P],
                           diag[:, 4 * hf:4 * hf + 4, :].rearrange("p a b -> p (a b)"), start=True, stop=True)
                i.then_inc(S("gate_mm"), 1)
                project(0, b, True)
            with pe.Fori(1, KT // 2) as i:
                for b in range(2):
                    project(i, b, False)
            pe.wait_ge(S("rt_prep"), 1)
            pe.wait_ge(S("rg_out"), this(HEADS - 1, 1))
            down_k(bank[2][:, 0:NG + NE], lambda k: ones[:, 0:P], lambda k: w_sh[:, k, :]).then_inc(S("gate_mm"), 1)
            pe.wait_ge(S("wo_in"), 32)
            pe.wait_ge(S("merged_out1"), KT // 2)
            pe.wait_ge(S("gate_rows"), 2)

            def w_out_half(t, hf):
                down_k(bank[(4, 0)[t] + hf][:], lambda k: merged[:, k, P * t:P * t + P],
                       lambda k: wo[:, k, 512 * hf:512 * hf + 512]).then_inc(S("wo_mm"), 1)

            def turn_x1(t):
                for hf in range(2):
                    pe.wait_ge(S("x1_out"), 2 * t + hf + 1)
                    if (t, hf) == (1, 0):
                        pe.wait_ge(S("rt_prep"), 3)
                    for k in range(4):
                        i = pe.transpose(bank[(6, 2)[t] + hf][:, P * k:P * k + P],
                                         x1[:, t, 512 * hf + P * k:512 * hf + P * k + P], ident[:])
                    i.then_inc(S("x1_T"), 1)

            def logits(t):
                return down_k(bank[5][:, 64 * t:64 * t + NG + NE], lambda k: x1T[:, k, P * t:P * t + P],
                              lambda k: w_rt[:, k, :])

            w_out_half(0, 0)
            w_out_half(0, 1)
            w_out_half(1, 0)
            turn_x1(0)
            w_out_half(1, 1)
            pe.wait_ge(S("rt_prep"), 2)
            pe.wait_ge(S("x1T_out"), 2)
            logits(0)
            turn_x1(1)
            pe.wait_ge(S("x1T_out"), 3)
            pe.wait_ge(S("x1T_out2"), 1)
            logits(1).then_inc(S("rt_mm"), 1)
            pe.wait_ge(S("sel_out"), 1)
            sel = rt[:, 8]
            mm(bank[7][:, 0:NE], before[:], sel[:, 0, :], start=True, stop=True)
            mm(bank[7][:, NE:2 * NE], ones[:, 0:P], sel[:, 0, :], start=True, stop=False)
            mm(bank[7][:, NE:2 * NE], before[:], sel[:, 1, :], start=False, stop=True)
            mm(bank[7][:, 2 * NE:3 * NE], ones[:, 0:P], sel[:, 0, :], start=True, stop=False)
            mm(bank[7][:, 2 * NE:3 * NE], ones[:, 0:P], sel[:, 1, :], start=False, stop=True).then_inc(S("rank_mm"), 1)

            def gather(half):
                for k in range(4):
                    kt = 4 * half + k
                    for t in range(2):
                        i = mm((GX if half else UX)[:, P * k:P * k + P], xn[:, t, P * kt:P * kt + P],
                               hot[:, t].rearrange("p e s -> p (e s)"), start=t == 0, stop=t == 1)
                i.then_inc(S("mx"), 1)

            def up(acc, kind):
                for k in range(KT):
                    for b in range(2):
                        i = mm(acc[SLOTS * b:SLOTS * b + SLOTS, :], xg[:, k, SLOTS * b:SLOTS * b + SLOTS],
                               wslot(kind, b)[:, k, :], start=k == 0, stop=k == KT - 1)
                return i

            def down(acc, hf):
                for j in range(F // P):
                    for b in range(2):
                        i = mm(acc[SLOTS * b:SLOTS * b + SLOTS, :], gT[:, j, SLOTS * b:SLOTS * b + SLOTS],
                               wslot("w2", b)[:, j, 512 * hf:512 * hf + 512], start=j == 0, stop=j == F // P - 1)
                i.then_inc(S("my"), 1)

            def combine():
                for hf in range(2):
                    for t in range(2):
                        i = mm(ACC[t][hf][:], ct[:, t, :], ys[:, hf, :], start=False, stop=False,
                               skip_group_check=True)
                i.then_inc(S("mc"), 1)

            pe.wait_ge(S("rounds_ready"), 1)
            n_rounds = pe.value_load(rcnt_i[0:1, 0:1], min_val=1, max_val=T // SLOTS)
            with pe.Fori(0, n_rounds) as r:
                g = r * (PAIRS + 1)
                pe.wait_ge(S("hotc"), g + 2)
                pe.wait_ge(S("xgc"), last(g, 1))
                pe.wait_ge(S("xn_out"), 2)
                for half in range(2):
                    gather(half)
                pe.wait_ge(S("acc_read"), r + 1)
                for t in range(2):
                    for hf in range(2):
                        mm(ACC[t][hf][:], zb[:, 0:P], zb[:], start=True, stop=False, skip_group_check=True)
                with pe.Fori(0, PAIRS) as p:
                    q = r * PAIRS + p
                    g = r * (PAIRS + 1) + p
                    pe.wait_ge(S("xgc"), this(g, 1))
                    pe.wait_ge(S("in_w1"), (q + 1) * 32)
                    up(UX, "w1").then_inc(S("m1"), 1)
                    pe.wait_ge(S("ysc"), last(q, 1))
                    pe.wait_ge(S("ctc"), last(q))
                    combine()
                    pe.wait_ge(S("in_w3"), (q + 1) * 32)
                    pe.wait_ge(S("ysc"), last(q, 0))
                    up(VY, "w3").then_inc(S("m3"), 1)
                    pe.wait_ge(S("hw"), this(q))
                    for t in range(2):
                        i = pe.transpose(CY[:, P * t:P * t + P], hotw[:, t].rearrange("p e s -> p (e s)"), ident[:])
                    i.then_inc(S("mtc"), 1)
                    pe.wait_ge(S("gm"), this(q))
                    for j in range(F // P):
                        i = pe.transpose(GX[:, P * j:P * j + P], gm[:, P * j:P * j + P], ident[:])
                    i.then_inc(S("mtg"), 1)
                    pe.wait_ge(S("hotc"), g + 3)
                    gather(0)
                    pe.wait_ge(S("in_w2"), (q + 1) * 32)
                    pe.wait_ge(S("gtc"), this(q))
                    down(VY, 0)
                    gather(1)
                    pe.wait_ge(S("ctc"), this(q))
                    down(CY, 1)
                q = r * PAIRS + PAIRS - 1
                pe.wait_ge(S("ysc"), this(q, 1))
                pe.wait_ge(S("ctc"), this(q))
                combine()

        @block.scalar
        def _(act):
            A = act.activation
            for t in range(4):
                act.wait_ge(S("x_in" if t < 2 else "ctx_in"), 32)
                A(junk[:, t, :], tok[:, t, :], ACT.Square, accum_out=ssq[:, t:t + 1]).then_inc(S("ssq_out"), 1)
            act.wait_ge(S("ms_out"), 1)
            A(rstd[:], rstd[:], ACT.Sqrt).then_inc(S("rms_out"), 1)
            act.wait_ge(S("par_copy"), 1)
            for k in range(2):
                i = A(csil[:, :, k, :], par2[:, 48 + 8 * k:56 + 8 * k].unsqueeze(2).to_broadcast([P, KT, 16]), ACT.Silu)
            i.then_inc(S("csil_out"), 1)
            act.wait_ge(S("sp0"), 1)
            A(spt[:, 0, :], spt[:, 0, :], ACT.Exp, scale=-1.0).then_inc(S("sp1"), 1)
            A(par[:, V_LBV, :], spt[:, 3, 0:8], ACT.Sigmoid).then_inc(S("lb_out"), 1)
            for k in range(KT):
                act.wait_ge(S("tok_T"), k + 1)
                A(h_ct[:, k, EDGE:], PJ[k % 2][:], ACT.Copy).then_inc(S("tok_copy"), 1)
            for i in range(4):
                act.wait_ge(S("pro_rows"), i + 1)
                A(wpro[i][:, 0, :], bank[2 + i][:], ACT.Copy).then_inc(S("pro_part"), 1)
            act.wait_ge(S("aff1_out"), 1)
            act.wait_ge(S("tok_copy"), KT)
            for k in range(0, KT, 2):
                for s in range(2):
                    i = A(h_ct[:, k, EDGE + T * s:EDGE + T * s + T], h_ct[:, k, EDGE + T * s:EDGE + T * s + T], ACT.Identity,
                          scale=aff1[:, s, k:k + 1], bias=modA[:, k, s:s + 1])
            i.then_inc(S("h_ct_out"), 1)
            act.wait_ge(S("zero_set"), 1)

            with act.Fori(0, HEADS) as h:
                def col(v):
                    return hp[:, v:v + 1]

                act.wait_ge(S("a_mm"), this(h))
                act.wait_ge(S("conv_out"), last(h))
                A(a_pad[:, 2:2 + T].rearrange("p (r c) -> p r c", r=ROWS),
                  PJ[0][:, EDGE:EDGE + T].rearrange("p (c r) -> p r c", r=ROWS), ACT.Copy)
                A(a_edge[:, 2:2 + EDGE], PJ[0][:, 0:EDGE], ACT.Copy).then_inc(S("a_out"), 1)
                act.wait_ge(S("q_mm"), this(h))
                act.wait_ge(S("qs_out"), last(h))
                A(sq, PJ[1][:, 0:T], ACT.Sigmoid).then_inc(S("sq_out"), 1)
                act.wait_ge(S("ya_out"), last(h))
                A(gl, PJ[1][:, T:], ACT.Gelu_apprx_tanh).then_inc(S("ay_out"), 1)

                def forget(d, bank_, mm_sem, out_sem):
                    act.wait_ge(S(mm_sem), this(h))
                    act.wait_ge(S("ln_out"), last(h, d))
                    act.wait_ge(S("g_out"), last(h, d))
                    A(gg[d], bank_[:], ACT.Sigmoid).then_inc(S(out_sem), 1)

                def gates(d):
                    act.wait_ge(S("ra_mm"), this(h, d))
                    act.wait_ge(S("hp_out"), this(h))
                    act.wait_ge(S("aa_out"), last(h, d))
                    A(rg[d], GT[0][:, 0:TU], ACT.Sigmoid, bias=col(V_BA + d)).then_inc(S("rg_out"), 1)
                    act.wait_ge(S("ix_mm"), this(h, d))
                    act.wait_ge(S("b_out"), last(h, d))
                    A(ig[d], GT[1][:, 0:TU], ACT.Sigmoid, bias=col(V_BX + d)).then_inc(S("ig_out"), 1)
                    act.wait_ge(S("scan_out"), last(h, d))
                    act.wait_ge(S("rg_out"), this(h, d))
                    A(tz[d], rg[d], ACT.Tanh, scale=col(V_PSP + d)).then_inc(S("tz_out"), 1)

                def logs(d):
                    act.wait_ge(S("g_out"), this(h, d))
                    act.wait_ge(S("lc_out"), last(h, d))
                    A(lf[d], gg[d], ACT.Ln).then_inc(S("ln_out"), 1)

                def exps(d):
                    act.wait_ge(S("rg_out"), this(h, d))
                    act.wait_ge(S("scan_out"), last(h, d))
                    A(aa[d], rg[d], ACT.Exp, scale=col(V_NSP + d)).then_inc(S("aa_out"), 1)
                    act.wait_ge(S("lc_out"), this(h, d))
                    act.wait_ge(S("kdt_mm"), last(h, d))
                    A(ec[d], rcx[d], ACT.Exp).then_inc(S("ec_out"), 1)
                    A(e4[d], d4[d], ACT.Exp).then_inc(S("e4_out"), 1)
                    act.wait_ge(S("att_mm"), last(h, d))
                    A(e1[d], dm[d], ACT.Exp)
                    A(e2[d], dm[d], ACT.Exp, scale=-1.0).then_inc(S("e1_out"), 1)
                    act.wait_ge(S("inter_mm"), last(h, d))
                    act.wait_ge(S("chain_b"), last(h, d))
                    A(etot[:, d, :], lcx[d][:, (CH - 1 if d == 0 else 0):T:CH], ACT.Exp)
                    A(e3[d], lcx[d], ACT.Exp).then_inc(S("exps_out"), 1)

                forget(0, PJ[0], "ff_mm", "ff_out")
                gates(0)
                logs(0)
                exps(0)
                forget(1, PJ[1], "fb_mm", "fb_out")
                gates(1)
                logs(1)
                exps(1)
                act.wait_ge(S("v_mm"), this(h))
                act.wait_ge(S("zero_set"), 1)
                act.wait_ge(S("inter_mm"), last(h, 1))
                for j in range(P // CH):
                    s = slice(CH * j, CH * j + CH)
                    A(vbd[s, :, j, :], PJ[0][s, 0:2 * P].rearrange("p (t n) -> p t n", t=2), ACT.Copy)
                A(vv.rearrange("p a b -> p (a b)"), PJ[0][:], ACT.Copy).then_inc(S("v_out"), 1)

                def keys_out(d):
                    act.wait_ge(S("kdt_mm"), this(h, d))
                    act.wait_ge(S("kv_b"), last(h, d))
                    A(kdT[d].rearrange("p a b -> p (a b)"), TB[:], ACT.Copy).then_inc(S("kdT_out"), 1)

                keys_out(0)
                keys_out(1)
                for d in range(2):
                    act.wait_ge(S("w_out"), this(h, d))
                    A(tz[d], tz[d], ACT.Sqrt, scale=2.0).then_inc(S("sqrt_out"), 1)
                act.wait_ge(S("og_mm"), this(h))
                act.wait_ge(S("yb_out"), last(h))
                A(sog, PJ[1][:, 0:T], ACT.Silu).then_inc(S("og_out"), 1)
                A(s_ga[:, h, :], PJ[1][:, T:], ACT.Sigmoid).then_inc(S("ga_out"), 1)
                act.wait_ge(S("gb_mm"), this(h))
                A(s_gb[:, h, :], PJ[0][:, 0:T], ACT.Sigmoid).then_inc(S("gb_out"), 1)
                act.wait_ge(S("modr_mm"), this(h))
                A(wmod[:, 0, :], PJ[1][:], ACT.Copy).then_inc(S("modr_out"), 1)
                act.wait_ge(S("inter_mm"), this(h, 1))
                act.wait_ge(S("rms_mm"), last(h))
                A(osq, OB[:, 0:T], ACT.Square).then_inc(S("osq_out"), 1)
                act.wait_ge(S("rms_mm"), this(h))
                act.wait_ge(S("on_out"), last(h))
                A(orr, AB[:, 0:T], ACT.Sqrt, bias=eps_t[:, 0:1]).then_inc(S("orms_out"), 1)

            def square(t, hf):
                act.wait_ge(S("x1_out"), 2 * t + hf + 1)
                s = slice(512 * hf, 512 * hf + 512)
                A(junk2[:, t, s], x1[:, t, s], ACT.Square, accum_out=ssq[:, 2 * hf + t:2 * hf + t + 1]).then_inc(S("ssq_out"), 1)

            def x1T_copy(t, hf):
                act.wait_ge(S("x1_T"), 2 * t + hf + 1)
                A(x1T[:, 4 * hf:4 * hf + 4, P * t:P * t + P],
                  bank[(6, 2)[t] + hf][:].rearrange("p (k n) -> p k n", k=4), ACT.Copy).then_inc(S("x1T_out"), 1)

            square(0, 0)
            square(0, 1)
            x1T_copy(0, 0)
            x1T_copy(0, 1)
            square(1, 0)
            x1T_copy(1, 0)
            square(1, 1)
            act.wait_ge(S("ms_out"), 2)
            A(rstd[:, 0:2], rstd[:, 0:2], ACT.Sqrt).then_inc(S("rms_out"), 1)
            act.wait_ge(S("rstd_out"), 1)
            act.wait_ge(S("wo_mm"), 4)
            for t in range(2):
                A(xn[:, t, :], x1[:, t, :], ACT.Identity, scale=rstd[:, t:t + 1]).then_inc(S("xn_out"), 1)
            for n in range(2):
                act.wait_ge(S("rt_sub"), n + 1)
                src_ = rt_g[:, :, 1, :] if n == 0 else rcol[:, 6, :]
                A(src_, src_, ACT.Exp).then_inc(S("rt_exp"), 1)

            act.wait_ge(S("rounds_ready"), 1)
            n_rounds = act.value_load(rcnt_i[0:1, 0:1], min_val=1, max_val=T // SLOTS)
            with act.Fori(0, n_rounds) as r:
                def xg_out(half, g):
                    act.wait_ge(S("mx"), this(g, half))
                    for k in range(4):
                        kt = 4 * half + k
                        i = A(xg[:, kt, :], (GX if half else UX)[:, P * k:P * k + P], ACT.Identity,
                              scale=aff2[:, kt:kt + 1], bias=modB[:, 8 + kt:9 + kt])
                    i.then_inc(S("xgc"), 1)

                act.wait_ge(S("m3"), last(r * PAIRS))
                for half in range(2):
                    xg_out(half, r * (PAIRS + 1))
                with act.Fori(0, PAIRS) as p:
                    q = r * PAIRS + p
                    g = r * (PAIRS + 1) + p
                    act.wait_ge(S("m1"), this(q))
                    act.wait_ge(S("gm"), last(q))
                    A(sh, UX[:], ACT.Silu).then_inc(S("sh"), 1)
                    act.wait_ge(S("mtc"), this(q))
                    act.wait_ge(S("mc"), g + 2)
                    A(ct.rearrange("p a b -> p (a b)"), CY[:, 0:2 * P], ACT.Copy).then_inc(S("ctc"), 1)
                    act.wait_ge(S("mtg"), this(q))
                    act.wait_ge(S("my"), last(q, 1))
                    A(gT.rearrange("p a b -> p (a b)"), GX[:], ACT.Copy).then_inc(S("gtc"), 1)
                    act.wait_ge(S("m3"), this(q))
                    xg_out(0, g + 1)
                    xg_out(1, g + 1)

            act.wait_ge(S("x1_out"), 5)
            for t in range(2):
                A(xn[:, t, :], x1[:, t, :], ACT.Square, accum_out=ssq[:, t:t + 1]).then_inc(S("ssq_out"), 1)
            act.wait_ge(S("ms_out"), 3)
            A(rstd[:, 0:2], rstd[:, 0:2], ACT.Sqrt).then_inc(S("rms_out"), 1)

        @block.vector
        def _(dve):
            cp, tt, ts, stt = dve.tensor_copy, dve.tensor_tensor, dve.tensor_scalar, dve.scalar_tensor_tensor

            class Chain:

                def __init__(self, name, base=0, per=None):
                    self.sem, self.base, self.n, self.per = S(name), base, 0, per

                def __call__(self, ins):
                    self.n += 1
                    ins.then_inc(self.sem, 1)
                    dve.wait_ge(self.sem, self.base + self.n)

            serial = Chain("serial_step")
            link = serial
            link(dve.memset(eps_t[:], EPS))
            dve.wait_ge(S("ident_set"), 1)
            for n in range(2):
                i = dve.tensor_reduce(quad[:, n:n + 1], ident[:, 16 * n:P:32], AX.X, ALU.add)
            i.then_inc(S("quad_set"), 1)
            dve.wait_ge(S("par_T"), 1)
            cp(par[:, 0:16, :].rearrange("p a b -> p (a b)"), bank[7][:, 0:P])
            cp(par2[:], bank[7][:, P:P + 64]).then_inc(S("par_copy"), 1)
            dve.wait_ge(S("par_copy"), 1)
            lam = par[:, V_LAM:V_LAM + 2, :].rearrange("p a b -> p (a b)")
            link(ts(spt[:, 1, :], lam, -1.0, None, ALU.mult))
            tt(spt[:, 3, 0:8], par[:, V_LB, :], par[:, V_LB + 1, :], ALU.subtract)
            tt(spt[:, 0, :], spt[:, 1, :], lam, ALU.max).then_inc(S("sp0"), 1)
            dve.wait_ge(S("ssq_out"), 4)
            ts(rstd[:], ssq[:], 1.0 / D, EPS, ALU.mult, ALU.add).then_inc(S("ms_out"), 1)
            dve.wait_ge(S("rms_out"), 1)
            link(dve.reciprocal(rstd[:], rstd[:]))
            for t in range(4):
                ts(tok[:, t, :], tok[:, t, :], rstd[:, t:t + 1], None, ALU.mult).then_inc(S("xs_out"), 1)
            dve.wait_ge(S("sp1"), 1)
            e_, s_, s2 = spt[:, 0, :], spt[:, 2, :], spt[:, 4, :]
            link(ts(s_, e_, 2.0, None, ALU.add))
            link(dve.reciprocal(s_, s_))
            link(tt(s_, s_, e_, ALU.mult))
            link(tt(s2, s_, s_, ALU.mult))
            acc = spt[:, 0, :]
            link(ts(acc, s2, 1.0 / 17, None, ALU.mult))
            for n in range(15, 1, -2):
                link(stt(acc, acc, 1.0 / n, s2, ALU.add, ALU.mult))
            link(stt(acc, acc, 1.0, s_, ALU.add, ALU.mult))
            link(ts(acc, acc, 2.0, None, ALU.mult))
            link(stt(acc, spt[:, 1, :], 0.0, acc, ALU.max, ALU.add))
            sp2 = lambda v: par[:, v:v + 2, :].rearrange("p a b -> p (a b)")
            ts(sp2(V_PSP), acc, 8.0, None, ALU.mult)
            ts(sp2(V_NSP), acc, -8.0, None, ALU.mult)
            dve.wait_ge(S("lb_out"), 1)
            ts(par[:, V_OML, :], par[:, V_LBV, :], -1.0, 1.0, ALU.mult, ALU.add).then_inc(S("par_done"), 1)
            dve.wait_ge(S("pro_mm"), 1)
            link(tt(modA[:], bank[6][:, 0:32].rearrange("p (m s) -> p m s", s=2),
               par2[:, 0:16].unsqueeze(2).to_broadcast([P, 16, 2]), ALU.add))
            link(ts(aff1[:], modA[:, 8:16, :].rearrange("p m s -> p s m"), 1.0, None, ALU.add))
            tt(aff1[:], aff1[:], par[:, V_N1, :].unsqueeze(1).to_broadcast([P, 2, KT]), ALU.mult).then_inc(S("aff1_out"), 1)
            dve.wait_ge(S("aff1_out"), 1)
            dve.wait_ge(S("tok_copy"), KT)
            for k in range(1, KT, 2):
                for s in range(2):
                    i = ts(h_ct[:, k, EDGE + T * s:EDGE + T * s + T], h_ct[:, k, EDGE + T * s:EDGE + T * s + T], aff1[:, s, k:k + 1],
                           modA[:, k, s:s + 1], ALU.mult, ALU.add)
            link(i)
            dve.wait_ge(S("h_ct_out"), 1)
            cp(h_ct[:, :, 0:3], h_ct[:, :, EDGE + T:EDGE + T + 3])
            cp(h_ct[:, :, 3:EDGE], h_ct[:, :, EDGE + 2 * T - 3:]).then_inc(S("edges_out"), 1)
            dve.wait_ge(S("par_done"), 1)
            dve.wait_ge(S("zero_set"), 1)

            N_STEP = 13
            with dve.Fori(0, HEADS) as h:
                link = Chain("head_step", h * N_STEP)

                def col(v):
                    return hp[:, v:v + 1]

                dve.wait_ge(S("aa_out"), last(h, 1))
                dve.wait_ge(S("yb_out"), last(h))
                cp(hp[:], par[:, :, h]).then_inc(S("hp_out"), 1)
                dve.wait_ge(S("hp_out"), this(h))
                dve.wait_ge(S("a_out"), this(h))
                dve.wait_ge(S("ix_mm"), last(h, 1))
                dve.wait_ge(S("iu_out"), last(h, 1))
                parts = [(u[:, 0:T], lambda k: a_pad[:, k:k + T]), (u[:, T:], lambda k: a_edge[:, k:k + 6:5])]
                for n, k in enumerate((2, 0, 1, 3)):
                    for dst, window in parts:
                        if n == 0:
                            i = ts(dst, window(k), col(V_CW + k), col(V_CB), ALU.mult, ALU.add)
                        else:
                            i = stt(dst, window(k), col(V_CW + k), dst, ALU.mult, ALU.add)
                    if n < 3:
                        link(i)
                i.then_inc(S("conv_out"), 1)
                dve.wait_ge(S("sq_out"), this(h))
                dve.wait_ge(S("ay_out"), this(h))
                dve.wait_ge(S("prod_q"), last(h, 1))
                dve.wait_ge(S("qe3_out"), last(h, 1))
                tt(qs, PJ[1][:, 0:T], sq, ALU.mult).then_inc(S("qs_out"), 1)

                def forget(d):
                    dve.wait_ge(S(("ff_out", "fb_out")[d]), this(h))
                    dve.wait_ge(S("prod_q"), last(h, d))
                    dve.wait_ge(S("kdc_out"), last(h, d))
                    link(ts(gg[d], gg[d], col(V_OML), col(V_LBV), ALU.mult, ALU.add))
                    ts(kk[d], gg[d], -1.0, 1.0, ALU.mult, ALU.add).then_inc(S("g_out"), 1)

                def logs(d):
                    dve.wait_ge(S("ln_out"), this(h, d))
                    dve.wait_ge(S("exps_out"), last(h, d))
                    if d == 0:
                        link(dve.tensor_tensor_scan(lcx[d], resets[:], lf[d][:, 0:T], 0.0, ALU.mult, ALU.add))
                        dve.tensor_tensor_scan(rcx[d][:, T - 2::-1], ones[:, 0:T - 1], lf[d][:, 2 * T - 1:T:-1],
                                               0.0, ALU.mult, ALU.add)
                    else:
                        link(dve.tensor_tensor_scan(lcx[d][:, T - 1::-1], resets[:], lf[d][:, T - 1::-1], 0.0,
                                                    ALU.mult, ALU.add))
                        dve.tensor_tensor_scan(rcx[d][:, 1:T], ones[:, 0:T - 1], lf[d][:, T:2 * T - 1],
                                               0.0, ALU.mult, ALU.add)
                    lc = lcx[d].rearrange("p (c s) -> p c s", s=CH)
                    mid, tot = (MID, CH - 1) if d == 0 else (CH - 1 - MID, 0)
                    tt(dm[d].rearrange("p (c s) -> p c s", s=CH), lc,
                       lc[:, :, mid:mid + 1].to_broadcast([P, NCH, CH]), ALU.subtract)
                    tt(d4[d].rearrange("p (c s) -> p c s", s=CH),
                       lc[:, :, tot:tot + 1].to_broadcast([P, NCH, CH]), lc, ALU.subtract).then_inc(S("lc_out"), 1)

                def ratios(d):
                    dve.wait_ge(S("tz_out"), this(h, d))
                    link(ts(rc[d], tz[d], 1.0, None, ALU.add))
                    link(dve.reciprocal(rc[d], rc[d]))
                    tt(tz[d], tz[d], rc[d], ALU.mult).then_inc(S("w_out"), 1)

                def prods(d):
                    dve.wait_ge(S("e4_out"), this(h, d))
                    tt(e4[d], e4[d], kk[d][:, 0:T], ALU.mult).then_inc(S("prod_k"), 1)
                    dve.wait_ge(S("e1_out"), this(h, d))
                    dve.wait_ge(S("qs_out"), this(h))
                    tt(e2[d], e2[d], kk[d][:, 0:T], ALU.mult)
                    tt(e1[d], e1[d], qs, ALU.mult).then_inc(S("prod_q"), 1)

                def scans(d):
                    dve.wait_ge(S("b_out"), this(h, d))
                    dve.wait_ge(S("aa_out"), this(h, d))
                    dve.wait_ge(S("ya_out"), last(h))
                    seq = slice(0, T) if d == 0 else slice(T - 1, None, -1)
                    dve.tensor_tensor_scan(hs[d][:, seq], aa[d][:, seq], tz[d][:, seq], tz[d][:, T + d:T + d + 1],
                                           ALU.mult, ALU.add).then_inc(S("scan_out"), 1)

                def states(d):
                    dve.wait_ge(S("zero_set"), 1)
                    dve.wait_ge(S("att_mm"), this(h, d))
                    dve.wait_ge(S("inter_mm"), last(h, d))
                    dve.wait_ge(S("exps_out"), this(h, d))
                    dve.copy_predicated(att[d], causal[d][:].bitcast(u32).unsqueeze(1).to_broadcast([P, 2, P]),
                                        AB[:, 0:256].rearrange("p (a b) -> p a b", a=2))
                    cp(st[d][:, 0, :], AB[:, 256:384]).then_inc(S("att_out"), 1)
                    dve.wait_ge(S("att_out"), this(h, d))
                    step = Chain(f"state_step{d}", h * (NCH - 3))
                    for j in range(NCH - 1):
                        cj = j if d == 0 else NCH - 1 - j
                        if j == 0:
                            dve.wait_ge(S("kv_a"), this(h, d))
                        if j == 4:
                            dve.wait_ge(S("kv_b"), this(h, d))
                        kv = (KB if j < 4 else TB)[:, P * (cj % 4):P * (cj % 4) + P]
                        i = stt(st[d][:, j + 1, :], st[d][:, j, :], etot[:, d, cj:cj + 1], kv, ALU.mult, ALU.add)
                        if j == 3:
                            i.then_inc(S("chain_a"), 1)
                            dve.wait_ge(S("chain_a"), this(h, d))
                        elif j == NCH - 2:
                            i.then_inc(S("chain_b"), 1)
                        else:
                            step(i)
                    assert step.n == NCH - 3

                forget(0)
                logs(0)
                ratios(0)
                prods(0)
                forget(1)
                logs(1)
                ratios(1)
                prods(1)
                scans(0)
                scans(1)
                dve.wait_ge(S("scan_out"), this(h, 0))
                dve.wait_ge(S("scan_out"), this(h, 1))
                link(tt(hsum, hs[0][:, 0:T], hs[1][:, 0:T], ALU.add))
                tt(ya_g[:, h, :].rearrange("p (c r) -> p c r", r=ROWS), hsum.rearrange("p (r c) -> p c r", r=ROWS),
                   gl.rearrange("p (c r) -> p c r", r=ROWS), ALU.mult).then_inc(S("ya_out"), 1)
                states(0)
                states(1)
                dve.wait_ge(S("mod_mm"), this(h))
                tt(modB[:, bass.ds(h * 4, 4)], PJ[1][:, 0:4], par2[:, bass.ds(h * 4 + 16, 4)], ALU.add).then_inc(S("mod_out"), 1)
                dve.wait_ge(S("orms_out"), this(h))
                link(dve.reciprocal(orr, orr))
                dve.wait_ge(S("osq_out"), this(h))
                tt(on, OB[:, 0:T], orr, ALU.mult).then_inc(S("on_out"), 1)
                dve.wait_ge(S("on_out"), this(h))
                dve.wait_ge(S("og_out"), this(h))
                stt(yb_g[:, h, :], on, col(V_HG), sog, ALU.mult, ALU.mult).then_inc(S("yb_out"), 1)
                assert link.n == N_STEP, link.n

            def merge(i, b, first):
                m = 2 * i + b
                dve.wait_ge(S(f"proj_mm{b}"), i + 1)
                if not first:
                    dve.wait_ge(S(f"merged_out{b}"), i)
                tt(m1[b], PJ[b][:, 0:T], s_ga[:, m, :], ALU.mult)
                tt(m2[b], PJ[b][:, T:], s_gb[:, m, :], ALU.mult).then_inc(S(f"m2_out{b}"), 1)
                dve.wait_ge(S(f"m2_out{b}"), i + 1)
                tt(merged[:, m, :], m1[b], m2[b], ALU.add).then_inc(S(f"merged_out{b}"), 1)
            dve.wait_ge(S("mod_out"), this(HEADS - 1))
            dve.wait_ge(S("gb_mm"), this(HEADS - 1))
            for v, (row, c0) in enumerate(((gate1, 0), (gate2, 24))):
                tt(diag, ident[:].unsqueeze(1).to_broadcast([P, KT, P]),
                   modB[:, c0:c0 + KT].unsqueeze(2).to_broadcast([P, KT, P]), ALU.mult).then_inc(S("diag_out"), 1)
                dve.wait_ge(S("gate_mm"), v + 1)
                for hf in range(2):
                    i = cp(row[:, 512 * hf:512 * hf + 512], bank[6 + hf][:])
                i.then_inc(S("gate_rows"), 1)
            dve.wait_ge(S("ga_out"), this(HEADS - 1))
            dve.wait_ge(S("gb_out"), this(HEADS - 1))
            for b in range(2):
                merge(0, b, True)
            with dve.Fori(1, KT // 2) as i:
                for b in range(2):
                    merge(i, b, False)

            link = serial
            link(ts(aff2[:], modB[:, 16:24], 1.0, None, ALU.add))
            link(tt(aff2[:], aff2[:], par[:, V_N2, :], ALU.mult))
            dve.wait_ge(S("rt_in"), 64)
            across = lambda v: v.unsqueeze(2).to_broadcast([P, KT, NG + NE])
            tt(w_sh, w_rt[:], across(modB[:, 8:16]), ALU.mult).then_inc(S("rt_prep"), 1)
            dve.wait_ge(S("rt_prep"), 1)
            tt(w_rt[:], w_rt[:], across(aff2[:]), ALU.mult).then_inc(S("rt_prep"), 1)
            dve.wait_ge(S("gate_mm"), 3)
            tt(b_rt[:], b_rt[:], bank[2][:, 0:NG + NE], ALU.add).then_inc(S("rt_prep"), 1)
            dve.wait_ge(S("gate_rows"), 2)
            dve.wait_ge(S("xr_in"), 32)
            for t in range(2):
                for hf in range(2):
                    dve.wait_ge(S("wo_mm"), 2 * t + hf + 1)
                    s = slice(512 * hf, 512 * hf + 512)
                    link(tt(x1[:, t, s], bank[(4, 0)[t] + hf][:], gate1[:, s], ALU.mult))
                    tt(x1[:, t, s], x1[:, t, s], xr[:, t, s], ALU.add).then_inc(S("x1_out"), 1)
            dve.wait_ge(S("x1_T"), 4)
            cp(x1T[:, 4:8, P:], bank[3][:].rearrange("p (k n) -> p k n", k=4)).then_inc(S("x1T_out2"), 1)
            dve.wait_ge(S("ssq_out"), 8)
            link(tt(rstd[:, 0:2], ssq[:, 0:2], ssq[:, 2:4], ALU.add))
            ts(rstd[:, 0:2], rstd[:, 0:2], 1.0 / D, EPS, ALU.mult, ALU.add).then_inc(S("ms_out"), 1)
            dve.wait_ge(S("rms_out"), 2)
            dve.reciprocal(rstd[:, 0:2], rstd[:, 0:2]).then_inc(S("rstd_out"), 1)
            dve.wait_ge(S("rstd_out"), 1)

            dve.wait_ge(S("rt_mm"), 1)
            dve.wait_ge(S("rt_prep"), 3)
            for t in range(2):
                i = stt(lg[:, t, :], bank[5][:, 64 * t:64 * t + NG + NE], rstd[:, t:t + 1], b_rt[:], ALU.mult, ALU.add)
            link(i)
            R = lambda j: rcol[:, j, :]
            bc = lambda a, n: a.unsqueeze(2).to_broadcast([P, 2, n])
            lgg = lg[:, :, 0:NG]
            link(dve.tensor_reduce(R(0), lgg, AX.X, ALU.max))
            tt(rt_g[:, :, 1, :], lgg, bc(R(0), NG), ALU.subtract).then_inc(S("rt_sub"), 1)
            link(tt(rt_g[:, :, 0, :], lgg, bc(R(0), NG), ALU.is_equal))

            def first_of(eq, dst, cum):
                for t in range(2):
                    i = dve.tensor_tensor_scan(cum[:, t, :], ones[:, 0:eq[:, t, :].shape[-1]], eq[:, t, :], 0.0,
                                               ALU.mult, ALU.add)
                link(i)
                link(stt(dst, cum, 1.0, eq, ALU.is_equal, ALU.mult))
            first_of(rt_g[:, :, 0, :], rt_g[:, :, 3, :], rt_g[:, :, 2, :])
            dve.wait_ge(S("rt_exp"), 1)
            link(dve.tensor_reduce(R(1), rt_g[:, :, 1, :], AX.X, ALU.add))
            link(dve.reciprocal(R(2), R(1)))
            link(ts(rt_g[:, :, 0, :], rt_g[:, :, 3, :], 1.0, BIG, ALU.subtract, ALU.mult))
            for t in range(2):
                i = tt(rt[:, 0, t, :].rearrange("p (g e) -> p g e", g=NG),
                       lg[:, t, NG:].rearrange("p (g e) -> p g e", g=NG),
                       rt_g[:, t, 0, :].unsqueeze(2).to_broadcast([P, NG, EPG]), ALU.add)
            link(i)
            link(dve.tensor_reduce(R(3), rt[:, 0], AX.X, ALU.max))
            link(tt(rt[:, 1], rt[:, 0], bc(R(3), NE), ALU.is_equal))
            first_of(rt[:, 1], rt[:, 3], rt[:, 2])
            link(stt(rt[:, 4], rt[:, 3], -3 * BIG, rt[:, 0], ALU.mult, ALU.add))
            link(dve.tensor_reduce(R(4), rt[:, 4], AX.X, ALU.max))
            link(tt(rt[:, 5], rt[:, 4], bc(R(4), NE), ALU.is_equal))
            tt(R(6), R(4), R(3), ALU.subtract).then_inc(S("rt_sub"), 1)
            first_of(rt[:, 5], rt[:, 7], rt[:, 6])
            dve.wait_ge(S("rt_exp"), 2)
            link(ts(R(7), R(6), 1.0, None, ALU.add))
            link(dve.reciprocal(R(7), R(7)))
            link(tt(R(8), R(7), R(2), ALU.mult))
            link(tt(R(9), R(8), R(6), ALU.mult))
            tt(rt[:, 8], rt[:, 3], rt[:, 7], ALU.add).then_inc(S("sel_out"), 1)
            link(tt(rt[:, 9], rt[:, 3], bc(R(8), NE), ALU.mult))
            link(tt(rt[:, 10], rt[:, 7], bc(R(9), NE), ALU.mult))
            tt(cw[:], rt[:, 9], rt[:, 10], ALU.add)
            link(dve.memset(rank, -1.0))
            dve.wait_ge(S("sel_out"), 1)
            dve.wait_ge(S("rank_mm"), 1)
            link(stt(rt[:, 11], bank[7][:, 0:2 * NE].rearrange("p (t n) -> p t n", t=2), 1.0, rt[:, 8],
                     ALU.add, ALU.mult))
            link(ts(rank[:, :, 0:NE], rt[:, 11], 1.0, None, ALU.subtract))
            link(dve.tensor_reduce(rcnt[:, 0:1], bank[7][:, 2 * NE:3 * NE], AX.X, ALU.max))
            link(ts(rcnt[:, 1:2], rcnt[:, 0:1], float(SLOTS), 1.0, ALU.is_gt, ALU.add))
            link(stt(rcnt[:, 2:3], rcnt[:, 0:1], float(2 * SLOTS), rcnt[:, 1:2], ALU.is_gt, ALU.add))
            link(stt(rcnt[:, 3:4], rcnt[:, 0:1], float(3 * SLOTS), rcnt[:, 2:3], ALU.is_gt, ALU.add))
            dve.memset(ct, 0.0)
            dve.memset(ys, 0.0)
            cp(rcnt_i[:], rcnt[:, 3:4].to_broadcast([P, 4])).then_inc(S("rounds_ready"), 1)
            dve.wait_ge(S("rounds_ready"), 1)
            n_rounds = dve.value_load(rcnt_i[0:1, 0:1], min_val=1, max_val=T // SLOTS)
            with dve.Fori(0, n_rounds) as r:
                def one_hots(first, g):
                    dve.wait_ge(S("mx"), last(g, 1))
                    for e in range(2):
                        i = tt(hot[:, :, e, :], slot_no[:].unsqueeze(1).to_broadcast([P, 2, SLOTS]),
                               rank[:, :, bass.ds(first + e, 1)].to_broadcast([P, 2, SLOTS]), ALU.is_equal)
                    i.then_inc(S("hotc"), 1)

                dve.wait_ge(S("hw"), last(r * PAIRS))
                one_hots(0, r * (PAIRS + 1))
                with dve.Fori(0, PAIRS) as p:
                    q = r * PAIRS + p
                    g = r * (PAIRS + 1) + p
                    dve.wait_ge(S("hotc"), g + 2)
                    dve.wait_ge(S("mtc"), last(q))
                    for e in range(2):
                        i = tt(hotw[:, :, e, :], hot[:, :, e, :],
                               cw[:, :, bass.ds(p * 2 + e, 1)].to_broadcast([P, 2, SLOTS]), ALU.mult)
                    i.then_inc(S("hw"), 1)
                    dve.wait_ge(S("hw"), this(q))
                    one_hots(p * 2 + 2, g + 1)
                    dve.wait_ge(S("m3"), this(q))
                    dve.wait_ge(S("sh"), this(q))
                    dve.wait_ge(S("mtg"), last(q))
                    tt(gm, sh, VY[:], ALU.mult).then_inc(S("gm"), 1)
                    dve.wait_ge(S("mc"), g + 2)
                    for hf in range(2):
                        dve.wait_ge(S("my"), this(q, hf))
                        cp(ys[:, hf, :], (CY if hf else VY)[:]).then_inc(S("ysc"), 1)
                dve.wait_ge(S("mc"), (r + 1) * (PAIRS + 1) + 1)
                dve.memset(ct, 0.0)
                step = Chain("res_step", r * 4)
                for t in range(2):
                    for hf in range(2):
                        s = slice(512 * hf, 512 * hf + 512)
                        i = tt(res[:, s], ACC[t][hf][:], gate2[:, s], ALU.mult)
                    step(i)
                    step(tt(x1[:, t, :], x1[:, t, :], res, ALU.add))
                ts(rank, rank, float(SLOTS), None, ALU.subtract).then_inc(S("acc_read"), 1)
                dve.wait_ge(S("acc_read"), r + 2)

            link = serial
            dve.memset(ssq[:], 0.0).then_inc(S("x1_out"), 1)
            dve.wait_ge(S("ssq_out"), 10)
            ts(rstd[:, 0:2], ssq[:, 0:2], 1.0 / D, EPS, ALU.mult, ALU.add).then_inc(S("ms_out"), 1)
            dve.wait_ge(S("rms_out"), 3)
            link(dve.reciprocal(rstd[:, 0:2], rstd[:, 0:2]))
            dve.wait_ge(S("fg_in"), 16)
            for t in range(2):
                stt(xn[:, t, :], x1[:, t, :], rstd[:, t:t + 1], fin_g, ALU.mult, ALU.mult).then_inc(S("y_out"), 1)


_INS = ['x', 'c', 'ctx', 'c_ctx', 'w_mod', 'b_mod', 'norm1_g', 'w_in', 'conv_w', 'conv_b', 'lru_wa', 'lru_ba',
        'lru_wx', 'lru_bx', 'lru_lam', 'hg_lb', 'hg_norm_g', 'w_proj_a', 'w_proj_b', 'w_out', 'norm2_g', 'w_rg',
        'b_rg', 'w_re', 'b_re', 'w1', 'w3', 'w2', 'final_g']


def kernel(**inputs):
    import numpy as np
    import concourse.bacc as bacc
    from concourse.bass_utils import run_bass_kernel_spmd

    nc = bacc.Bacc("TRN2", target_bir_lowering=False, num_devices=1)
    arrays, args = {}, []
    for name in _INS:
        a = np.ascontiguousarray(inputs[name])
        arrays[f"in_{name}"] = a
        args.append(nc.dram_tensor(f"in_{name}", a.shape, mybir.dt.from_np(a.dtype), kind="ExternalInput").ap())
    out = nc.dram_tensor("out_0", (1, T, D), mybir.dt.float32, kind="ExternalOutput").ap()
    build(nc, *args, out)
    r = run_bass_kernel_spmd(nc, [arrays], core_ids=[0])
    return r.results[0]["out_0"]
```

```python
import concourse.bass as bass
from concourse import mybir
from contextlib import ExitStack

D = 1024
P = 128
KT = D // P
T = 256
GW = 64
ROWS = T // GW
HEADS = 8
CH = 32
NCH = T // CH
MID = CH // 2
EPS = 1e-6
NE = 32
NG = 4
EPG = NE // NG
F = 512
SLOTS = 64
PAIRS = NE // 2
BIG = 1e30

BLK = {"a": 0, "ay": 1, "q": 2, "ff": 3, "fb": 4, "v": 5, "og": 6, "ga": 7, "gb": 8}
ORDER = ["a", "q", "ay", "ff", "fb", "v", "og", "ga", "gb"]
SHARED = {"ay": "q", "ga": "og"}

V_CW, V_CB, V_BA, V_BX, V_LAM, V_LB, V_HG, V_N1, V_N2 = 0, 4, 5, 7, 9, 11, 13, 14, 15
V_NSP, V_PSP, V_LBV, V_OML = 16, 18, 20, 21
NV = 22

SLOT = 4096
RING = (1, 2, 3, 4, 5, 6, 0, 7)
UNROLL = 4
A_WBLK = 0
A_WLRU = 9 * 1024
A_WMOD = A_WLRU + 512
A_PRO = 7680
A_R = A_WMOD + 4096
A_YA = 6 * SLOT
A_CS = A_YA - 256
A_YB = A_YA + 2048
A_GA = A_YB + 2048
A_GB = A_GA + 2048
A_HT = A_GB + 2048
EDGE = 6
TU = T + 2
A_MG = A_HT + KT * (EDGE + 2 * T)
A_T = A_MG + 2048
ARENA = A_T + 11784


def build(nc, x, c, ctx_in, c_ctx, w_mod, b_mod, norm1_g, w_in, conv_w, conv_b, lru_wa, lru_ba, lru_wx, lru_bx,
          lru_lam, hg_lb, hg_norm_g, w_proj_a, w_proj_b, w_out, norm2_g, w_rg, b_rg, w_re, b_re,
          w1, w3, w2, final_g, out):
    f32 = mybir.dt.float32
    bf16 = mybir.dt.bfloat16
    u32 = mybir.dt.uint32
    i32 = mybir.dt.int32
    ACT = mybir.ActivationFunctionType
    ALU = mybir.AluOpType
    AX = mybir.AxisListType

    with ExitStack() as es:
        arena = es.enter_context(nc.sbuf_tensor("arena", [P, ARENA], f32))

        def at(start, *shape):
            n = 1
            for s in shape:
                n *= s
            v = arena[:, start:start + n]
            if len(shape) == 2:
                v = v.rearrange("p (a b) -> p a b", a=shape[0])
            if len(shape) == 3:
                v = v.rearrange("p (a b c) -> p a b c", a=shape[0], b=shape[1])
            return v

        def sb(name, *shape, dt=f32):
            return es.enter_context(nc.sbuf_tensor(name, [P, *shape], dt))

        sems = {}

        def S(name):
            if name not in sems:
                sems[name] = es.enter_context(nc.semaphore(name))
            return sems[name]

        ident = sb("ident", P)
        mean_w = sb("mean_w", P)
        ones = sb("ones", T)
        resets = sb("resets", T)
        causal = [sb("causal_f", P), sb("causal_b", P)]
        before = sb("before", P)
        slot_no = sb("slot_no", SLOTS)
        zb = sb("zb", 4 * P, dt=bf16)
        prows = at(A_T + 5120, 2, P)
        par = sb("par", NV, HEADS)
        par2 = sb("par2", 64)
        quad = sb("quad", 2)
        modA = sb("modA", 16, 2)
        modB = sb("modB", 32)
        aff1 = sb("aff1", 2, KT)
        aff2 = sb("aff2", KT)
        ssq = sb("ssq", 4)
        rstd = sb("rstd", 4)
        hp = sb("hp", NV)
        etot = sb("etot", 2, NCH)
        w_rt = sb("w_rt", KT, NG + NE)
        b_rt = sb("b_rt", NG + NE)
        spt = sb("spt", 5, 16)
        rcnt = sb("rcnt", 4)
        rcnt_i = sb("rcnt_i", 4, dt=i32)
        eps_t = sb("eps_t", 1)
        cw = sb("cw", 2, NE)

        bank = [es.enter_context(nc.psum_tensor(f"bank{i}", [P, 512], f32)) for i in range(8)]
        PJ = [bank[0], bank[1]]
        GT = [bank[2], bank[3]]
        TB, KB, AB, OB = bank[4:8]

        h_ct = at(A_HT, KT, EDGE + 2 * T)
        wblk = {n: at(A_WBLK + 1024 * i, KT, P) for i, n in enumerate(ORDER)}
        wlru = at(A_WLRU, 4, P)
        wmod = at(A_WMOD, KT, 512)
        wpro = [at(A_PRO + 4096 * i, KT, 512) for i in range(4)]
        csil = at(A_CS, KT, 2, 16)
        ya_g, yb_g, s_ga, s_gb = (at(a, HEADS, T) for a in (A_YA, A_YB, A_GA, A_GB))
        merged = at(A_MG, KT, T)
        tok = at(A_T, 4, D)
        junk = at(A_YA, 4, D)
        o = A_T
        a_pad = at(o, T + 3)
        a_edge = at(o + T + 4, EDGE + 4)
        o += 520
        u = at(o, TU)
        o += 512
        rg, ig, tz, aa, rc, hs = ([at(o + 512 * (2 * j + d), TU) for d in range(2)] for j in range(6))
        o += 12 * 512
        gl = at(o, T)
        hsum = at(o + 256, T)
        qs = at(o + 512, T)
        sq = at(o + 768, T)
        o += 1024
        kdT = [at(o + 512 * d, 4, P) for d in range(2)]
        o += 1024
        att = [at(o + 256 * d, 2, P) for d in range(2)]
        o += 512
        st = [at(o + 1024 * d, NCH, P) for d in range(2)]
        o += 2048
        assert o <= ARENA
        o = A_R
        gg, kk, lf = ([at(o + 512 * (2 * j + d), 2 * T) for d in range(2)] for j in range(3))
        o += 6 * 512
        lcx, rcx, dm, d4, e1, e2, e3, e4, ec = ([at(o + 256 * (2 * j + d), T) for d in range(2)] for j in range(9))
        o += 18 * 256
        vv = at(o, 4, P)
        o += 512
        vbd = at(o, 2, 4, P)
        o += 1024
        osq, orr, on, sog = (at(o + 256 * j, T) for j in range(4))
        o += 1024
        assert o <= A_CS
        wp = [[at(2048 * b + 1024 * j, KT, P) for j in range(2)] for b in range(2)]
        wo = at(A_T, KT, D)
        xr = at(A_HT, 2, D)
        x1 = at(A_HT + 2048, 2, D)
        gate1, gate2, fin_g = (at(A_T + 8192 + 1024 * j, D) for j in range(3))
        diag = at(A_HT + 3072, KT, P)
        w_sh = at(A_HT + 3072, KT, NG + NE)
        m1 = [at(A_HT + 2048 + 512 * b, T) for b in range(2)]
        m2 = [at(A_HT + 2048 + 512 * b + 256, T) for b in range(2)]
        junk2 = at(A_GB, 2, D)
        res = at(A_T, D)
        xn = at(A_MG, 2, D)
        x1T = at(A_GA, KT, T)
        xg = at(A_HT, KT, 2 * SLOTS)
        o = A_T + 2048
        hot = at(o, 2, 2, SLOTS)
        o += 256
        hotw = at(o, 2, 2, SLOTS)
        o += 256
        ct = at(o, 2, P)
        o += 256
        sh = at(o, F)
        o += 512
        gm = at(o, F)
        o += 512
        gT = at(o, 4, P)
        o += 512
        ys = at(o, 2, F)
        o += 1024
        lg = at(o, 2, NG + NE)
        o += 72
        rt_g = at(o, 2, 4, NG)
        o += 32
        rt = at(o, 12, 2, NE)
        o += 12 * 64
        rcol = at(o, 16, 2)
        o += 32
        rank = at(o, 2, NE + 2)
        o += 2 * (NE + 2)
        assert o <= A_T + 8192
        ring = [at(SLOT * s, SLOT) for s in RING]
        KINDS = [(k, b) for k in ("w1", "w3", "w2") for b in range(2)]

        def wslot(kind, b, j):
            s = ring[(6 * j + KINDS.index((kind, b))) % len(RING)]
            return s.rearrange("p (k n) -> p k n", n=D if kind == "w2" else F)

        ACC = [[bank[0], bank[1]], [bank[2], bank[3]]]
        UX, VY, CY, GX = bank[4:8]

        cm = "(r c) d -> c r d"
        x_cm = x[0].rearrange(cm, r=ROWS)
        out_cm = out[0].rearrange(cm, r=ROWS)
        wi_v = w_in[0].rearrange("(k p) n -> p k n", p=P)
        wm_v = w_mod[0].rearrange("(k p) n -> p k n", p=P)
        lru_v = [[w[0, d].rearrange("h i j -> i h j") for w in (lru_wa, lru_wx)] for d in range(2)]
        wpa_v, wpb_v, wo_v = (w[0].rearrange("(k p) n -> p k n", p=P) for w in (w_proj_a, w_proj_b, w_out))
        w1_v, w3_v, w2_v = (w[0].rearrange("e (k p) n -> e p k n", p=P) for w in (w1, w3, w2))
        rows = [(conv_w[0], 4), (conv_b, 1), (lru_ba[0], 2), (lru_bx[0], 2), (lru_lam[0], 2), (hg_lb, 2),
                (hg_norm_g, 1), (norm1_g, 1), (norm2_g, 1)]

        def this(h, d=None):
            return h + 2 if d is None else 2 * h + d + 3

        def last(h, d=None):
            return h + 1 if d is None else 2 * h + d + 1

        HEAD_SEMS = ("a_mm q_mm ff_mm fb_mm v_mm og_mm gb_mm mod_mm modr_mm rms_mm a_out sq_out ay_out ff_out fb_out "
                     "v_out og_out ga_out gb_out osq_out orms_out hp_out conv_out qs_out ya_out mod_out modr_out on_out "
                     "yb_out").split()
        DIR_SEMS = ("kdt_mm att_mm kv_a kv_b inter_mm rg_out "
                     " ig_out tz_out ln_out aa_out exps_out ec_out e4_out e1_out kdT_out sqrt_out g_out lc_out w_out prod_k prod_q att_out chain_a chain_b scan_out iu_out b_out kdc_out qe3_out ra_mm ix_mm").split()
        MOE_SEMS = "m1 m3 mtc mtg acc_read hotc sh gm ctc gtc hw".split()
        EXP_SEMS = "my mx ysc xgc mc".split()

        block = es.enter_context(nc.Block())

        @block.sync
        def _(sp):
            for t in range(2):
                sp.dma_start(tok[:, t, :], x_cm[32 * t:32 * t + 32]).then_inc(S("x_in"), 16)
            for t in range(2):
                sp.dma_start(tok[:, 2 + t, :], ctx_in[0, P * t:P * t + P, :]).then_inc(S("ctx_in"), 16)
            sp.dma_start(wpro[0], wm_v[:, :, 0:512]).then_inc(S("pro_in0"), 16)
            r0 = 0
            for v, n in rows:
                sp.dma_start(prows[r0:r0 + 8 * n, 0, :], v.rearrange("a (h n) -> (a h) n", n=P)).then_inc(S("par_in"), 16)
                r0 += 8 * n
            sp.dma_start(prows[0:48, 1, :], b_mod[0].rearrange("(h n) -> h n", n=P)).then_inc(S("par_in"), 16)
            sp.dma_start(prows[48:56, 1, :], c[0].rearrange("(h n) -> h n", n=P)).then_inc(S("par_in"), 16)
            sp.dma_start(prows[56:64, 1, :], c_ctx.rearrange("(h n) -> h n", n=P)).then_inc(S("par_in"), 16)
            for i in range(1, 4):
                sp.dma_start(wpro[i], wm_v[:, :, 512 * i:512 * i + 512]).then_inc(S(f"pro_in{i}"), 16)

            def head_loads(h, first):
                for n, used in zip(ORDER, ("a", "q", "q", "ff", "fb", "v", "og", "og", "gb")):
                    if not first:
                        sp.wait_ge(S(used + "_mm"), last(h))
                    elif n == "ga":
                        sp.wait_ge(S("pro_mm"), 1)
                    sp.dma_start(wblk[n], wi_v[:, :, bass.ds(BLK[n] * D + h * P, P)]).then_inc(S("in_" + SHARED.get(n, n)), 16)
                    if n == "fb":
                        if first:
                            sp.wait_ge(S("pro_mm"), 1)
                        else:
                            sp.wait_ge(S("ix_mm"), last(h, 1))
                        for d in range(2):
                            for j in range(2):
                                sp.dma_start(wlru[:, 2 * d + j, :], lru_v[d][j][:, h, :]).then_inc(S("in_lru"), 16)
                        if not first:
                            sp.wait_ge(S("mod_mm"), last(h))
                        sp.dma_start(wmod, wm_v[:, :, bass.ds(2 * D + h * 512, 512)]).then_inc(S("in_wmod"), 16)

            head_loads(0, True)
            sp.dma_start(w_rt[:, :, 0:NG], w_rg[0].rearrange("(k p) n -> p k n", p=P)).then_inc(S("rt_in"), 16)
            sp.dma_start(w_rt[:, :, NG:], w_re[0].rearrange("(k p) n -> p k n", p=P)).then_inc(S("rt_in"), 16)
            sp.dma_start(b_rt[:, 0:NG], b_rg.to_broadcast([P, NG])).then_inc(S("rt_in"), 16)
            sp.dma_start(b_rt[:, NG:], b_re.to_broadcast([P, NE])).then_inc(S("rt_in"), 16)
            with sp.Fori(1, HEADS) as h:
                head_loads(h, False)

            def proj_loads(m, b, first):
                if first:
                    sp.wait_ge(S("ff_mm"), this(HEADS - 1))
                else:
                    sp.wait_ge(S(f"proj_mm{b}"), (m - b) // 2 if isinstance(m, int) else m)
                mm = m if isinstance(m, int) else 2 * m + b
                sp.dma_start(wp[b][0], wpa_v[:, :, bass.ds(mm * P, P)]).then_inc(S(f"wp_in{b}"), 16)
                sp.dma_start(wp[b][1], wpb_v[:, :, bass.ds(mm * P, P)]).then_inc(S(f"wp_in{b}"), 16)

            for b in range(2):
                proj_loads(b, b, True)
            sp.wait_ge(S("yb_out"), this(HEADS - 1))
            sp.wait_ge(S("ya_out"), this(HEADS - 1))
            for i in range(2):
                sp.dma_start(wo[:, 4 * i:4 * i + 4, :], wo_v[:, 4 * i:4 * i + 4, :]).then_inc(S("wo_in"), 16)
                if i == 0:
                    for b in range(2):
                        proj_loads(2 + b, b, False)
            with sp.Fori(2, KT // 2) as m:
                for b in range(2):
                    proj_loads(m, b, False)
            sp.wait_ge(S("gb_mm"), this(HEADS - 1))
            for t in range(2):
                sp.dma_start(xr[:, t, :], x_cm[32 * t:32 * t + 32]).then_inc(S("xr_in"), 16)
            sp.dma_start(fin_g, final_g[None, :].to_broadcast([P, D])).then_inc(S("xr_in"), 16)

            src = {"w1": w1_v, "w3": w3_v, "w2": w2_v}

            def load_pair(q, j, experts):
                for n, (k, b) in enumerate(KINDS):
                    u = 6 * j + n if isinstance(q, int) else len(RING)
                    if u == 5:
                        sp.wait_ge(S("proj_mm1"), KT // 2)
                    if u == 7:
                        sp.wait_ge(S("rt_mm"), 1)
                        sp.wait_ge(S("ssq_out"), 8)
                    if u >= len(RING) and b == 0:
                        if k == "w1":
                            sp.wait_ge(S("my"), this(q - 2, 1))
                        else:
                            sp.wait_ge(S("m1" if k == "w3" else "m3"), this(q - 1))
                        if k == "w1" and not isinstance(q, int):
                            sp.sem_inc(S("slot_free"), 1)
                    sp.dma_start(wslot(k, b, j), src[k][experts[b]]).then_inc(S(f"in_{k}_{j % 2}"), 16)

            for j in range(UNROLL):
                load_pair(j, j, (2 * j, 2 * j + 1))
            sp.wait_ge(S("rounds_ready"), 1)
            n_rounds = sp.value_load(rcnt_i[0:1, 0:1], min_val=1, max_val=T // SLOTS)
            with sp.Fori(1, n_rounds * (PAIRS // UNROLL)) as g:
                for j in range(UNROLL):
                    e = [sp.snap((g & (PAIRS // UNROLL - 1)) * (2 * UNROLL) + (2 * j + b)) for b in range(2)]
                    load_pair(g * UNROLL + j, j, e)
            for t in range(2):
                sp.wait_ge(S("y_out"), t + 1)
                sp.dma_start(out_cm[32 * t:32 * t + 32], xn[:, t, :]).then_inc(S("stored"), 16)
            sp.wait_ge(S("stored"), 32)

        @block.gpsimd
        def _(pool):
            for const in (ident, resets, causal[0], causal[1], before, ones):
                i = pool.memset(const[:], 1.0)
            i.then_inc(S("consts"), 1)
            pool.wait_ge(S("consts"), 1)

            def keep(v, base, pattern, per_partition, op=ALU.is_ge):
                return pool.affine_select(out=v, in_=v, compare_op=op, fill=0.0, base=base, pattern=pattern,
                                          channel_multiplier=per_partition)
            keep(ident[:], 0, [[1, P]], -1, ALU.is_equal).then_inc(S("ident_set"), 1)
            pool.memset(mean_w[:], 1.0 / P)
            pool.memset(resets[:, 0:T:CH], 0.0)
            keep(before[:], -1, [[1, P]], -1)
            blocks = [m[:].rearrange("p (a b) -> p a b", b=CH) for m in causal]
            keep(blocks[0], 0, [[CH, P // CH], [1, CH]], -1)
            keep(blocks[1], 0, [[-CH, P // CH], [-1, CH]], 1).then_inc(S("consts"), 1)
            pool.wait_ge(S("consts"), 2)
            keep(blocks[0], 0, [[-CH, P // CH], [0, CH]], 1)
            keep(blocks[1], CH - 1, [[CH, P // CH], [0, CH]], -1)
            pool.iota(slot_no[:], pattern=[[1, SLOTS]], base=0, channel_multiplier=0,
                      allow_small_or_imprecise_dtypes=True)
            pool.memset(zb[:], 0.0).then_inc(S("consts"), 1)
            for n in HEAD_SEMS + MOE_SEMS:
                pool.sem_inc(S(n), 1)
            for n in DIR_SEMS + EXP_SEMS:
                pool.sem_inc(S(n), 2)
            pool.wait_ge(S("pro_mm"), 1)
            pool.wait_ge(S("tok_T"), 8)
            for d in range(2):
                pool.memset(att[d], 0.0)
            pool.memset(vbd, 0.0)
            pool.memset(a_pad, 0.0)
            pool.memset(a_edge, 0.0)
            for d in range(2):
                pool.memset(rcx[d], 0.0)
            last_set = pool.memset(etot[:], 0.0)
            last_set.then_inc(S("zero_set"), 1)
            pool.wait_ge(S("zero_set"), 1)
            with pool.Fori(0, HEADS) as h:
                def gates(d):
                    pool.wait_ge(S("ig_out"), this(h, d))
                    pool.wait_ge(S("conv_out"), this(h))
                    pool.tensor_tensor(ig[d], ig[d], u, ALU.mult).then_inc(S("iu_out"), 1)

                def prods(d):
                    pool.wait_ge(S("ec_out"), this(h, d))
                    pool.tensor_tensor(ec[d], ec[d], kk[d][:, T:], ALU.mult).then_inc(S("kdc_out"), 1)
                    pool.wait_ge(S("exps_out"), this(h, d))
                    pool.wait_ge(S("qs_out"), this(h))
                    pool.tensor_tensor(e3[d], e3[d], qs, ALU.mult).then_inc(S("qe3_out"), 1)

                def inputs(d):
                    pool.wait_ge(S("sqrt_out"), this(h, d))
                    pool.wait_ge(S("iu_out"), this(h, d))
                    pool.tensor_tensor(tz[d], tz[d], ig[d], ALU.mult).then_inc(S("b_out"), 1)

                gates(0)
                prods(0)
                gates(1)
                prods(1)
                inputs(0)
                inputs(1)

        @block.tensor
        def _(pe):
            mm = pe.matmul
            LATE = 2

            def down_k(dst, w, rhs, first=0, end=KT):
                for k in range(first, end):
                    i = mm(dst, w(k), rhs(k), start=k == 0, stop=k == KT - 1)
                return i

            pe.wait_ge(S("ident_set"), 1)
            pe.wait_ge(S("par_in"), 16 * (len(rows) + 3))
            pe.transpose(bank[7][:, 0:P], prows[:, 0, :], ident[:])
            pe.transpose(bank[7][:, P:P + 64], prows[0:64, 1, :], ident[0:64, 0:64]).then_inc(S("par_T"), 1)
            for k in range(KT):
                if k == 0:
                    pe.wait_ge(S("xs_out"), 4)
                if k >= 2:
                    pe.wait_ge(S("tok_copy"), k - 1)
                for t in range(4):
                    i = pe.transpose(PJ[k % 2][:, P * t:P * t + P], tok[:, t, P * k:P * k + P], ident[:])
                i.then_inc(S("tok_T"), 1)
            def mod_rows(dst, w):
                for k in range(KT):
                    r = 32 * (k % 4)
                    i = mm(dst[r:r + 32, :], csil[:, k].rearrange("p s r -> p (s r)"), w[:, k, :],
                           start=k < 4, stop=k >= 4)
                return i

            def mod_sums(dst, n, rows_):
                for m in range(4):
                    i = mm(dst[:, n * m:n * m + n], rows_[:, P * m:P * m + P], quad[:, 0:n], start=True, stop=True)
                return i

            pe.wait_ge(S("csil_out"), 1)
            for i in range(5):
                if i < 4:
                    pe.wait_ge(S(f"pro_in{i}"), 16)
                    mod_rows(bank[2 + i], wpro[i]).then_inc(S("pro_rows"), 1)
                if i > 0:
                    pe.wait_ge(S("pro_part"), i)
                    ins = mod_sums(bank[6][:, 8 * i - 8:8 * i], 2, wpro[i - 1][:, 0, :])
            ins.then_inc(S("pro_mm"), 1)
            pe.wait_ge(S("h_ct_out"), 1)
            pe.wait_ge(S("edges_out"), 1)
            pe.wait_ge(S("consts"), 3)
            pe.wait_ge(S("zero_set"), 1)

            with pe.Fori(0, HEADS) as h:
                h_edge_x = lambda k: h_ct[:, k, 0:EDGE + T]
                h_x = lambda k: h_ct[:, k, EDGE:EDGE + T]
                h_all = lambda k: h_ct[:, k, EDGE:]
                W = lambda n: (lambda k: wblk[n][:, k, :])

                def loaded(n, times=1):
                    pe.wait_ge(S("in_" + n), (h + 1) * (16 * times))

                def gate_products(d):
                    if d == 0:
                        loaded("lru", 4)
                        pe.wait_ge(S("conv_out"), this(h))
                        pe.wait_ge(S("rg_out"), last(h, 1))
                        pe.wait_ge(S("ig_out"), last(h, 1))
                    else:
                        pe.wait_ge(S("rg_out"), this(h, 0))
                        pe.wait_ge(S("ig_out"), this(h, 0))
                    mm(GT[0][:, 0:TU], wlru[:, 2 * d, :], u, start=True, stop=True).then_inc(S("ra_mm"), 1)
                    mm(GT[1][:, 0:TU], wlru[:, 2 * d + 1, :], u, start=True, stop=True).then_inc(S("ix_mm"), 1)

                def decayed_keys_T(d):
                    pe.wait_ge(S("prod_k"), this(h, d))
                    pe.wait_ge(S("kdc_out"), this(h, d))
                    if d == 0:
                        pe.wait_ge(S("chain_b"), last(h, 1))
                    else:
                        pe.wait_ge(S("kdT_out"), this(h, 0))
                    for t in range(2):
                        pe.transpose(TB[:, P * t:P * t + P], e4[d][:, P * t:P * t + P], ident[:])
                    for t in range(2):
                        i = pe.transpose(TB[:, P * (2 + t):P * (3 + t)], ec[d][:, P * t:P * t + P], ident[:])
                    i.then_inc(S("kdt_mm"), 1)

                def attention(d):
                    pe.wait_ge(S("prod_q"), this(h, d))
                    if d == 0:
                        pe.wait_ge(S("orms_out"), last(h))
                    else:
                        pe.wait_ge(S("att_out"), this(h, 0))
                    for t in range(2):
                        s = slice(P * t, P * t + P)
                        mm(AB[:, s], e2[d][:, s], e1[d][:, s], start=True, stop=True)
                    pe.wait_ge(S("kdT_out"), this(h, d))
                    pe.wait_ge(S("v_out"), this(h))
                    for t in range(2):
                        i = mm(AB[:, 256:384], kdT[d][:, 2 + t, :], vv[:, 2 + t, :], start=t == 0, stop=t == 1)
                    i.then_inc(S("att_mm"), 1)

                def chunk_states(d):
                    ta, tb = (0, 1) if d == 0 else (1, 0)
                    if d == 0:
                        pe.wait_ge(S("chain_a"), last(h, 1))
                    else:
                        pe.wait_ge(S("chain_a"), this(h, 0))
                    mm(KB[:], kdT[d][:, ta, :], vbd[:, ta].rearrange("p a b -> p (a b)"),
                       start=True, stop=True).then_inc(S("kv_a"), 1)
                    if d == 0:
                        pe.wait_ge(S("kdT_out"), this(h, 1))
                    else:
                        pe.wait_ge(S("chain_b"), this(h, 0))
                    s = slice(0, 384) if d == 0 else slice(128, 512)
                    mm(TB[:, s], kdT[d][:, tb, :], vbd[:, tb].rearrange("p a b -> p (a b)")[:, s],
                       start=True, stop=True).then_inc(S("kv_b"), 1)

                def outputs(d):
                    if d == 0:
                        pe.wait_ge(S("mod_out"), this(h))
                    pe.wait_ge(S("att_out"), this(h, d))
                    for t in range(2):
                        s = slice(P * t, P * t + P)
                        mm(OB[:, s], vv[:, t, :], att[d][:, t, :], start=d == 0 and t == 0, stop=False,
                           skip_group_check=True)
                    pe.wait_ge(S("qe3_out"), this(h, d))
                    pe.wait_ge(S("chain_a"), this(h, d))
                    pe.wait_ge(S("chain_b"), this(h, d))
                    for j in range(NCH):
                        cj = j if d == 0 else NCH - 1 - j
                        s = slice(CH * cj, CH * cj + CH)
                        i = mm(OB[:, s], st[d][:, j, :], e3[d][:, s], start=False, stop=d == 1,
                               skip_group_check=True)
                    i.then_inc(S("inter_mm"), 1)

                loaded("a")
                pe.wait_ge(S("ig_out"), last(h, 1))
                down_k(GT[1][:, 0:EDGE + T], W("a"), h_edge_x).then_inc(S("a_mm"), 1)
                loaded("q", 2)
                pe.wait_ge(S("ga_out"), last(h))
                down_k(PJ[1][:, 0:T], W("q"), h_x)
                down_k(PJ[1][:, T:], W("ay"), h_x).then_inc(S("q_mm"), 1)
                loaded("ff")
                pe.wait_ge(S("gb_out"), last(h))
                down_k(PJ[0][:], W("ff"), h_all).then_inc(S("ff_mm"), 1)
                gate_products(0)
                loaded("fb")
                pe.wait_ge(S("ay_out"), this(h))
                pe.wait_ge(S("qs_out"), this(h))
                down_k(PJ[1][:], W("fb"), h_all).then_inc(S("fb_mm"), 1)
                gate_products(1)
                loaded("wmod")
                pe.wait_ge(S("osq_out"), last(h))
                pe.wait_ge(S("on_out"), last(h))
                mod_rows(OB, wmod).then_inc(S("modr_mm"), 1)
                loaded("v")
                pe.wait_ge(S("ff_out"), this(h))
                for t in range(4):
                    i = down_k(PJ[0][:, P * t:P * t + P], lambda k: h_ct[:, k, EDGE + P * t:EDGE + P * t + P], W("v"))
                i.then_inc(S("v_mm"), 1)
                decayed_keys_T(0)
                loaded("og", 2)
                pe.wait_ge(S("fb_out"), this(h))
                down_k(PJ[1][:, 0:T], W("og"), h_x)
                decayed_keys_T(1)
                down_k(PJ[1][:, T:], W("ga"), h_x, end=KT - LATE)
                attention(0)
                chunk_states(0)
                down_k(PJ[1][:, T:], W("ga"), h_x, first=KT - LATE).then_inc(S("og_mm"), 1)
                pe.wait_ge(S("modr_out"), this(h))
                mod_sums(OB, 1, wmod[:, 0, :]).then_inc(S("mod_mm"), 1)
                attention(1)
                chunk_states(1)
                outputs(0)
                loaded("gb")
                down_k(PJ[0][:, 0:T], W("gb"), h_x, end=KT - LATE)
                outputs(1)
                down_k(PJ[0][:, 0:T], W("gb"), h_x, first=KT - LATE).then_inc(S("gb_mm"), 1)
                pe.wait_ge(S("osq_out"), this(h))
                pe.wait_ge(S("att_out"), this(h, 1))
                mm(AB[:, 0:T], mean_w[:], osq, start=True, stop=True).then_inc(S("rms_mm"), 1)

            pe.wait_ge(S("ya_out"), this(HEADS - 1))
            pe.wait_ge(S("ga_out"), this(HEADS - 1))
            pe.wait_ge(S("mod_out"), this(HEADS - 1))

            def project(i, b, first):
                pe.wait_ge(S(f"wp_in{b}"), 32 * (i + 1))
                if not first:
                    pe.wait_ge(S(f"merged_out{b}"), i)
                if first and b == 1:
                    pe.wait_ge(S("gb_out"), this(HEADS - 1))
                down_k(PJ[1 - b][:, 0:T], lambda k: wp[b][0][:, k, :], lambda k: ya_g[:, k, :])
                if first:
                    pe.wait_ge(S("yb_out"), this(HEADS - 1))
                down_k(PJ[1 - b][:, T:], lambda k: wp[b][1][:, k, :], lambda k: yb_g[:, k, :]).then_inc(S(f"proj_mm{b}"), 1)
                if first:
                    gate_rows(b)
            def gate_rows(v):
                pe.wait_ge(S("diag_out"), v + 1)
                if v == 0:
                    pe.wait_ge(S("orms_out"), this(HEADS - 1))
                    pe.wait_ge(S("on_out"), this(HEADS - 1))
                else:
                    pe.wait_ge(S("gate_rows"), 1)
                for hf in range(2):
                    i = mm(bank[6 + hf][:], ones[:, 0:P],
                           diag[:, 4 * hf:4 * hf + 4, :].rearrange("p a b -> p (a b)"), start=True, stop=True)
                i.then_inc(S("gate_mm"), 1)

            for b in range(2):
                project(0, b, True)
            with pe.Fori(1, KT // 2) as i:
                for b in range(2):
                    project(i, b, False)
            pe.wait_ge(S("wo_in"), 32)
            pe.wait_ge(S("gate_rows"), 2)

            def w_out_half(t, hf):
                for k in range(KT):
                    if (t, hf) == (0, 0) and k >= KT - 2:
                        pe.wait_ge(S(f"merged_out{k % 2}"), KT // 2)
                    i = mm(bank[(4, 0)[t] + hf][:], merged[:, k, P * t:P * t + P],
                           wo[:, k, 512 * hf:512 * hf + 512], start=k == 0, stop=k == KT - 1)
                i.then_inc(S("wo_mm"), 1)

            def turn_x1(t):
                for hf in range(2):
                    pe.wait_ge(S("x1_out"), 2 * t + hf + 1)
                    if (t, hf) == (1, 0):
                        pe.wait_ge(S("rt_prep"), 3)
                    for k in range(4):
                        i = pe.transpose(bank[(6, 2)[t] + hf][:, P * k:P * k + P],
                                         x1[:, t, 512 * hf + P * k:512 * hf + P * k + P], ident[:])
                    i.then_inc(S("x1_T"), 1)

            def logits(t):
                return down_k(bank[5][:, 64 * t:64 * t + NG + NE], lambda k: x1T[:, k, P * t:P * t + P],
                              lambda k: w_rt[:, k, :])

            w_out_half(0, 0)
            w_out_half(0, 1)
            pe.wait_ge(S("rt_prep"), 1)
            pe.wait_ge(S("rg_out"), this(HEADS - 1, 1))
            down_k(bank[2][:, 0:NG + NE], lambda k: ones[:, 0:P], lambda k: w_sh[:, k, :]).then_inc(S("gate_mm"), 1)
            w_out_half(1, 0)
            turn_x1(0)
            w_out_half(1, 1)
            pe.wait_ge(S("rt_prep"), 2)
            pe.wait_ge(S("x1T_out"), 2)
            logits(0)
            turn_x1(1)
            pe.wait_ge(S("x1T_out"), 3)
            pe.wait_ge(S("x1T_out2"), 1)
            logits(1).then_inc(S("rt_mm"), 1)
            pe.wait_ge(S("sel_out"), 1)
            sel = rt[:, 8]
            mm(bank[0][:, 0:NE], before[:], sel[:, 0, :], start=True, stop=True)
            mm(bank[0][:, NE:2 * NE], ones[:, 0:P], sel[:, 0, :], start=True, stop=False)
            mm(bank[0][:, NE:2 * NE], before[:], sel[:, 1, :], start=False, stop=True).then_inc(S("rank_mm"), 1)
            mm(bank[1][:, 0:NE], ones[:, 0:P], sel[:, 0, :], start=True, stop=False)
            mm(bank[1][:, 0:NE], ones[:, 0:P], sel[:, 1, :], start=False, stop=True).then_inc(S("rank_mm"), 1)

            def gather(half):
                for k in range(4):
                    kt = 4 * half + k
                    for t in range(2):
                        i = mm((GX if half else UX)[:, P * k:P * k + P], xn[:, t, P * kt:P * kt + P],
                               hot[:, t].rearrange("p e s -> p (e s)"), start=t == 0, stop=t == 1)
                i.then_inc(S("mx"), 1)

            def up(acc, kind, j):
                for k in range(KT):
                    for b in range(2):
                        i = mm(acc[SLOTS * b:SLOTS * b + SLOTS, :], xg[:, k, SLOTS * b:SLOTS * b + SLOTS],
                               wslot(kind, b, j)[:, k, :], start=k == 0, stop=k == KT - 1)
                return i

            def down(acc, hf, j):
                for f in range(F // P):
                    for b in range(2):
                        i = mm(acc[SLOTS * b:SLOTS * b + SLOTS, :], gT[:, f, SLOTS * b:SLOTS * b + SLOTS],
                               wslot("w2", b, j)[:, f, 512 * hf:512 * hf + 512], start=f == 0, stop=f == F // P - 1)
                i.then_inc(S("my"), 1)

            def combine(q):
                pe.wait_ge(S("ctc"), this(q))
                for hf in range(2):
                    pe.wait_ge(S("ysc"), this(q, hf))
                    for t in range(2):
                        i = mm(ACC[t][hf][:], ct[:, t, :], ys[:, hf, :], start=False, stop=False,
                               skip_group_check=True)
                        if hf:
                            i.then_inc(S("mc"), 1)

            def pair(j, q, loads):
                pe.wait_ge(S("xgc"), this(q, 1))
                pe.wait_ge(S(f"in_w1_{j % 2}"), loads * 32)
                up(UX, "w1", j).then_inc(S("m1"), 1)
                combine(q - 1)
                pe.wait_ge(S(f"in_w3_{j % 2}"), loads * 32)
                up(VY, "w3", j).then_inc(S("m3"), 1)
                pe.wait_ge(S("hw"), this(q))
                for t in range(2):
                    i = pe.transpose(CY[:, P * t:P * t + P], hotw[:, t].rearrange("p e s -> p (e s)"), ident[:])
                i.then_inc(S("mtc"), 1)
                pe.wait_ge(S("gm"), this(q))
                for f in range(F // P):
                    i = pe.transpose(GX[:, P * f:P * f + P], gm[:, P * f:P * f + P], ident[:])
                i.then_inc(S("mtg"), 1)
                pe.wait_ge(S("hotc"), q + 3)
                gather(0)
                pe.wait_ge(S("gtc"), this(q))
                gather(1)
                pe.wait_ge(S(f"in_w2_{j % 2}"), loads * 32)
                down(VY, 0, j)
                pe.wait_ge(S("ctc"), this(q))
                down(CY, 1, j)

            pe.wait_ge(S("hotc"), 2)
            pe.wait_ge(S("xn_out"), 2)
            for half in range(2):
                gather(half)
            pe.wait_ge(S("rounds_ready"), 1)
            n_rounds = pe.value_load(rcnt_i[0:1, 0:1], min_val=1, max_val=T // SLOTS)
            with pe.Fori(0, n_rounds) as r:
                pe.wait_ge(S("acc_read"), r + 1)
                for t in range(2):
                    for hf in range(2):
                        mm(ACC[t][hf][:], zb[:, 0:P], zb[:], start=True, stop=False, skip_group_check=True)
                with pe.Fori(0, PAIRS // UNROLL) as g:
                    for j in range(UNROLL):
                        pair(j, r * PAIRS + g * UNROLL + j, r * (PAIRS // 2) + g * (UNROLL // 2) + (j // 2 + 1))
                q = r * PAIRS + PAIRS - 1
                combine(q)

        @block.scalar
        def _(act):
            A = act.activation
            for t in range(4):
                act.wait_ge(S("x_in" if t < 2 else "ctx_in"), 32)
                A(junk[:, t, :], tok[:, t, :], ACT.Square, accum_out=ssq[:, t:t + 1]).then_inc(S("ssq_out"), 1)
            act.wait_ge(S("ms_out"), 1)
            A(rstd[:], rstd[:], ACT.Sqrt).then_inc(S("rms_out"), 1)
            act.wait_ge(S("par_copy"), 1)
            for k in range(2):
                i = A(csil[:, :, k, :], par2[:, 48 + 8 * k:56 + 8 * k].unsqueeze(2).to_broadcast([P, KT, 16]), ACT.Silu)
            i.then_inc(S("csil_out"), 1)
            act.wait_ge(S("sp0"), 1)
            A(spt[:, 0, :], spt[:, 0, :], ACT.Exp, scale=-1.0).then_inc(S("sp1"), 1)
            A(par[:, V_LBV, :], spt[:, 3, 0:8], ACT.Sigmoid).then_inc(S("sp1"), 1)
            for k in range(KT):
                act.wait_ge(S("tok_T"), k + 1)
                A(h_ct[:, k, EDGE:], PJ[k % 2][:], ACT.Copy).then_inc(S("tok_copy"), 1)
            for i in range(4):
                act.wait_ge(S("pro_rows"), i + 1)
                A(wpro[i][:, 0, :], bank[2 + i][:], ACT.Copy).then_inc(S("pro_part"), 1)
            act.wait_ge(S("aff1_out"), 1)
            act.wait_ge(S("tok_copy"), KT)
            for k in range(3):
                for s in range(2):
                    i = A(h_ct[:, k, EDGE + T * s:EDGE + T * s + T], h_ct[:, k, EDGE + T * s:EDGE + T * s + T], ACT.Identity,
                          scale=aff1[:, s, k:k + 1], bias=modA[:, k, s:s + 1])
            i.then_inc(S("h_ct_out"), 1)
            act.wait_ge(S("zero_set"), 1)

            with act.Fori(0, HEADS) as h:
                def col(v):
                    return hp[:, v:v + 1]

                act.wait_ge(S("a_mm"), this(h))
                act.wait_ge(S("conv_out"), last(h))
                A(a_pad[:, 2:2 + T].rearrange("p (r c) -> p r c", r=ROWS),
                  GT[1][:, EDGE:EDGE + T].rearrange("p (c r) -> p r c", r=ROWS), ACT.Copy)
                A(a_edge[:, 2:2 + EDGE], GT[1][:, 0:EDGE], ACT.Copy).then_inc(S("a_out"), 1)
                act.wait_ge(S("q_mm"), this(h))
                act.wait_ge(S("qs_out"), last(h))
                A(sq, PJ[1][:, 0:T], ACT.Sigmoid).then_inc(S("sq_out"), 1)
                act.wait_ge(S("ya_out"), last(h))
                A(gl, PJ[1][:, T:], ACT.Gelu_apprx_tanh).then_inc(S("ay_out"), 1)

                def forget(d, bank_, mm_sem, out_sem):
                    act.wait_ge(S(mm_sem), this(h))
                    act.wait_ge(S("ln_out"), last(h, d))
                    act.wait_ge(S("g_out"), last(h, d))
                    A(gg[d], bank_[:], ACT.Sigmoid).then_inc(S(out_sem), 1)

                def gates(d):
                    act.wait_ge(S("ra_mm"), this(h, d))
                    act.wait_ge(S("hp_out"), this(h))
                    act.wait_ge(S("aa_out"), last(h, d))
                    A(rg[d], GT[0][:, 0:TU], ACT.Sigmoid, bias=col(V_BA + d)).then_inc(S("rg_out"), 1)
                    act.wait_ge(S("ix_mm"), this(h, d))
                    act.wait_ge(S("b_out"), last(h, d))
                    A(ig[d], GT[1][:, 0:TU], ACT.Sigmoid, bias=col(V_BX + d)).then_inc(S("ig_out"), 1)
                    act.wait_ge(S("scan_out"), last(h, d))
                    act.wait_ge(S("rg_out"), this(h, d))
                    A(tz[d], rg[d], ACT.Tanh, scale=col(V_PSP + d)).then_inc(S("tz_out"), 1)

                def logs(d):
                    act.wait_ge(S("g_out"), this(h, d))
                    act.wait_ge(S("lc_out"), last(h, d))
                    A(lf[d], gg[d], ACT.Ln).then_inc(S("ln_out"), 1)

                def exps(d):
                    act.wait_ge(S("rg_out"), this(h, d))
                    act.wait_ge(S("scan_out"), last(h, d))
                    A(aa[d], rg[d], ACT.Exp, scale=col(V_NSP + d)).then_inc(S("aa_out"), 1)
                    act.wait_ge(S("lc_out"), this(h, d))
                    act.wait_ge(S("kdt_mm"), last(h, d))
                    A(ec[d], rcx[d], ACT.Exp).then_inc(S("ec_out"), 1)
                    A(e4[d], d4[d], ACT.Exp).then_inc(S("e4_out"), 1)
                    act.wait_ge(S("att_mm"), last(h, d))
                    A(e1[d], dm[d], ACT.Exp)
                    A(e2[d], dm[d], ACT.Exp, scale=-1.0).then_inc(S("e1_out"), 1)
                    act.wait_ge(S("inter_mm"), last(h, d))
                    act.wait_ge(S("chain_b"), last(h, d))
                    A(etot[:, d, :], lcx[d][:, (CH - 1 if d == 0 else 0):T:CH], ACT.Exp)
                    A(e3[d], lcx[d], ACT.Exp).then_inc(S("exps_out"), 1)

                forget(0, PJ[0], "ff_mm", "ff_out")
                gates(0)
                logs(0)
                exps(0)
                forget(1, PJ[1], "fb_mm", "fb_out")
                gates(1)
                logs(1)
                exps(1)
                act.wait_ge(S("modr_mm"), this(h))
                A(wmod[:, 0, :], OB[:], ACT.Copy).then_inc(S("modr_out"), 1)
                act.wait_ge(S("v_mm"), this(h))
                act.wait_ge(S("zero_set"), 1)
                act.wait_ge(S("inter_mm"), last(h, 1))
                for j in range(P // CH):
                    s = slice(CH * j, CH * j + CH)
                    A(vbd[s, :, j, :], PJ[0][s, 0:2 * P].rearrange("p (t n) -> p t n", t=2), ACT.Copy)
                A(vv.rearrange("p a b -> p (a b)"), PJ[0][:], ACT.Copy).then_inc(S("v_out"), 1)

                def keys_out(d):
                    act.wait_ge(S("kdt_mm"), this(h, d))
                    act.wait_ge(S("kv_b"), last(h, d))
                    A(kdT[d].rearrange("p a b -> p (a b)"), TB[:], ACT.Copy).then_inc(S("kdT_out"), 1)

                keys_out(0)
                keys_out(1)
                for d in range(2):
                    act.wait_ge(S("w_out"), this(h, d))
                    A(tz[d], tz[d], ACT.Sqrt, scale=2.0).then_inc(S("sqrt_out"), 1)
                act.wait_ge(S("og_mm"), this(h))
                act.wait_ge(S("yb_out"), last(h))
                A(sog, PJ[1][:, 0:T], ACT.Silu).then_inc(S("og_out"), 1)
                A(s_ga[:, h, :], PJ[1][:, T:], ACT.Sigmoid).then_inc(S("ga_out"), 1)
                act.wait_ge(S("inter_mm"), this(h, 1))
                act.wait_ge(S("rms_mm"), last(h))
                A(osq, OB[:, 0:T], ACT.Square).then_inc(S("osq_out"), 1)
                act.wait_ge(S("rms_mm"), this(h))
                act.wait_ge(S("on_out"), last(h))
                A(orr, AB[:, 0:T], ACT.Sqrt, bias=eps_t[:, 0:1]).then_inc(S("orms_out"), 1)
                act.wait_ge(S("gb_mm"), this(h))
                A(s_gb[:, h, :], PJ[0][:, 0:T], ACT.Sigmoid).then_inc(S("gb_out"), 1)

            def square(t, hf):
                act.wait_ge(S("x1_out"), 2 * t + hf + 1)
                s = slice(512 * hf, 512 * hf + 512)
                A(junk2[:, t, s], x1[:, t, s], ACT.Square, accum_out=ssq[:, 2 * hf + t:2 * hf + t + 1]).then_inc(S("ssq_out"), 1)

            def x1T_copy(t, hf):
                act.wait_ge(S("x1_T"), 2 * t + hf + 1)
                A(x1T[:, 4 * hf:4 * hf + 4, P * t:P * t + P],
                  bank[(6, 2)[t] + hf][:].rearrange("p (k n) -> p k n", k=4), ACT.Copy).then_inc(S("x1T_out"), 1)

            square(0, 0)
            square(0, 1)
            x1T_copy(0, 0)
            x1T_copy(0, 1)
            square(1, 0)
            x1T_copy(1, 0)
            square(1, 1)
            act.wait_ge(S("ms_out"), 2)
            A(rstd[:, 0:2], rstd[:, 0:2], ACT.Sqrt).then_inc(S("rms_out"), 1)
            act.wait_ge(S("rstd_out"), 1)
            act.wait_ge(S("wo_mm"), 4)
            for t in range(2):
                A(xn[:, t, :], x1[:, t, :], ACT.Identity, scale=rstd[:, t:t + 1]).then_inc(S("xn_out"), 1)
            for n in range(2):
                act.wait_ge(S("rt_sub"), n + 1)
                src_ = rt_g[:, :, 1, :] if n == 0 else rcol[:, 6, :]
                A(src_, src_, ACT.Exp).then_inc(S("rt_exp"), 1)

            def xg_out(half, g):
                act.wait_ge(S("mx"), this(g, half))
                for k in range(4):
                    kt = 4 * half + k
                    i = A(xg[:, kt, :], (GX if half else UX)[:, P * k:P * k + P], ACT.Identity,
                          scale=aff2[:, kt:kt + 1], bias=modB[:, 8 + kt:9 + kt])
                i.then_inc(S("xgc"), 1)

            for half in range(2):
                xg_out(half, 0)
            act.wait_ge(S("rounds_ready"), 1)
            n_rounds = act.value_load(rcnt_i[0:1, 0:1], min_val=1, max_val=T // SLOTS)
            with act.Fori(0, n_rounds) as r:
                with act.Fori(0, PAIRS) as p:
                    q = r * PAIRS + p
                    act.wait_ge(S("m1"), this(q))
                    act.wait_ge(S("gm"), last(q))
                    A(sh, UX[:], ACT.Silu).then_inc(S("sh"), 1)
                    act.wait_ge(S("mtc"), this(q))
                    act.wait_ge(S("mc"), this(r * (PAIRS + 1) + p, 1))
                    A(ct.rearrange("p a b -> p (a b)"), CY[:, 0:2 * P], ACT.Copy).then_inc(S("ctc"), 1)
                    act.wait_ge(S("mtg"), this(q))
                    act.wait_ge(S("my"), last(q, 1))
                    A(gT.rearrange("p a b -> p (a b)"), GX[:], ACT.Copy).then_inc(S("gtc"), 1)
                    act.wait_ge(S("m3"), this(q))
                    xg_out(0, q + 1)
                    xg_out(1, q + 1)

            act.wait_ge(S("x1_out"), 5)
            for t in range(2):
                A(xn[:, t, :], x1[:, t, :], ACT.Square, accum_out=ssq[:, t:t + 1]).then_inc(S("ssq_out"), 1)
            act.wait_ge(S("ms_out"), 3)
            A(rstd[:, 0:2], rstd[:, 0:2], ACT.Sqrt).then_inc(S("rms_out"), 1)

        @block.vector
        def _(dve):
            cp, tt, ts, stt = dve.tensor_copy, dve.tensor_tensor, dve.tensor_scalar, dve.scalar_tensor_tensor

            class Chain:

                def __init__(self, name, base=0, per=None):
                    self.sem, self.base, self.n, self.per = S(name), base, 0, per

                def __call__(self, ins):
                    self.n += 1
                    ins.then_inc(self.sem, 1)
                    dve.wait_ge(self.sem, self.base + self.n)

            serial = Chain("serial_step")
            link = serial
            link(dve.memset(eps_t[:], EPS))
            dve.wait_ge(S("ident_set"), 1)
            for n in range(2):
                dve.tensor_reduce(quad[:, n:n + 1], ident[:, 16 * n:P:32], AX.X, ALU.add)
            dve.wait_ge(S("par_T"), 1)
            cp(par[:, 0:16, :].rearrange("p a b -> p (a b)"), bank[7][:, 0:P])
            cp(par2[:], bank[7][:, P:P + 64]).then_inc(S("par_copy"), 1)
            dve.wait_ge(S("par_copy"), 1)
            lam = par[:, V_LAM:V_LAM + 2, :].rearrange("p a b -> p (a b)")
            link(ts(spt[:, 1, :], lam, -1.0, None, ALU.mult))
            tt(spt[:, 3, 0:8], par[:, V_LB, :], par[:, V_LB + 1, :], ALU.subtract)
            tt(spt[:, 0, :], spt[:, 1, :], lam, ALU.max).then_inc(S("sp0"), 1)
            dve.wait_ge(S("ssq_out"), 4)
            ts(rstd[:], ssq[:], 1.0 / D, EPS, ALU.mult, ALU.add).then_inc(S("ms_out"), 1)
            dve.wait_ge(S("rms_out"), 1)
            link(dve.reciprocal(rstd[:], rstd[:]))
            for t in range(4):
                ts(tok[:, t, :], tok[:, t, :], rstd[:, t:t + 1], None, ALU.mult).then_inc(S("xs_out"), 1)
            dve.wait_ge(S("sp1"), 1)
            e_, s_, s2 = spt[:, 0, :], spt[:, 2, :], spt[:, 4, :]
            link(ts(s_, e_, 2.0, None, ALU.add))
            link(dve.reciprocal(s_, s_))
            link(tt(s_, s_, e_, ALU.mult))
            link(tt(s2, s_, s_, ALU.mult))
            acc = spt[:, 0, :]
            link(ts(acc, s2, 1.0 / 17, None, ALU.mult))
            for n in range(15, 1, -2):
                link(stt(acc, acc, 1.0 / n, s2, ALU.add, ALU.mult))
            link(stt(acc, acc, 1.0, s_, ALU.add, ALU.mult))
            link(ts(acc, acc, 2.0, None, ALU.mult))
            link(stt(acc, spt[:, 1, :], 0.0, acc, ALU.max, ALU.add))
            sp2 = lambda v: par[:, v:v + 2, :].rearrange("p a b -> p (a b)")
            ts(sp2(V_PSP), acc, 8.0, None, ALU.mult)
            ts(sp2(V_NSP), acc, -8.0, None, ALU.mult)
            dve.wait_ge(S("sp1"), 2)
            ts(par[:, V_OML, :], par[:, V_LBV, :], -1.0, 1.0, ALU.mult, ALU.add).then_inc(S("par_done"), 1)
            dve.wait_ge(S("pro_mm"), 1)
            link(tt(modA[:], bank[6][:, 0:32].rearrange("p (m s) -> p m s", s=2),
               par2[:, 0:16].unsqueeze(2).to_broadcast([P, 16, 2]), ALU.add))
            link(ts(aff1[:], modA[:, 8:16, :].rearrange("p m s -> p s m"), 1.0, None, ALU.add))
            tt(aff1[:], aff1[:], par[:, V_N1, :].unsqueeze(1).to_broadcast([P, 2, KT]), ALU.mult).then_inc(S("aff1_out"), 1)
            dve.wait_ge(S("aff1_out"), 1)
            dve.wait_ge(S("tok_copy"), KT)
            for k in range(3, KT):
                for s in range(2):
                    i = ts(h_ct[:, k, EDGE + T * s:EDGE + T * s + T], h_ct[:, k, EDGE + T * s:EDGE + T * s + T], aff1[:, s, k:k + 1],
                           modA[:, k, s:s + 1], ALU.mult, ALU.add)
            link(i)
            dve.wait_ge(S("h_ct_out"), 1)
            cp(h_ct[:, :, 0:3], h_ct[:, :, EDGE + T:EDGE + T + 3])
            cp(h_ct[:, :, 3:EDGE], h_ct[:, :, EDGE + 2 * T - 3:]).then_inc(S("edges_out"), 1)
            dve.wait_ge(S("par_done"), 1)
            dve.wait_ge(S("zero_set"), 1)

            N_STEP = 13
            with dve.Fori(0, HEADS) as h:
                link = Chain("head_step", h * N_STEP)

                def col(v):
                    return hp[:, v:v + 1]

                dve.wait_ge(S("aa_out"), last(h, 1))
                dve.wait_ge(S("yb_out"), last(h))
                cp(hp[:], par[:, :, h]).then_inc(S("hp_out"), 1)
                dve.wait_ge(S("hp_out"), this(h))
                dve.wait_ge(S("a_out"), this(h))
                dve.wait_ge(S("ix_mm"), last(h, 1))
                dve.wait_ge(S("iu_out"), last(h, 1))
                parts = [(u[:, 0:T], lambda k: a_pad[:, k:k + T]), (u[:, T:], lambda k: a_edge[:, k:k + 6:5])]
                for n, k in enumerate((2, 0, 1, 3)):
                    for dst, window in parts:
                        if n == 0:
                            i = ts(dst, window(k), col(V_CW + k), col(V_CB), ALU.mult, ALU.add)
                        else:
                            i = stt(dst, window(k), col(V_CW + k), dst, ALU.mult, ALU.add)
                    if n < 3:
                        link(i)
                i.then_inc(S("conv_out"), 1)
                dve.wait_ge(S("sq_out"), this(h))
                dve.wait_ge(S("ay_out"), this(h))
                dve.wait_ge(S("prod_q"), last(h, 1))
                dve.wait_ge(S("qe3_out"), last(h, 1))
                tt(qs, PJ[1][:, 0:T], sq, ALU.mult).then_inc(S("qs_out"), 1)

                def forget(d):
                    dve.wait_ge(S(("ff_out", "fb_out")[d]), this(h))
                    dve.wait_ge(S("prod_q"), last(h, d))
                    dve.wait_ge(S("kdc_out"), last(h, d))
                    link(ts(gg[d], gg[d], col(V_OML), col(V_LBV), ALU.mult, ALU.add))
                    ts(kk[d], gg[d], -1.0, 1.0, ALU.mult, ALU.add).then_inc(S("g_out"), 1)

                def logs(d):
                    dve.wait_ge(S("ln_out"), this(h, d))
                    dve.wait_ge(S("exps_out"), last(h, d))
                    if d == 0:
                        link(dve.tensor_tensor_scan(lcx[d], resets[:], lf[d][:, 0:T], 0.0, ALU.mult, ALU.add))
                        dve.tensor_tensor_scan(rcx[d][:, T - 2::-1], ones[:, 0:T - 1], lf[d][:, 2 * T - 1:T:-1],
                                               0.0, ALU.mult, ALU.add)
                    else:
                        link(dve.tensor_tensor_scan(lcx[d][:, T - 1::-1], resets[:], lf[d][:, T - 1::-1], 0.0,
                                                    ALU.mult, ALU.add))
                        dve.tensor_tensor_scan(rcx[d][:, 1:T], ones[:, 0:T - 1], lf[d][:, T:2 * T - 1],
                                               0.0, ALU.mult, ALU.add)
                    lc = lcx[d].rearrange("p (c s) -> p c s", s=CH)
                    mid, tot = (MID, CH - 1) if d == 0 else (CH - 1 - MID, 0)
                    tt(dm[d].rearrange("p (c s) -> p c s", s=CH), lc,
                       lc[:, :, mid:mid + 1].to_broadcast([P, NCH, CH]), ALU.subtract)
                    tt(d4[d].rearrange("p (c s) -> p c s", s=CH),
                       lc[:, :, tot:tot + 1].to_broadcast([P, NCH, CH]), lc, ALU.subtract).then_inc(S("lc_out"), 1)

                def ratios(d):
                    dve.wait_ge(S("tz_out"), this(h, d))
                    link(ts(rc[d], tz[d], 1.0, None, ALU.add))
                    link(dve.reciprocal(rc[d], rc[d]))
                    tt(tz[d], tz[d], rc[d], ALU.mult).then_inc(S("w_out"), 1)

                def prods(d):
                    dve.wait_ge(S("e4_out"), this(h, d))
                    tt(e4[d], e4[d], kk[d][:, 0:T], ALU.mult).then_inc(S("prod_k"), 1)
                    dve.wait_ge(S("e1_out"), this(h, d))
                    dve.wait_ge(S("qs_out"), this(h))
                    tt(e2[d], e2[d], kk[d][:, 0:T], ALU.mult)
                    tt(e1[d], e1[d], qs, ALU.mult).then_inc(S("prod_q"), 1)

                def scans(d):
                    dve.wait_ge(S("b_out"), this(h, d))
                    dve.wait_ge(S("aa_out"), this(h, d))
                    dve.wait_ge(S("ya_out"), last(h))
                    seq = slice(0, T) if d == 0 else slice(T - 1, None, -1)
                    dve.tensor_tensor_scan(hs[d][:, seq], aa[d][:, seq], tz[d][:, seq], tz[d][:, T + d:T + d + 1],
                                           ALU.mult, ALU.add).then_inc(S("scan_out"), 1)

                def states(d):
                    dve.wait_ge(S("zero_set"), 1)
                    dve.wait_ge(S("att_mm"), this(h, d))
                    dve.wait_ge(S("inter_mm"), last(h, d))
                    dve.wait_ge(S("exps_out"), this(h, d))
                    dve.copy_predicated(att[d], causal[d][:].bitcast(u32).unsqueeze(1).to_broadcast([P, 2, P]),
                                        AB[:, 0:256].rearrange("p (a b) -> p a b", a=2))
                    cp(st[d][:, 0, :], AB[:, 256:384]).then_inc(S("att_out"), 1)
                    dve.wait_ge(S("att_out"), this(h, d))
                    step = Chain(f"state_step{d}", h * (NCH - 3))
                    for j in range(NCH - 1):
                        cj = j if d == 0 else NCH - 1 - j
                        if j == 0:
                            dve.wait_ge(S("kv_a"), this(h, d))
                        if j == 4:
                            dve.wait_ge(S("kv_b"), this(h, d))
                        kv = (KB if j < 4 else TB)[:, P * (cj % 4):P * (cj % 4) + P]
                        i = stt(st[d][:, j + 1, :], st[d][:, j, :], etot[:, d, cj:cj + 1], kv, ALU.mult, ALU.add)
                        if j == 3:
                            i.then_inc(S("chain_a"), 1)
                            dve.wait_ge(S("chain_a"), this(h, d))
                        elif j == NCH - 2:
                            i.then_inc(S("chain_b"), 1)
                        else:
                            step(i)
                    assert step.n == NCH - 3

                forget(0)
                logs(0)
                ratios(0)
                prods(0)
                forget(1)
                logs(1)
                ratios(1)
                prods(1)
                scans(0)
                scans(1)
                dve.wait_ge(S("scan_out"), this(h, 0))
                dve.wait_ge(S("scan_out"), this(h, 1))
                link(tt(hsum, hs[0][:, 0:T], hs[1][:, 0:T], ALU.add))
                tt(ya_g[:, h, :].rearrange("p (c r) -> p c r", r=ROWS), hsum.rearrange("p (r c) -> p c r", r=ROWS),
                   gl.rearrange("p (c r) -> p c r", r=ROWS), ALU.mult).then_inc(S("ya_out"), 1)
                states(0)
                dve.wait_ge(S("mod_mm"), this(h))
                tt(modB[:, bass.ds(h * 4, 4)], OB[:, 0:4], par2[:, bass.ds(h * 4 + 16, 4)], ALU.add).then_inc(S("mod_out"), 1)
                states(1)
                dve.wait_ge(S("orms_out"), this(h))
                link(dve.reciprocal(orr, orr))
                dve.wait_ge(S("osq_out"), this(h))
                tt(on, OB[:, 0:T], orr, ALU.mult).then_inc(S("on_out"), 1)
                dve.wait_ge(S("on_out"), this(h))
                dve.wait_ge(S("og_out"), this(h))
                stt(yb_g[:, h, :], on, col(V_HG), sog, ALU.mult, ALU.mult).then_inc(S("yb_out"), 1)
                assert link.n == N_STEP, link.n

            def merge(i, b, first):
                m = 2 * i + b
                dve.wait_ge(S(f"proj_mm{b}"), i + 1)
                if not first:
                    dve.wait_ge(S(f"merged_out{b}"), i)
                tt(m1[b], PJ[1 - b][:, 0:T], s_ga[:, m, :], ALU.mult)
                tt(m2[b], PJ[1 - b][:, T:], s_gb[:, m, :], ALU.mult).then_inc(S("m2_out"), 1)
                dve.wait_ge(S("m2_out"), 2 * i + (b + 1))
                tt(merged[:, m, :], m1[b], m2[b], ALU.add).then_inc(S(f"merged_out{b}"), 1)
            dve.wait_ge(S("mod_out"), this(HEADS - 1))
            dve.wait_ge(S("gb_mm"), this(HEADS - 1))

            def diagonal(c0):
                tt(diag, ident[:].unsqueeze(1).to_broadcast([P, KT, P]),
                   modB[:, c0:c0 + KT].unsqueeze(2).to_broadcast([P, KT, P]), ALU.mult).then_inc(S("diag_out"), 1)

            def rows_out(row, v):
                dve.wait_ge(S("gate_mm"), v + 1)
                for hf in range(2):
                    i = cp(row[:, 512 * hf:512 * hf + 512], bank[6 + hf][:])
                i.then_inc(S("gate_rows"), 1)

            diagonal(0)
            dve.wait_ge(S("ga_out"), this(HEADS - 1))
            dve.wait_ge(S("gb_out"), this(HEADS - 1))
            merge(0, 0, True)
            rows_out(gate1, 0)
            diagonal(24)
            merge(0, 1, True)
            rows_out(gate2, 1)
            with dve.Fori(1, KT // 2) as i:
                for b in range(2):
                    merge(i, b, False)

            link = serial
            link(ts(aff2[:], modB[:, 16:24], 1.0, None, ALU.add))
            link(tt(aff2[:], aff2[:], par[:, V_N2, :], ALU.mult))
            dve.wait_ge(S("rt_in"), 64)
            across = lambda v: v.unsqueeze(2).to_broadcast([P, KT, NG + NE])
            tt(w_sh, w_rt[:], across(modB[:, 8:16]), ALU.mult).then_inc(S("rt_prep"), 1)
            dve.wait_ge(S("rt_prep"), 1)
            tt(w_rt[:], w_rt[:], across(aff2[:]), ALU.mult).then_inc(S("rt_prep"), 1)
            dve.wait_ge(S("gate_rows"), 2)
            dve.wait_ge(S("xr_in"), 48)
            for t in range(2):
                if t:
                    dve.wait_ge(S("gate_mm"), 3)
                    tt(b_rt[:], b_rt[:], bank[2][:, 0:NG + NE], ALU.add).then_inc(S("rt_prep"), 1)
                for hf in range(2):
                    dve.wait_ge(S("wo_mm"), 2 * t + hf + 1)
                    s = slice(512 * hf, 512 * hf + 512)
                    link(tt(x1[:, t, s], bank[(4, 0)[t] + hf][:], gate1[:, s], ALU.mult))
                    tt(x1[:, t, s], x1[:, t, s], xr[:, t, s], ALU.add).then_inc(S("x1_out"), 1)
            dve.wait_ge(S("x1_T"), 4)
            cp(x1T[:, 4:8, P:], bank[3][:].rearrange("p (k n) -> p k n", k=4)).then_inc(S("x1T_out2"), 1)
            dve.wait_ge(S("ssq_out"), 8)
            link(tt(rstd[:, 0:2], ssq[:, 0:2], ssq[:, 2:4], ALU.add))
            ts(rstd[:, 0:2], rstd[:, 0:2], 1.0 / D, EPS, ALU.mult, ALU.add).then_inc(S("ms_out"), 1)
            dve.wait_ge(S("rms_out"), 2)
            dve.reciprocal(rstd[:, 0:2], rstd[:, 0:2]).then_inc(S("rstd_out"), 1)
            dve.wait_ge(S("rstd_out"), 1)

            dve.wait_ge(S("rt_mm"), 1)
            dve.wait_ge(S("rt_prep"), 3)
            for t in range(2):
                i = stt(lg[:, t, :], bank[5][:, 64 * t:64 * t + NG + NE], rstd[:, t:t + 1], b_rt[:], ALU.mult, ALU.add)
            link(i)
            R = lambda j: rcol[:, j, :]
            bc = lambda a, n: a.unsqueeze(2).to_broadcast([P, 2, n])
            lgg = lg[:, :, 0:NG]
            link(dve.tensor_reduce(R(0), lgg, AX.X, ALU.max))
            tt(rt_g[:, :, 1, :], lgg, bc(R(0), NG), ALU.subtract).then_inc(S("rt_sub"), 1)
            link(tt(rt_g[:, :, 0, :], lgg, bc(R(0), NG), ALU.is_equal))

            def first_of(eq, dst, cum):
                for t in range(2):
                    i = dve.tensor_tensor_scan(cum[:, t, :], ones[:, 0:eq[:, t, :].shape[-1]], eq[:, t, :], 0.0,
                                               ALU.mult, ALU.add)
                link(i)
                link(stt(dst, cum, 1.0, eq, ALU.is_equal, ALU.mult))
            first_of(rt_g[:, :, 0, :], rt_g[:, :, 3, :], rt_g[:, :, 2, :])
            link(ts(rt_g[:, :, 0, :], rt_g[:, :, 3, :], 1.0, BIG, ALU.subtract, ALU.mult))
            for t in range(2):
                i = tt(rt[:, 0, t, :].rearrange("p (g e) -> p g e", g=NG),
                       lg[:, t, NG:].rearrange("p (g e) -> p g e", g=NG),
                       rt_g[:, t, 0, :].unsqueeze(2).to_broadcast([P, NG, EPG]), ALU.add)
            link(i)
            link(dve.tensor_reduce(R(3), rt[:, 0], AX.X, ALU.max))
            link(tt(rt[:, 1], rt[:, 0], bc(R(3), NE), ALU.is_equal))
            first_of(rt[:, 1], rt[:, 3], rt[:, 2])
            link(stt(rt[:, 4], rt[:, 3], -3 * BIG, rt[:, 0], ALU.mult, ALU.add))
            link(dve.tensor_reduce(R(4), rt[:, 4], AX.X, ALU.max))
            link(tt(rt[:, 5], rt[:, 4], bc(R(4), NE), ALU.is_equal))
            tt(R(6), R(4), R(3), ALU.subtract).then_inc(S("rt_sub"), 1)
            first_of(rt[:, 5], rt[:, 7], rt[:, 6])
            tt(rt[:, 8], rt[:, 3], rt[:, 7], ALU.add).then_inc(S("sel_out"), 1)
            dve.wait_ge(S("rt_exp"), 2)
            link(dve.tensor_reduce(R(1), rt_g[:, :, 1, :], AX.X, ALU.add))
            link(dve.reciprocal(R(2), R(1)))
            link(ts(R(7), R(6), 1.0, None, ALU.add))
            link(dve.reciprocal(R(7), R(7)))
            link(tt(R(8), R(7), R(2), ALU.mult))
            link(tt(R(9), R(8), R(6), ALU.mult))
            link(tt(rt[:, 9], rt[:, 3], bc(R(8), NE), ALU.mult))
            link(tt(rt[:, 10], rt[:, 7], bc(R(9), NE), ALU.mult))
            tt(cw[:], rt[:, 9], rt[:, 10], ALU.add)
            dve.wait_ge(S("sel_out"), 1)
            dve.wait_ge(S("rank_mm"), 1)
            link(stt(rt[:, 11], bank[0][:, 0:2 * NE].rearrange("p (t n) -> p t n", t=2), 1.0, rt[:, 8],
                     ALU.add, ALU.mult))
            link(ts(rank[:, :, 0:NE], rt[:, 11], 1.0, None, ALU.subtract))
            link(ts(rank[:, :, NE:], rank[:, :, 0:2], float(SLOTS), None, ALU.subtract))

            def one_hots(first, g):
                dve.wait_ge(S("mx"), last(g, 1))
                for e in range(2):
                    i = tt(hot[:, :, e, :], slot_no[:].unsqueeze(1).to_broadcast([P, 2, SLOTS]),
                           rank[:, :, bass.ds(first + e, 1)].to_broadcast([P, 2, SLOTS]), ALU.is_equal)
                i.then_inc(S("hotc"), 1)

            one_hots(0, 0)
            dve.memset(ct, 0.0)
            dve.memset(ys, 0.0)
            dve.wait_ge(S("rank_mm"), 2)
            link(dve.tensor_reduce(rcnt[:, 0:1], bank[1][:, 0:NE], AX.X, ALU.max))
            link(ts(rcnt[:, 1:2], rcnt[:, 0:1], float(SLOTS), 1.0, ALU.is_gt, ALU.add))
            link(stt(rcnt[:, 2:3], rcnt[:, 0:1], float(2 * SLOTS), rcnt[:, 1:2], ALU.is_gt, ALU.add))
            link(stt(rcnt[:, 3:4], rcnt[:, 0:1], float(3 * SLOTS), rcnt[:, 2:3], ALU.is_gt, ALU.add))
            cp(rcnt_i[:], rcnt[:, 3:4].to_broadcast([P, 4])).then_inc(S("rounds_ready"), 1)
            dve.wait_ge(S("rounds_ready"), 1)
            n_rounds = dve.value_load(rcnt_i[0:1, 0:1], min_val=1, max_val=T // SLOTS)
            with dve.Fori(0, n_rounds) as r:
                with dve.Fori(0, PAIRS) as p:
                    q = r * PAIRS + p
                    dve.wait_ge(S("hotc"), q + 2)
                    dve.wait_ge(S("mtc"), last(q))
                    for e in range(2):
                        i = tt(hotw[:, :, e, :], hot[:, :, e, :],
                               cw[:, :, bass.ds(p * 2 + e, 1)].to_broadcast([P, 2, SLOTS]), ALU.mult)
                    i.then_inc(S("hw"), 1)
                    dve.wait_ge(S("hw"), this(q))
                    one_hots(p * 2 + 2, q + 1)
                    dve.wait_ge(S("m3"), this(q))
                    dve.wait_ge(S("sh"), this(q))
                    dve.wait_ge(S("mtg"), last(q))
                    tt(gm, sh, VY[:], ALU.mult).then_inc(S("gm"), 1)
                    dve.wait_ge(S("mc"), this(r * (PAIRS + 1) + p, 1))
                    for hf in range(2):
                        dve.wait_ge(S("my"), this(q, hf))
                        cp(ys[:, hf, :], (CY if hf else VY)[:]).then_inc(S("ysc"), 1)
                step = Chain("res_step", r * 4)
                for t in range(2):
                    dve.wait_ge(S("mc"), this(r * (PAIRS + 1) + PAIRS, t))
                    for hf in range(2):
                        s = slice(512 * hf, 512 * hf + 512)
                        i = tt(res[:, s], ACC[t][hf][:], gate2[:, s], ALU.mult)
                    step(i)
                    step(tt(x1[:, t, :], x1[:, t, :], res, ALU.add))
                dve.memset(ct, 0.0)
                ts(rank, rank, float(SLOTS), None, ALU.subtract).then_inc(S("acc_read"), 1)
                dve.wait_ge(S("acc_read"), r + 2)

            link = serial
            dve.memset(ssq[:], 0.0).then_inc(S("x1_out"), 1)
            dve.wait_ge(S("ssq_out"), 10)
            ts(rstd[:, 0:2], ssq[:, 0:2], 1.0 / D, EPS, ALU.mult, ALU.add).then_inc(S("ms_out"), 1)
            dve.wait_ge(S("rms_out"), 3)
            link(dve.reciprocal(rstd[:, 0:2], rstd[:, 0:2]))
            dve.wait_ge(S("xr_in"), 48)
            for t in range(2):
                stt(xn[:, t, :], x1[:, t, :], rstd[:, t:t + 1], fin_g, ALU.mult, ALU.mult).then_inc(S("y_out"), 1)


_INS = ['x', 'c', 'ctx', 'c_ctx', 'w_mod', 'b_mod', 'norm1_g', 'w_in', 'conv_w', 'conv_b', 'lru_wa', 'lru_ba',
        'lru_wx', 'lru_bx', 'lru_lam', 'hg_lb', 'hg_norm_g', 'w_proj_a', 'w_proj_b', 'w_out', 'norm2_g', 'w_rg',
        'b_rg', 'w_re', 'b_re', 'w1', 'w3', 'w2', 'final_g']


def kernel(**inputs):
    import numpy as np
    import concourse.bacc as bacc
    from concourse.bass_utils import run_bass_kernel_spmd

    nc = bacc.Bacc("TRN2", target_bir_lowering=False, num_devices=1)
    arrays, args = {}, []
    for name in _INS:
        a = np.ascontiguousarray(inputs[name])
        arrays[f"in_{name}"] = a
        args.append(nc.dram_tensor(f"in_{name}", a.shape, mybir.dt.from_np(a.dtype), kind="ExternalInput").ap())
    out = nc.dram_tensor("out_0", (1, T, D), mybir.dt.float32, kind="ExternalOutput").ap()
    build(nc, *args, out)
    r = run_bass_kernel_spmd(nc, [arrays], core_ids=[0])
    return r.results[0]["out_0"]
```
